# Optimizing a Trainium2 kernel written in Bass

```python
import math
import jax, jax.numpy as jnp
from jax import lax
import numpy as np

D_MODEL = 1024
BATCH = 1
SEQ = 512
DEPTH = 2

N_HEADS = D_MODEL // 128
HEAD_DIM = 64
ATTN_W = N_HEADS * 2 * HEAD_DIM
CONV_CH = D_MODEL
CONV_K = 31
D_FF = ((8 * D_MODEL // 3 + 255) // 256) * 256
NUM_BUCKETS = 32
MAX_DISTANCE = 128
Q_BLOCK = 128
N_BRANCH = 2
MIX_IN = 3 * ATTN_W + 2 * CONV_CH + N_BRANCH * D_MODEL
N_MOD = 9
EPS = 1e-6

kernel_name = "hybrid_diffattn_conformer_conv_macaron_adaln"

def rms_norm(x, g):
    xf = x.astype(jnp.float32)
    y = xf * lax.rsqrt(jnp.mean(xf * xf, axis=-1, keepdims=True) + EPS)
    return (y * g.astype(jnp.float32)).astype(x.dtype)

def layer_norm(x, g, b):
    xf = x.astype(jnp.float32)
    mu = jnp.mean(xf, axis=-1, keepdims=True)
    xc = xf - mu
    y = xc * lax.rsqrt(jnp.mean(xc * xc, axis=-1, keepdims=True) + EPS)
    return (y * g.astype(jnp.float32) + b.astype(jnp.float32)).astype(x.dtype)

def modulate(h, shift, scale):
    return h * (1 + scale[:, None, :]) + shift[:, None, :]

def swiglu(h, w_in, w_out):
    g, u = jnp.split(h @ w_in, 2, axis=-1)
    return (jax.nn.silu(g) * u) @ w_out

def t5_bucket(dist):
    n = jnp.maximum(dist, 0)
    max_exact = NUM_BUCKETS // 2
    nf = jnp.maximum(n, 1).astype(jnp.float32)
    large = max_exact + (jnp.log(nf / max_exact) / math.log(MAX_DISTANCE / max_exact)
                         * (NUM_BUCKETS - max_exact)).astype(jnp.int32)
    large = jnp.minimum(large, NUM_BUCKETS - 1)
    return jnp.where(n < max_exact, n, large)

def diff_attention(q, k, v, lam, rel_bias):
    B, S = q.shape[0], q.shape[1]
    nb = S // Q_BLOCK
    qb = q.reshape(B, nb, Q_BLOCK, N_HEADS, 2, HEAD_DIM).swapaxes(0, 1)
    kpos = jnp.arange(S)
    scale = HEAD_DIM ** -0.5
    table = rel_bias.astype(jnp.float32)
    neg = jnp.finfo(jnp.float32).min

    def block(args):
        qblk, i = args
        qpos = i * Q_BLOCK + jnp.arange(Q_BLOCK)
        dist = qpos[:, None] - kpos[None, :]
        bias = jnp.take(table, t5_bucket(dist), axis=1)
        s = jnp.einsum('bqhmd,bkhmd->bhmqk', qblk, k).astype(jnp.float32) * scale
        s = s + bias[None, :, None]
        s = jnp.where(dist >= 0, s, neg)
        p = jax.nn.softmax(s, axis=-1)
        w = p[:, :, 0] - lam * p[:, :, 1]
        return jnp.einsum('bhqk,bkhe->bqhe', w.astype(v.dtype), v)

    o = lax.map(block, (qb, jnp.arange(nb)))
    return o.swapaxes(0, 1).reshape(B, S, N_HEADS, 2 * HEAD_DIM)

def conformer_conv(u, w_dw, b_dw, ln_g, ln_b, w_out):
    a, g = jnp.split(u, 2, axis=-1)
    z = a * jax.nn.sigmoid(g)
    z = lax.conv_general_dilated(z, w_dw[:, None, :], window_strides=(1,),
                                 padding=[(CONV_K - 1, 0)],
                                 dimension_numbers=('NWC', 'WIO', 'NWC'),
                                 feature_group_count=CONV_CH) + b_dw
    z = jax.nn.silu(layer_norm(z, ln_g, ln_b))
    return z @ w_out

def setup_inputs(seed: int = 0) -> dict:
    key = jax.random.key(seed)
    ks = jax.random.split(key, 32)

    def nrm(k, shape, scale):
        return jax.random.normal(k, shape, jnp.float32) * scale

    def gain(k, shape):
        return 1.0 + 0.05 * jax.random.normal(k, shape, jnp.float32)

    L, D = DEPTH, D_MODEL
    return {
        "x": nrm(ks[0], (BATCH, SEQ, D), 1.0),
        "c": nrm(ks[1], (BATCH, D), 1.0),
        "ffn1_norm": gain(ks[2], (L, D)),
        "ffn1_w_in": nrm(ks[3], (L, D, 2 * D_FF), D ** -0.5),
        "ffn1_w_out": nrm(ks[4], (L, D_FF, D), D_FF ** -0.5),
        "mix_norm": gain(ks[5], (L, D)),
        "w_mix_in": nrm(ks[6], (L, D, MIX_IN), D ** -0.5),
        "lambda_q1": nrm(ks[7], (L, HEAD_DIM), 0.1),
        "lambda_k1": nrm(ks[8], (L, HEAD_DIM), 0.1),
        "lambda_q2": nrm(ks[9], (L, HEAD_DIM), 0.1),
        "lambda_k2": nrm(ks[10], (L, HEAD_DIM), 0.1),
        "subln_gain": gain(ks[11], (L, 2 * HEAD_DIM)),
        "w_attn_branch": nrm(ks[12], (L, ATTN_W, D), ATTN_W ** -0.5),
        "conv_dw": nrm(ks[13], (L, CONV_K, CONV_CH), CONV_K ** -0.5),
        "conv_dw_bias": nrm(ks[14], (L, CONV_CH), 0.02),
        "conv_ln_gain": gain(ks[15], (L, CONV_CH)),
        "conv_ln_bias": nrm(ks[16], (L, CONV_CH), 0.02),
        "w_conv_branch": nrm(ks[17], (L, CONV_CH, D), CONV_CH ** -0.5),
        "w_mix_out": nrm(ks[18], (L, D, D), D ** -0.5),
        "ffn2_norm": gain(ks[19], (L, D)),
        "ffn2_w_in": nrm(ks[20], (L, D, 2 * D_FF), D ** -0.5),
        "ffn2_w_out": nrm(ks[21], (L, D_FF, D), D_FF ** -0.5),
        "ada_w": nrm(ks[22], (L, D, N_MOD * D), 0.5 * D ** -0.5),
        "ada_b": nrm(ks[23], (L, N_MOD * D), 0.02),
        "rel_bias": nrm(ks[24], (N_HEADS, NUM_BUCKETS), 0.5),
        "final_norm": gain(ks[25], (D,)),
    }

def reference(x, c, ffn1_norm, ffn1_w_in, ffn1_w_out, mix_norm, w_mix_in,
              lambda_q1, lambda_k1, lambda_q2, lambda_k2, subln_gain,
              w_attn_branch, conv_dw, conv_dw_bias, conv_ln_gain, conv_ln_bias,
              w_conv_branch, w_mix_out, ffn2_norm, ffn2_w_in, ffn2_w_out,
              ada_w, ada_b, rel_bias, final_norm):
    B, S, _ = x.shape
    c_act = jax.nn.silu(c)
    for l in range(DEPTH):
        lam_init = 0.8 - 0.6 * math.exp(-0.3 * l)
        mod = c_act @ ada_w[l] + ada_b[l]
        sh1, sc1, g1, sh2, sc2, g2, sh3, sc3, g3 = jnp.split(mod, N_MOD, axis=-1)

        h = modulate(rms_norm(x, ffn1_norm[l]), sh1, sc1)
        x = x + 0.5 * g1[:, None, :] * swiglu(h, ffn1_w_in[l], ffn1_w_out[l])

        h = modulate(rms_norm(x, mix_norm[l]), sh2, sc2)
        proj = h @ w_mix_in[l]
        q, k, v, u, gates = jnp.split(
            proj, [ATTN_W, 2 * ATTN_W, 3 * ATTN_W, 3 * ATTN_W + 2 * CONV_CH], axis=-1)
        q = q.reshape(B, S, N_HEADS, 2, HEAD_DIM)
        k = k.reshape(B, S, N_HEADS, 2, HEAD_DIM)
        v = v.reshape(B, S, N_HEADS, 2 * HEAD_DIM)
        lam = (jnp.exp(jnp.sum(lambda_q1[l].astype(jnp.float32) * lambda_k1[l].astype(jnp.float32)))
               - jnp.exp(jnp.sum(lambda_q2[l].astype(jnp.float32) * lambda_k2[l].astype(jnp.float32)))
               + lam_init)
        o = diff_attention(q, k, v, lam, rel_bias)
        o = rms_norm(o, subln_gain[l]) * (1 - lam_init)
        y_attn = o.reshape(B, S, ATTN_W) @ w_attn_branch[l]
        y_conv = conformer_conv(u, conv_dw[l], conv_dw_bias[l], conv_ln_gain[l],
                                conv_ln_bias[l], w_conv_branch[l])
        ga, gb = jnp.split(gates, N_BRANCH, axis=-1)
        merged = jax.nn.sigmoid(ga) * y_attn + jax.nn.sigmoid(gb) * y_conv
        x = x + g2[:, None, :] * (merged @ w_mix_out[l])

        h = modulate(rms_norm(x, ffn2_norm[l]), sh3, sc3)
        x = x + 0.5 * g3[:, None, :] * swiglu(h, ffn2_w_in[l], ffn2_w_out[l])
    return rms_norm(x, final_norm)


_drawn_inputs = setup_inputs


def setup_inputs(seed=0):
    import zlib

    import numpy as np

    out = dict(_drawn_inputs(seed))
    spreads = {}
    factors = {'ffn1_norm': 5.051,
     'mix_norm': 4.316,
     'lambda_q1': 5.259,
     'lambda_k1': 59.56,
     'lambda_q2': 8.0,
     'lambda_k2': 8.0,
     'subln_gain': 6.356,
     'conv_dw_bias': 8.0,
     'conv_ln_gain': 6.245,
     'conv_ln_bias': 28.801,
     'ffn2_norm': 5.474}
    for name, (base, spread) in spreads.items():
        noise = np.random.default_rng([zlib.crc32(name.encode()), seed]).standard_normal(out[name].shape)
        drawn = base * np.exp(spread * noise) if base else spread * noise
        out[name] = __import__('jax').numpy.asarray(drawn.astype(out[name].dtype))
    for name, factor in factors.items():
        out[name] = (out[name] * factor).astype(out[name].dtype)
    return out
```

```python
import math
from contextlib import ExitStack

import numpy as np

import concourse.bass as bass
from concourse import mybir
from concourse.bass import ds

F32 = mybir.dt.float32
F32R = mybir.dt.float32r
ACT = mybir.ActivationFunctionType
ALU = mybir.AluOpType

P = 128
D = 1024
TOK = 512
DEPTH = 2
HEADS = D // 128
HD = 64
CK = 31
PADL = CK - 1
FF = ((8 * D // 3 + 255) // 256) * 256
BUCKETS = 32
MAXDIST = 128
EPS = 1e-6
NEG = -3.0e38

KT = D // P
FT = FF // P
QB = TOK // P
NMOD = 9
HC = 2 * NMOD
HCW = 512
RING = 6
OUTG = (8, 8, 6)
assert sum(OUTG) == FT

PH_PAIRS = dict(ffn1_in=FT, ffn1_out=12, mix=3 * HEADS, bra=KT, brb=KT // 2, mo=KT // 2, ffn2_in=FT, ffn2_out=12)
PH_USES = dict(ffn1_in=FT, ffn1_out=KT // 2, mix=3 * HEADS, bra=KT, brb=KT // 2, mo=KT // 2, ffn2_in=FT, ffn2_out=KT // 2)


def starts(sizes):
    out, at = {}, 0
    for name, n in sizes.items():
        out[name] = at
        at += n
    return out, at


PAIR0, PAIRS = starts(PH_PAIRS)
USE0, USES = starts(PH_USES)

AUXN = 3 + HEADS + 2
AUX_NORM = (0, 1, AUXN - 1)
AUX_HEAD, AUX_MEAN, AUX_VAR = 2, 2 + HEADS, 3 + HEADS
RSN = 3 + HEADS + 1
RS_NORM = (0, 1, RSN - 1)
RS_HEAD, RS_VAR = 2, 2 + HEADS
UNITS = 3 * KT + HEADS + KT
UNIT_NORM = (0, KT, UNITS - KT)
UNIT_HEAD, UNIT_LN = 2 * KT, 2 * KT + HEADS
ZERO_FFN1, ZERO_CONV, ZERO_LN, ZERO_MO, ZERO_FFN2, ZEROS = 1, 2, 3, 4, 5, 5

PC_NORM = (0, 8, 16)
PC_DWB, PC_LNG, PC_LNB, PC_SUB, PC_ADA = 24, 32, 40, 48, 49
PC = PC_ADA + NMOD * KT
DVE_TAPS = 23
POOL_TAPS = CK - DVE_TAPS


def bias_selection():
    x = np.arange(TOK + P)
    dist = (TOK - 1) - x
    n = np.maximum(dist, 0)
    exact = BUCKETS // 2
    nf = np.maximum(n, 1).astype(np.float32)
    large = exact + (np.log(nf / np.float32(exact)) / np.float32(math.log(MAXDIST / exact))
                     * np.float32(BUCKETS - exact)).astype(np.int32)
    large = np.minimum(large, BUCKETS - 1)
    bucket = np.where(n < exact, n, large)
    sel = np.zeros((BUCKETS + 1, x.size), np.float32)
    ok = dist >= 0
    sel[bucket[ok], x[ok]] = 1.0
    sel[BUCKETS, ~ok] = 1.0
    return sel



def build(nc, a, onehot, out):
    ctx = ExitStack()
    names = {}

    def sem(name):
        if name not in names:
            names[name] = ctx.enter_context(nc.semaphore(name))
        return names[name]

    place = [(nc.sbuf_base + 31) // 32 * 32]

    def at(name, shape, dt, offset=None):
        size = int(np.prod(shape[1:])) * 4
        if offset is None:
            offset = place[0]
            place[0] += (size + 31) // 32 * 32
        assert offset + size <= nc.sbuf_usable_end - 64, name
        return nc.alloc_sbuf_tensor_at(name, shape, dt, offset=offset)

    KB = 1024
    X = at("x_res", [P, KT, TOK], F32)
    h0 = place[0]
    HHI = at("h_hi", [P, KT, TOK], F32R)
    HLO = at("h_lo", [P, KT, TOK], F32R)
    r0 = place[0]
    place[0] += 96 * KB
    raw = [at(f"w_raw{s}", [P, 8, P], F32) for s in range(2)]
    whi = [at(f"w_hi{s}", [P, 8, P], F32R) for s in range(2)]
    wlo = [at(f"w_lo{s}", [P, 8, P], F32R) for s in range(2)]
    SQ = at("squares", [P, TOK], F32)
    SSUM = at("running_sum", [P, TOK], F32)
    RSTD = at("rstd", [P, TOK], F32)
    T = [at(f"scaled{i}", [P, TOK], F32) for i in range(2)]
    F = [at(f"full{i}", [P, TOK], F32) for i in range(2)]
    ada_raw = [at(f"ada_raw{i}", [P, HCW], F32) for i in range(2)]
    ada_tmp = at("ada_tmp", [P, HCW], F32)
    ACC = at("ada_acc", [P, RING, HCW], F32)
    BT = at("bias_tile", [P, TOK], F32)
    ident = at("ident", [P, P], F32)
    invd = at("inv_d", [P, P], F32)
    PT = at("params", [P, DEPTH * PC], F32)
    PT2 = at("params2", [P, 2 * KT], F32)
    CA = at("c_act", [P, KT], F32)
    MODC = at("modulation", [P, DEPTH * NMOD * KT], F32)
    AC = at("norm_scale", [P, 3, KT], F32)
    GC = at("gates", [P, 3, KT], F32)
    CW = at("conv_taps", [P, DEPTH * HEADS, CK], F32)
    tapw = at("pool_taps", [P, POOL_TAPS], F32)
    spare = at("spare", [P, 2], F32)
    eps = at("eps", [P, 1], F32)
    lam_dot = at("lam_dot", [P, 2 * DEPTH], F32)
    lam_exp = at("lam_exp", [P, 2 * DEPTH], F32)
    nlam = at("neg_lambda", [P, DEPTH], F32)
    subg = at("subln", [P, DEPTH], F32)
    mx = at("row_max", [P, 2, 2], F32)
    nmx = at("neg_row_max", [P, 2, 2], F32)
    rsum = at("row_sum", [P, 2, 2], F32)
    rinv = at("row_inv", [P, 2, 2], F32)
    rlam = at("row_inv_lam", [P, 2], F32)
    SHI = at("s_hi", [P, FT, TOK], F32R, r0)
    SLO = at("s_lo", [P, FT, TOK], F32R, r0 + FT * TOK * 4)
    AOHI = at("ao_hi", [P, KT, TOK], F32R, r0)
    AOLO = at("ao_lo", [P, KT, TOK], F32R, r0 + 16 * KB)
    C = at("conv", [P, KT, TOK], F32, r0 + 32 * KB)
    CHI = at("conv_hi", [P, KT, TOK], F32R, r0 + 32 * KB)
    GA = at("gate_a", [P, KT, TOK], F32, r0 + 48 * KB)
    MHI = at("merged_hi", [P, KT, TOK], F32R, r0 + 48 * KB)
    MLO = HLO
    ph = r0 + 64 * KB
    QT = at("q_t", [P, TOK], F32, ph)
    KTT = at("k_t", [P, TOK], F32, ph + 2 * KB)
    VT = at("v_t", [P, TOK], F32, ph + 4 * KB)
    V = at("v", [P, QB, P], F32, ph + 6 * KB)
    WT = at("weights_t", [P, QB, TOK], F32, ph + 8 * KB)
    GB = at("gate_b", [P, KT, TOK], F32, ph)
    CLO = at("conv_lo", [P, KT, TOK], F32R, ph + 16 * KB)
    PR = [[at(f"probs{par}_{m}", [P, (3 + par) * P], F32, ph + 16 * KB + par * 3 * KB + m * (3 + par) * 512)
           for m in range(2)] for par in range(2)]
    z0 = ph + 23 * KB
    Z = at("glu", [P, TOK + 32], F32, z0)
    CAB = [at(f"conv_part{i}", [P, TOK], F32, z0 + 2176 + 2 * KB * i) for i in range(2)]
    CP = at("conv_pool", [P, TOK], F32, z0 + 2176 + 4 * KB)
    ADA0 = at("ada_first", [P, KT, 4 * HCW], F32, r0)
    XS = at("x_rows", [P, QB, D], F32, r0 + 64 * KB)
    s0 = r0 + 80 * KB
    PV = [at(f"param_rows{l}", [P, P], F32, s0 + 512 * l) for l in range(DEPTH)]
    PV2 = at("param_rows2", [P, P], F32, s0 + 1024)
    OH = at("onehot_sb", [P, TOK + P], F32, s0 + 1536)
    TBR = at("table_rows", [P, BUCKETS], F32, s0 + 4096)
    TB = at("table_t", [P, HEADS], F32, s0 + 4224)
    TBX = at("table_wide", [P, HEADS, P], F32, s0 + 4256)
    LV = at("lambda_rows", [P, DEPTH, 4, HD], F32, s0 + 8352)
    BR = [at(f"bias_row{i}", [P, TOK + P], F32, h0 + 8 * KB + 2560 * i) for i in range(2)]
    CWR = at("tap_rows", [P, DEPTH, D], F32, h0)
    YO = at("y_rows", [P, QB, D], F32, r0)

    bank = [ctx.enter_context(nc.psum_tensor(f"bank{i}", [P, TOK], F32)) for i in range(8)]
    G = bank[0:2]
    S = bank[2:4]
    TP = bank[4:6]
    O = bank[6]
    AUX = bank[7]

    def flat(t):
        return t[:, :, :].rearrange("p k t -> p (k t)")

    def tile(view, j, width=TOK):
        return view[:, ds(j * width, width)]

    X2, C2, GA2, GB2 = flat(X), flat(C), flat(GA), flat(GB)
    SHI2, SLO2, MHI2, MLO2 = flat(SHI), flat(SLO), flat(MHI), flat(MLO)
    AOHI2, AOLO2, CW2 = flat(AOHI), flat(AOLO), flat(CW)

    BD = nc.dram_tensor("bias_rows", [HEADS + 1, P * (TOK + P)], F32, kind="Internal")

    w_in = [a["ffn1_w_in"].rearrange("l (k p) f -> p (l k) f", p=P), a["ffn2_w_in"].rearrange("l (k p) f -> p (l k) f", p=P)]
    w_out = [a["ffn1_w_out"].rearrange("l (k p) f -> p (l k) f", p=P), a["ffn2_w_out"].rearrange("l (k p) f -> p (l k) f", p=P)]
    w_mix = a["w_mix_in"].rearrange("l (k p) f -> p (l k) f", p=P)
    w_ab = a["w_attn_branch"].rearrange("l (k p) f -> p (l k) f", p=P)
    w_cb = a["w_conv_branch"].rearrange("l (k p) f -> p (l k) f", p=P)
    w_mo = a["w_mix_out"].rearrange("l (k p) f -> p (l k) f", p=P)
    w_ada = a["ada_w"].rearrange("l (k p) f -> p (l k) f", p=P)

    block = ctx.enter_context(nc.Block())
    w_raw = [sem(f"w_raw_in{s}") for s in range(2)]
    w_hi = [sem(f"w_hi_done{s}") for s in range(2)]
    w_lo = [sem(f"w_lo_done{s}") for s in range(2)]
    w_used = [sem(f"w_used{s}") for s in range(2)]
    acc_read = [sem(f"acc_read{b}") for b in range(2)]

    @block.sync
    def _(sp):
        def slab(pair, slot, src, n=8):
            sp.wait_ge(w_lo[slot], pair)
            sp.dma_start(raw[slot][:, 0:n, :], src).then_inc(w_raw[slot], 16)

        def cols(w, k0, n, c0):
            return w[:, ds(k0, n), ds(c0, P)]

        for l in range(DEPTH):
            rows = [("ffn1_norm", KT), ("mix_norm", KT), ("ffn2_norm", KT), ("conv_dw_bias", KT),
                    ("conv_ln_gain", KT), ("conv_ln_bias", KT), ("subln_gain", 1), ("ada_b", NMOD * KT)]
            r = 0
            for name, n in rows:
                sp.dma_start(PV[l][r:r + n, :], a[name][l, :].rearrange("(r c) -> r c", c=P)).then_inc(sem("rows_in"), 16)
                r += n
            assert r == PC
        sp.dma_start(PV2[0:KT, :], a["final_norm"].rearrange("(r c) -> r c", c=P)).then_inc(sem("rows_in"), 16)
        sp.dma_start(PV2[KT:2 * KT, :], a["c"][0, :].rearrange("(r c) -> r c", c=P)).then_inc(sem("rows_in"), 16)
        for t in range(QB):
            sp.dma_start(XS[:, t, :], a["x"][0, t * P:(t + 1) * P, :]).then_inc(sem(f"x_in{t}"), 16)
        for k in range(KT):
            sp.dma_start(ADA0[:, k, :], w_ada[:, k, 0:4 * HCW]).then_inc(sem(f"ada0_in{k}"), 16)

        with sp.Fori(0, DEPTH) as l:
            pair = l * PAIRS
            for w in range(2):
                with sp.Fori(0, FT) as i:
                    p = pair + PAIR0[f"ffn{w + 1}_in"] + i
                    slab(p, 0, cols(w_in[w], l * KT, 8, i * P))
                    slab(p, 1, cols(w_in[w], l * KT, 8, i * P + FF))
                with sp.Fori(0, KT // 2) as i:
                    for m in range(6):
                        p = pair + PAIR0[f"ffn{w + 1}_out"] + i * 3 + m // 2
                        slab(p, m % 2, cols(w_out[w], l * FT + sum(OUTG[:m % 3]), OUTG[m % 3], i * (2 * P) + (m // 3) * P), OUTG[m % 3])
                if w == 1:
                    continue
                with sp.Fori(0, HEADS) as h:
                    for m in range(6):
                        slab(pair + PAIR0["mix"] + h * 3 + m // 2, m % 2, cols(w_mix, l * KT, 8, h * P + m * D))
                with sp.Fori(0, KT) as j:
                    slab(pair + PAIR0["bra"] + j, 0, cols(w_mix, l * KT, 8, j * P + 6 * D))
                    slab(pair + PAIR0["bra"] + j, 1, cols(w_ab, l * KT, 8, j * P))
                for name, wt in (("brb", w_cb), ("mo", w_mo)):
                    with sp.Fori(0, KT // 2) as i:
                        for t in range(2):
                            slab(pair + PAIR0[name] + i, t, cols(wt, l * KT, 8, i * (2 * P) + t * P))
        for s in range(2):
            slab(DEPTH * PAIRS, s, cols(w_mo, 0, 8, 0))

        for t in range(QB):
            sp.wait_ge(sem("y_ready"), KT)
            sp.dma_start(out[0, t * P:(t + 1) * P, :], YO[:, t, :]).then_inc(sem("y_out"), 16)
        sp.wait_ge(sem("y_out"), 16 * QB)
        for s in range(2):
            sp.wait_ge(w_raw[s], 16 * (DEPTH * PAIRS + 1))


    @block.gpsimd
    def _(pool):
        pool.memset(ident[:, :], 0.0).then_inc(sem("ident0"), 1)
        pool.memset(invd[:, :], 1.0 / D).then_inc(sem("consts"), 1)
        pool.memset(eps[:, :], EPS).then_inc(sem("consts"), 1)
        pool.wait_ge(sem("ident0"), 1)
        pool.affine_select(out=ident[:, :], in_=ident[:, :], compare_op=ALU.not_equal, fill=1.0, base=0,
                           pattern=[[-1, P]], channel_multiplier=1).then_inc(sem("consts"), 1)

        def carry_wait():
            pool.tensor_tensor(spare[:, 0:1], eps[:, 0:1], eps[:, 0:1], ALU.add)

        def ada_load(l, hc, k):
            pool.dma_start(ada_raw[k % 2][:, :], w_ada[:, l * KT + k, ds(hc * HCW, HCW)])\
                .then_inc(sem(f"ada_in{k % 2}"), 16)

        def half_chunk(l, hc, slot, more):
            c = hc + l * HC
            n = c - 4
            for k in range(KT):
                pool.wait_ge(sem(f"ada_in{k % 2}"), (n * (KT // 2) + (k // 2 + 1)) * 16)
                carry_wait()
                dst = ACC[:, slot, :] if k == 0 else ada_tmp[:, :]
                pool.tensor_scalar(dst, ada_raw[k % 2][:, :], CA[:, k:k + 1], 0.0, ALU.mult, ALU.add)\
                    .then_inc(sem("ada_mul"), 1)
                pool.wait_ge(sem("ada_mul"), n * KT + (k + 1))
                if k + 2 < KT:
                    ada_load(l, hc, k + 2)
                elif more:
                    ada_load(l, hc + 1, k + 2 - KT)
                if 0 < k < KT - 1:
                    pool.tensor_tensor(ACC[:, slot, :], ACC[:, slot, :], ada_tmp[:, :], ALU.add)\
                        .then_inc(sem("ada_add"), 1)
                    pool.wait_ge(sem("ada_add"), n * (KT - 2) + k)
                if k == KT - 1:
                    pool.tensor_tensor(ACC[:, slot, :], ACC[:, slot, :], ada_tmp[:, :], ALU.add)\
                        .then_inc(sem("mod_acc"), 1)

        def pool_taps(l, h):
            q = h + l * HEADS
            pool.wait_ge(sem("z_ready"), q + 1)
            pool.wait_ge(sem("c_ready"), q)
            pool.tensor_copy(tapw[:, :], CW2[:, ds(q * CK + DVE_TAPS, POOL_TAPS)]).then_inc(sem("tapw_ready"), 1)
            pool.wait_ge(sem("tapw_ready"), q + 1)
            carry_wait()
            for n in range(POOL_TAPS):
                t = DVE_TAPS + n
                tmp = (ada_raw[0], ada_tmp)[n % 2][:, :]
                dst = CP[:, :] if n == 0 else tmp
                pool.tensor_scalar(dst, Z[:, t:t + TOK], tapw[:, n:n + 1], 0.0, ALU.mult, ALU.add)\
                    .then_inc(sem("ptap_mul"), 1)
                if n == 0:
                    continue
                pool.wait_ge(sem("ptap_mul"), q * POOL_TAPS + (n + 1))
                if n > 1:
                    pool.wait_ge(sem("ptap_add"), q * (POOL_TAPS - 2) + (n - 1))
                pool.tensor_tensor(CP[:, :], CP[:, :], tmp, ALU.add)\
                    .then_inc(sem("cp_ready" if n == POOL_TAPS - 1 else "ptap_add"), 1)

        pool.wait_ge(sem("ca_ready"), 1)
        pool.wait_ge(sem("mod_acc"), 4)
        for l in range(DEPTH):
            if l == 0:
                ada_load(0, 4, 0)
                ada_load(0, 4, 1)
                half_chunk(0, 4, 4, True)
                half_chunk(0, 5, 5, False)
            with pool.Fori(1 if l == 0 else 0, HC // RING) as g:
                ada_load(l, g * RING, 0)
                ada_load(l, g * RING, 1)
                for s in range(RING):
                    pool.wait_ge(sem("modp_ready"), g * RING + (l * HC + s - (RING - 1)))
                    half_chunk(l, g * RING + s, s, s < RING - 1)
            pool.wait_ge(sem("cw_ready"), 2)
            with pool.Fori(0, HEADS) as h:
                pool_taps(l, h)
            pool.wait_ge(sem("cp_ready"), (l + 1) * HEADS)

    @block.scalar
    def _(act):
        def w_hi_part(pair, slot, n=8):
            act.wait_ge(w_raw[slot], (pair + 1) * 16)
            act.wait_ge(w_used[slot], pair)
            act.activation(whi[slot][:, 0:n, :], raw[slot][:, 0:n, :], ACT.Copy).then_inc(w_hi[slot], 1)

        def root(aux, unit, scale=1.0):
            act.wait_ge(sem("aux_ready"), aux + 1)
            act.wait_ge(sem("unit_t"), unit)
            act.activation(RSTD[:, :], AUX[:, :], ACT.Sqrt, bias=eps[:, 0:1], scale=scale).then_inc(sem("aux_read"), 1)

        def unit_split(u, b, first, hi, func, scale, bias):
            act.wait_ge(sem("unit_t"), u + 1)
            act.wait_ge(sem("unit_lo"), u if first else u - 1)
            act.activation(F[b][:, :], T[b][:, :], func, bias=bias, scale=scale).then_inc(sem("unit_f"), 1)
            act.activation(hi, T[b][:, :], func, bias=bias, scale=scale).then_inc(sem("unit_hi"), 1)

        def norm_units(l, k):
            root(l * AUXN + AUX_NORM[k], l * UNITS + UNIT_NORM[k])
            act.wait_ge(sem("ac_ready"), l * 2 + (2 if k else 1))
            for j in range(KT):
                unit_split(l * UNITS + UNIT_NORM[k] + j, j % 2, j == 0, HHI[:, j, :], ACT.Identity,
                           AC[:, k, j:j + 1], MODC[:, ds(l * (NMOD * KT) + 3 * k * KT + j, 1)])

        def square_x(bank_use, t, n8, j):
            act.wait_ge(acc_read[t], bank_use + 1)
            act.wait_ge(sem("ssum_add"), n8 + j)
            act.activation(SQ[:, :], tile(X2, j), ACT.Square).then_inc(sem("sq_ready"), 1)

        for l in range(DEPTH):
            act.dma_start(CWR[0:CK, l, :], a["conv_dw"][l, :, :]).then_inc(sem("taps_in"), 16)
        act.dma_start(TBR[0:HEADS, :], a["rel_bias"]).then_inc(sem("table_in"), 16)
        act.dma_start(OH[0:BUCKETS + 1, :], onehot).then_inc(sem("table_in"), 16)
        for l in range(DEPTH):
            for n, name in enumerate(("lambda_q1", "lambda_k1", "lambda_q2", "lambda_k2")):
                act.dma_start(LV[:, l, n, :], bass.AP(a[name].tensor, l * HD, [[0, P], [1, HD]]))\
                    .then_inc(sem("lambda_in"), 16)
        act.wait_ge(sem("pt_ready"), 3)
        act.activation(CA[:, :], PT2[:, KT:2 * KT], ACT.Silu).then_inc(sem("ca_ready"), 1)
        act.wait_ge(sem("tapsp_ready"), DEPTH)
        for l in range(DEPTH):
            act.activation(CW2[:, l * HEADS * CK:(l + 1) * HEADS * CK], G[l][:, 0:HEADS * CK], ACT.Copy)\
                .then_inc(sem("cw_ready"), 1)
        for s in range(2):
            w_hi_part(0, s)
        act.wait_ge(sem("consts"), 3)
        for j in range(KT):
            act.wait_ge(sem("x_ready"), j + 1)
            act.wait_ge(sem("ssum_add"), j)
            act.activation(SQ[:, :], X[:, j, :], ACT.Square).then_inc(sem("sq_ready"), 1)
        act.wait_ge(sem("lam_dots"), 2 * DEPTH)
        act.activation(lam_exp[:, :], lam_dot[:, :], ACT.Exp).then_inc(sem("lam_exps"), 1)
        for h in range(HEADS):
            act.wait_ge(sem("br_ready"), h + 1)
            if h >= 2:
                act.wait_ge(sem(f"br_out{h % 2}"), 16 * (h // 2))
            if h == 2:
                act.wait_ge(sem("br_again"), 16)
            act.activation(BR[h % 2][:, 0:TOK], O[:, :], ACT.Copy).then_inc(sem("br_part"), 1)
            act.activation(BR[h % 2][:, TOK:TOK + P], AUX[:, 0:P], ACT.Copy).then_inc(sem("br_copied"), 1)
            act.wait_ge(sem("br_copied"), h + 1)
            act.wait_ge(sem("br_part"), h + 1)
            act.dma_start(BD[h, :].rearrange("(p x) -> p x", p=P), BR[h % 2][:, :]).then_inc(sem(f"br_out{h % 2}"), 16)
            if h == 0:
                act.dma_start(BD[HEADS, :].rearrange("(p x) -> p x", p=P), BR[0][:, :]).then_inc(sem("br_again"), 16)
        for i in range(2):
            act.wait_ge(sem(f"br_out{i}"), 16 * (HEADS // 2))

        def load_bias_tile(h):
            src = BD[ds(h, 1), :]
            src = bass.AP(src.tensor, src.offset + (P - 1), [[TOK + P - 1, P], [1, TOK]])
            act.dma_start(BT[:, :], src).then_inc(sem("bt_in"), 16)

        load_bias_tile(0)

        with act.Fori(0, DEPTH) as l:
            for w in range(2):
                n_in, n_out = f"ffn{w + 1}_in", f"ffn{w + 1}_out"
                norm_units(l, 2 * w)
                with act.Fori(0, FT) as i:
                    p = l * PAIRS + PAIR0[n_in] + i
                    u = l * USES + USE0[n_in] + i
                    w_hi_part(p + 1, 0)
                    act.wait_ge(acc_read[1], u)
                    act.activation(T[0][:, :], G[0][:, :], ACT.Silu).then_inc(acc_read[0], 1)
                    w_hi_part(p + 1, 1)
                    act.wait_ge(acc_read[1], u + 1)
                    act.activation(tile(SHI2, i), F[0][:, :], ACT.Copy).then_inc(sem("s_hi"), 1)
                with act.Fori(0, KT // 2) as i:
                    for m in range(6):
                        w_hi_part(l * PAIRS + PAIR0[n_out] + i * 3 + m // 2 + 1, m % 2,
                                  OUTG[(m + 2) % 3] if m < 4 else 8)
                        if m % 3 == 2:
                            square_x(l * USES + USE0[n_out] + i, m // 3, (l * 3 + 1 + 2 * w) * KT, i * 2 + m // 3)
                if w == 1:
                    continue

                norm_units(l, 1)

                def mix(h, first):
                    hh = l * HEADS + h
                    p = l * PAIRS + PAIR0["mix"] + h * 3
                    b = l * USES + USE0["mix"] + h * 3

                    def exps(i):
                        par, si, n = i % 2, hh * 4 + (QB - 1 - i), (i + 1) * P
                        act.wait_ge(sem("nmax_ready"), si + 1)
                        for m in range(2):
                            act.activation(PR[par][m][:, 0:n], PR[par][m][:, 0:n], ACT.Exp, bias=nmx[:, par, m:m + 1],
                                           accum_out=rsum[:, par, m:m + 1]).then_inc(sem("exp_done"), 1)

                    def weights(i):
                        si = hh * 4 + (QB - 1 - i)
                        act.wait_ge(sem("t_ready"), si + 1)
                        act.activation(WT[:, 0:i + 1, i * P:(i + 1) * P],
                                       TP[i % 2][:, 0:(i + 1) * P].rearrange("p (j t) -> p j t", t=P),
                                       ACT.Copy).then_inc(sem("wt_ready"), 1)

                    w_hi_part(p + 1, 0)
                    act.activation(QT[:, :], G[0][:, :], ACT.Copy, scale=HD ** -0.5).then_inc(acc_read[0], 1)
                    if not first:
                        root(l * AUXN + AUX_HEAD + h - 1, l * UNITS + UNIT_HEAD + h - 1, float(D // P))
                    w_hi_part(p + 1, 1)
                    act.activation(KTT[:, :], G[1][:, :], ACT.Copy).then_inc(acc_read[1], 1)
                    if not first:
                        unit_split(l * UNITS + UNIT_HEAD + h - 1, 0, True, tile(AOHI2, h - 1), ACT.Identity,
                                   subg[:, ds(l, 1)], 0.0)
                    w_hi_part(p + 2, 0)
                    act.activation(VT[:, :], G[0][:, :], ACT.Copy).then_inc(acc_read[0], 1)
                    exps(3)
                    w_hi_part(p + 2, 1)
                    act.wait_ge(sem("z_ready"), hh)
                    act.activation(T[1][:, :], G[1][:, :], ACT.Copy, scale=0.5).then_inc(acc_read[1], 1)
                    act.wait_ge(sem("vtp_ready"), hh + 1)
                    act.activation(V[:, :, :].rearrange("p j e -> p (j e)"), TP[0][:, :], ACT.Copy).then_inc(sem("v_ready"), 1)
                    exps(2)
                    weights(3)
                    exps(1)
                    w_hi_part(p + 3, 0)
                    act.activation(F[1][:, :], G[0][:, :], ACT.Tanh, scale=0.5).then_inc(acc_read[0], 1)
                    weights(2)
                    exps(0)
                    load_bias_tile(h + 1)
                    weights(1)
                    w_hi_part(p + 3, 1)
                    act.activation(tile(GA2, h), G[1][:, :], ACT.Tanh, scale=0.5).then_inc(acc_read[1], 1)
                    weights(0)
                    act.wait_ge(sem("o_ready"), hh + 1)
                    act.activation(VT[:, :], O[:, :], ACT.Copy).then_inc(sem("o_copied"), 1)
                    act.activation(SQ[:, :], O[:, :], ACT.Square).then_inc(sem("o_read"), 1)

                mix(0, True)
                with act.Fori(1, HEADS) as h:
                    mix(h, False)

                for j in range(KT):
                    p = l * PAIRS + PAIR0["bra"] + j
                    w_hi_part(p + 1, 0)
                    act.activation(GB[:, j, :], G[0][:, :], ACT.Tanh, scale=0.5).then_inc(acc_read[0], 1)
                    if j == 0:
                        root(l * AUXN + AUX_HEAD + HEADS - 1, l * UNITS + UNIT_HEAD + HEADS - 1, float(D // P))
                        unit_split(l * UNITS + UNIT_HEAD + HEADS - 1, 0, True, AOHI[:, HEADS - 1, :], ACT.Identity,
                                   subg[:, ds(l, 1)], 0.0)
                    if j == 3:
                        act.wait_ge(sem("aux_ready"), l * AUXN + AUX_MEAN + 1)
                        act.activation(F[1][:, :], AUX[:, :], ACT.Copy).then_inc(sem("aux_read"), 1)
                    if j in (3, 4):
                        for n in range(4 * (j - 3), 4 * (j - 3) + 4):
                            act.wait_ge(sem("xc_ready"), l * KT + n + 1)
                            act.wait_ge(sem("lnadd"), l * KT + n)
                            act.activation(SQ[:, :], C[:, n, :], ACT.Square).then_inc(sem("lnsq"), 1)
                    if j == 5:
                        root(l * AUXN + AUX_VAR, l * UNITS + UNIT_LN)
                    for n in {5: (0, 1), 6: (2, 3, 4), 7: (5, 6, 7)}.get(j, ()):
                        unit_split(l * UNITS + UNIT_LN + n, n % 2, n == 0, CHI[:, n, :], ACT.Silu,
                                   PT[:, ds(l * PC + PC_LNG + n, 1)], PT[:, ds(l * PC + PC_LNB + n, 1)])
                    w_hi_part(p + 1, 1)
                with act.Fori(0, KT // 2) as i:
                    for t in range(2):
                        w_hi_part(l * PAIRS + PAIR0["brb"] + i + 1, t)
                        act.wait_ge(sem("merged"), l * KT + i * 2 + (t + 1))
                        act.activation(tile(MHI2, i * 2 + t), F[t][:, :], ACT.Copy).then_inc(sem("m_hi"), 1)
                with act.Fori(0, KT // 2) as i:
                    for t in range(2):
                        w_hi_part(l * PAIRS + PAIR0["mo"] + i + 1, t)
                        square_x(l * USES + USE0["mo"] + i, t, (l * 3 + 2) * KT, i * 2 + t)

        root(DEPTH * AUXN, DEPTH * UNITS)
        for j in range(KT):
            act.wait_ge(sem("unit_t"), DEPTH * UNITS + j + 1)
            if j >= 2:
                act.wait_ge(sem("yt_ready"), j - 1)
            act.activation(F[j % 2][:, :], T[j % 2][:, :], ACT.Identity, scale=PT2[:, j:j + 1]).then_inc(sem("fin"), 1)
        act.wait_ge(sem("bt_in"), 16 * (DEPTH * HEADS + 1))

    @block.vector
    def _(dve):
        def w_lo_part(pair, slot, n=8):
            dve.wait_ge(w_hi[slot], pair + 1)
            dve.tensor_tensor(wlo[slot][:, 0:n, :], raw[slot][:, 0:n, :], whi[slot][:, 0:n, :].bitcast(F32),
                              ALU.subtract).then_inc(w_lo[slot], 1)

        def clear_sum():
            dve.memset(SSUM[:, :], 0.0).then_inc(sem("ssum_clear"), 1)

        def sum_cleared(count):
            dve.wait_ge(sem("ssum_clear"), count)

        def reciprocal(aux, r):
            dve.wait_ge(sem("aux_read"), aux + 1)
            dve.reciprocal(RSTD[:, :], RSTD[:, :]).then_inc(sem("rstd_ready"), 1)
            dve.wait_ge(sem("rstd_ready"), r + 1)

        def unit_scale(u, b, first, src):
            dve.wait_ge(sem("unit_hi"), u if first else u - 1)
            dve.tensor_tensor(T[b][:, :], src, RSTD[:, :], ALU.mult).then_inc(sem("unit_t"), 1)

        def unit_rest(u, b, lo, hi):
            dve.wait_ge(sem("unit_hi"), u + 1)
            dve.tensor_tensor(lo, F[b][:, :], hi.bitcast(F32), ALU.subtract).then_inc(sem("unit_lo"), 1)

        def norm_units(l, k):
            reciprocal(l * AUXN + AUX_NORM[k], l * RSN + RS_NORM[k])
            u = l * UNITS + UNIT_NORM[k]
            for j in range(KT + 1):
                if j < KT:
                    unit_scale(u + j, j % 2, j == 0, X[:, j, :])
                if j:
                    unit_rest(u + (j - 1), (j - 1) % 2, HLO[:, j - 1, :], HHI[:, j - 1, :])

        def update_x(pair, slot, bank_use, t, k, j):
            dve.wait_ge(w_used[slot], pair + 1)
            dve.scalar_tensor_tensor(out=tile(X2, j), in0=G[t][:, :], scalar=GC[:, k, ds(j, 1)], in1=tile(X2, j),
                                     op0=ALU.mult, op1=ALU.add).then_inc(acc_read[t], 1)

        def add_square(n8, j):
            dve.wait_ge(sem("sq_ready"), n8 + j + 1)
            dve.wait_ge(sem("ssum_add"), n8 + j)
            dve.tensor_tensor(SSUM[:, :], SSUM[:, :], SQ[:, :], ALU.add).then_inc(sem("ssum_add"), 1)

        def mod_columns(l, hc):
            dve.wait_ge(sem("modp_ready"), l * HC + hc + 1)
            dve.scalar_tensor_tensor(out=MODC[:, ds(l * (NMOD * KT) + hc * 4, 4)], in0=O[:, 0:4], scalar=float(D),
                                     in1=PT[:, ds(l * PC + PC_ADA + hc * 4, 4)], op0=ALU.mult, op1=ALU.add)\
                .then_inc(sem("modc_ready"), 1)

        def scale_columns(l, k):
            return dve.scalar_tensor_tensor(out=AC[:, k, :], in0=MODC[:, ds(l * (NMOD * KT) + (3 * k + 1) * KT, KT)],
                                            scalar=1.0, in1=PT[:, ds(l * PC + PC_NORM[k], KT)], op0=ALU.add, op1=ALU.mult)

        dve.memset(TB[BUCKETS:BUCKETS + 1, :], NEG).then_inc(sem("tb_rows"), 1)
        clear_sum()
        sum_cleared(1)
        for n, (dst, src) in enumerate(((PT[:, 0:PC], TP[0][:, 0:PC]), (PT[:, PC:2 * PC], TP[1][:, 0:PC]),
                                        (PT2[:, :], O[:, 0:2 * KT]))):
            dve.wait_ge(sem("ptp_ready"), n + 1)
            dve.tensor_copy(dst, src).then_inc(sem("pt_ready"), 1)
        for j in range(KT + 1):
            if j < KT:
                dve.wait_ge(sem("xp_ready"), j + 1)
                dve.tensor_copy(X[:, j, :], bank[2 + j % 2][:, :]).then_inc(sem("x_ready"), 1)
            if j:
                add_square(0, j - 1)
        dve.wait_ge(sem("tbp_ready"), 1)
        dve.tensor_copy(TB[0:BUCKETS, :], TP[0][0:BUCKETS, 0:HEADS]).then_inc(sem("tb_rows"), 1)
        dve.wait_ge(sem("tb_rows"), 2)
        dve.tensor_copy(TBX[0:BUCKETS + 1, :, :], TB[0:BUCKETS + 1, :].unsqueeze(2).to_broadcast([BUCKETS + 1, HEADS, P]))\
            .then_inc(sem("tbx_ready"), 1)
        dve.wait_ge(sem("lambda_in"), 16 * 4 * DEPTH)
        for l in range(DEPTH):
            for n in range(2):
                dve.tensor_tensor_reduce(LV[:, l, 2 * n, :], LV[:, l, 2 * n, :], LV[:, l, 2 * n + 1, :], 1.0, 0.0,
                                         ALU.mult, ALU.add, lam_dot[:, 2 * l + n:2 * l + n + 1]).then_inc(sem("lam_dots"), 1)
        dve.wait_ge(sem("ca_ready"), 1)
        acc = ACC[:, 0:4, :].rearrange("p s c -> p (s c)")
        for k in range(KT):
            dve.wait_ge(sem(f"ada0_in{k}"), 16)
            if k == 0:
                dve.tensor_scalar(acc, ADA0[:, 0, :], CA[:, 0:1], None, ALU.mult).then_inc(sem("ada0_step"), 1)
                continue
            dve.wait_ge(sem("ada0_step"), k)
            if k < KT - 1:
                dve.scalar_tensor_tensor(out=acc, in0=ADA0[:, k, :], scalar=CA[:, k:k + 1], in1=acc,
                                         op0=ALU.mult, op1=ALU.add).then_inc(sem("ada0_step"), 1)
                continue
            for s in range(4):
                dve.scalar_tensor_tensor(out=ACC[:, s, :], in0=ADA0[:, k, s * HCW:(s + 1) * HCW], scalar=CA[:, k:k + 1],
                                         in1=ACC[:, s, :], op0=ALU.mult, op1=ALU.add).then_inc(sem("mod_acc"), 1)
        for s in range(2):
            w_lo_part(0, s)
        dve.wait_ge(sem("lam_exps"), 1)
        for l in range(DEPTH):
            lam_init = 0.8 - 0.6 * math.exp(-0.3 * l)
            dve.scalar_tensor_tensor(out=nlam[:, l:l + 1], in0=lam_exp[:, 2 * l + 1:2 * l + 2], scalar=lam_init,
                                     in1=lam_exp[:, 2 * l:2 * l + 1], op0=ALU.subtract, op1=ALU.subtract)\
                .then_inc(sem("lam_ready"), 1)
            dve.tensor_scalar(subg[:, l:l + 1], PT[:, l * PC + PC_SUB:l * PC + PC_SUB + 1], 1.0 - lam_init, None,
                              ALU.mult).then_inc(sem("lam_ready"), 1)
        dve.wait_ge(sem("lam_ready"), 2 * DEPTH)

        with dve.Fori(0, DEPTH) as l:
            for w in range(2):
                n_in, n_out = f"ffn{w + 1}_in", f"ffn{w + 1}_out"
                if w == 0:
                    for hc in range(4):
                        mod_columns(l, hc)
                    dve.wait_ge(sem("modc_ready"), l * HC + 4)
                    scale_columns(l, 0).then_inc(sem("ac_ready"), 1)
                norm_units(l, 2 * w)

                def ffn_tile(i):
                    p = l * PAIRS + PAIR0[n_in] + i
                    u = l * USES + USE0[n_in] + i
                    w_lo_part(p + 1, 0)
                    w_lo_part(p + 1, 1)
                    dve.wait_ge(acc_read[0], u + 1)
                    dve.wait_ge(w_used[1], p + 1)
                    dve.wait_ge(sem("s_lo"), (l * 2 + w) * FT + i)
                    dve.tensor_tensor(F[0][:, :], G[1][:, :], T[0][:, :], ALU.mult).then_inc(acc_read[1], 1)
                    dve.wait_ge(sem("s_hi"), (l * 2 + w) * FT + i + 1)
                    dve.tensor_tensor(tile(SLO2, i), F[0][:, :], tile(SHI2, i).bitcast(F32), ALU.subtract)\
                        .then_inc(sem("s_lo"), 1)

                if w == 0:
                    with dve.Fori(0, 5) as i:
                        ffn_tile(i)
                    mod_columns(l, 4)
                    mod_columns(l, 5)
                    with dve.Fori(0, 2) as g:
                        for q in range(8):
                            ffn_tile(g * 8 + 5 + q)
                            if q % 4 < 3:
                                mod_columns(l, g * 6 + (6 + 3 * (q // 4) + q % 4))
                    with dve.Fori(FT - 1, FT) as i:
                        ffn_tile(i)
                    dve.wait_ge(sem("modc_ready"), l * HC + HC)
                    for k in (1, 2):
                        scale_columns(l, k)
                    for k in range(3):
                        g = dve.tensor_scalar(GC[:, k, :], MODC[:, ds(l * (NMOD * KT) + (3 * k + 2) * KT, KT)], 0.5, None, ALU.mult)
                    g.then_inc(sem("ac_ready"), 1)
                    dve.wait_ge(sem("ac_ready"), l * 2 + 2)
                else:
                    with dve.Fori(0, FT) as i:
                        ffn_tile(i)

                clear_sum()
                with dve.Fori(0, KT // 2) as i:
                    for m in range(6):
                        p = l * PAIRS + PAIR0[n_out] + i * 3 + m // 2
                        w_lo_part(p + 1, m % 2, OUTG[(m + 2) % 3] if m < 4 else 8)
                        if m % 3 == 2:
                            t = m // 3
                            update_x(p, m % 2, l * USES + USE0[n_out] + i, t, 2 * w, i * 2 + t)
                            sum_cleared(l * ZEROS + 1 + (ZERO_FFN2 if w else ZERO_FFN1))
                            add_square((l * 3 + 1 + 2 * w) * KT, i * 2 + t)
                if w == 1:
                    continue

                norm_units(l, 1)
                clear_sum()
                dve.memset(Z[:, 0:PADL], 0.0).then_inc(sem("z_pad"), 1)
                dve.wait_ge(sem("z_pad"), l + 1)

                def taps(h, lo, hi):
                    q = l * HEADS + h
                    for t in range(lo, hi):
                        wt = CW2[:, ds(q * CK + t, 1)]
                        if t == 0:
                            dve.wait_ge(sem("z_ready"), q + 1)
                            ins = dve.tensor_scalar(CAB[0][:, :], Z[:, 0:TOK], wt, PT[:, ds(l * PC + PC_DWB + h, 1)],
                                                    ALU.mult, ALU.add)
                        elif t == 1:
                            ins = dve.tensor_scalar(CAB[1][:, :], Z[:, 1:1 + TOK], wt, None, ALU.mult)
                        else:
                            dve.wait_ge(sem("tap_done"), q * DVE_TAPS + (t - 1))
                            ins = dve.scalar_tensor_tensor(out=CAB[t % 2][:, :], in0=Z[:, t:t + TOK], scalar=wt,
                                                           in1=CAB[t % 2][:, :], op0=ALU.mult, op1=ALU.add)
                        ins.then_inc(sem("tap_done"), 1)

                def join(h):
                    q = l * HEADS + h
                    c = tile(C2, h)
                    dve.wait_ge(sem("tap_done"), q * DVE_TAPS + DVE_TAPS)
                    dve.tensor_tensor(c, CAB[0][:, :], CAB[1][:, :], ALU.add).then_inc(sem("c_part"), 1)
                    dve.wait_ge(sem("c_part"), q + 1)
                    dve.wait_ge(sem("cp_ready"), q + 1)
                    dve.tensor_tensor(c, c, CP[:, :], ALU.add).then_inc(sem("c_ready"), 1)
                    dve.wait_ge(sem("c_ready"), q + 1)
                    dve.wait_ge(sem("csum"), q)
                    sum_cleared(l * ZEROS + 1 + ZERO_CONV)
                    dve.tensor_tensor(SSUM[:, :], SSUM[:, :], c, ALU.add).then_inc(sem("csum"), 1)

                def mix(h, first):
                    hh = l * HEADS + h
                    p = l * PAIRS + PAIR0["mix"] + h * 3
                    b = l * USES + USE0["mix"] + h * 3
                    uh = l * UNITS + UNIT_HEAD + h - 1

                    def conv(lo, hi):
                        if not first:
                            taps(h - 1, lo, hi)

                    def scores(i):
                        par, r, n = i % 2, QB - 1 - i, (i + 1) * P
                        si = hh * 4 + r
                        dve.wait_ge(sem("s_ready"), si + 1)
                        dve.wait_ge(sem("t_ready"), si - 1 if r >= 2 else hh * 4)
                        dve.memset(spare[:, 1:2], 0.0)
                        for m in range(2):
                            dve.tensor_tensor_reduce(PR[par][m][:, 0:n], S[m][:, 0:n], BT[:, TOK - n:TOK], 1.0, NEG,
                                                     ALU.add, ALU.max, mx[:, par, m:m + 1]).then_inc(sem("max_done"), 1)
                        dve.wait_ge(sem("max_done"), (si + 1) * 2)
                        dve.tensor_scalar(nmx[:, par, :], mx[:, par, :], -1.0, None, ALU.mult).then_inc(sem("nmax_ready"), 1)

                    def combine(i):
                        par, n = i % 2, (i + 1) * P
                        si = hh * 4 + (QB - 1 - i)
                        p0, p1 = PR[par][0][:, 0:n], PR[par][1][:, 0:n]
                        dve.wait_ge(sem("exp_done"), (si + 1) * 2)
                        dve.reciprocal(rinv[:, par, :], rsum[:, par, :]).then_inc(sem("comb"), 1)
                        dve.wait_ge(sem("comb"), si * 3 + 1)
                        dve.tensor_scalar(rlam[:, par:par + 1], rinv[:, par, 1:2], nlam[:, ds(l, 1)], None, ALU.mult)\
                            .then_inc(sem("comb"), 1)
                        dve.wait_ge(sem("comb"), si * 3 + 2)
                        dve.tensor_scalar(p1, p1, rlam[:, par:par + 1], None, ALU.mult).then_inc(sem("comb"), 1)
                        dve.wait_ge(sem("comb"), si * 3 + 3)
                        dve.scalar_tensor_tensor(out=p0, in0=p0, scalar=rinv[:, par, 0:1], in1=p1,
                                                 op0=ALU.mult, op1=ALU.add).then_inc(sem("w_ready"), 1)

                    conv(0, 5)
                    w_lo_part(p + 1, 0)
                    conv(5, 6)
                    if not first:
                        reciprocal(l * AUXN + AUX_HEAD + h - 1, l * RSN + RS_HEAD + h - 1)
                        unit_scale(uh, 0, True, VT[:, :])
                    w_lo_part(p + 1, 1)
                    conv(6, 9)
                    if not first:
                        unit_rest(uh, 0, tile(AOLO2, h - 1), tile(AOHI2, h - 1))
                    conv(9, 11)
                    w_lo_part(p + 2, 0)
                    conv(11, 14)
                    dve.wait_ge(sem("bt_in"), (hh + 1) * 16)
                    scores(3)
                    w_lo_part(p + 2, 1)
                    scores(2)
                    conv(14, 18)
                    combine(3)
                    scores(1)
                    conv(18, 22)
                    combine(2)
                    w_lo_part(p + 3, 0)
                    conv(22, 23)
                    scores(0)
                    combine(1)
                    combine(0)
                    if not first:
                        join(h - 1)
                    w_lo_part(p + 3, 1)
                    dve.wait_ge(acc_read[0], b + 3)
                    dve.wait_ge(acc_read[1], b + 2)
                    dve.scalar_tensor_tensor(out=Z[:, PADL:PADL + TOK], in0=F[1][:, :], scalar=1.0, in1=T[1][:, :],
                                             op0=ALU.add, op1=ALU.mult).then_inc(sem("z_ready"), 1)

                mix(0, True)
                with dve.Fori(1, HEADS) as h:
                    mix(h, False)

                dve.wait_ge(acc_read[1], l * USES + USE0["bra"])
                for j in range(KT):
                    p = l * PAIRS + PAIR0["bra"] + j
                    u = l * USES + USE0["bra"] + j
                    w_lo_part(p + 1, 0)
                    if j == 0:
                        uh = l * UNITS + UNIT_HEAD + HEADS - 1
                        reciprocal(l * AUXN + AUX_HEAD + HEADS - 1, l * RSN + RS_HEAD + HEADS - 1)
                        unit_scale(uh, 0, True, VT[:, :])
                        taps(HEADS - 1, 0, 2)
                        unit_rest(uh, 0, AOLO[:, HEADS - 1, :], AOHI[:, HEADS - 1, :])
                        taps(HEADS - 1, 2, 7)
                    if j == 1:
                        taps(HEADS - 1, 7, 15)
                    if j == 2:
                        taps(HEADS - 1, 15, DVE_TAPS)
                        join(HEADS - 1)
                    if j == 3:
                        dve.wait_ge(sem("aux_read"), l * AUXN + AUX_MEAN + 1)
                        clear_sum()
                        sum_cleared(l * ZEROS + 1 + ZERO_LN)
                    if j in (3, 4):
                        n0 = 4 * (j - 3)
                        for n in range(n0, n0 + 5):
                            if n < n0 + 4:
                                dve.tensor_tensor(C[:, n, :], C[:, n, :], F[1][:, :], ALU.subtract).then_inc(sem("xc_ready"), 1)
                            if n > n0:
                                dve.wait_ge(sem("lnsq"), l * KT + n)
                                dve.wait_ge(sem("lnadd"), l * KT + n - 1)
                                dve.tensor_tensor(SSUM[:, :], SSUM[:, :], SQ[:, :], ALU.add).then_inc(sem("lnadd"), 1)
                    if j == 5:
                        reciprocal(l * AUXN + AUX_VAR, l * RSN + RS_VAR)
                    units = {5: (0, 1), 6: (2, 3, 4), 7: (5, 6, 7)}.get(j, ())
                    for n in (*units, None):
                        ul = l * UNITS + UNIT_LN
                        if n is not None:
                            unit_scale(ul + n, n % 2, n == 0, C[:, n, :])
                        if units and n != units[0]:
                            o = units[-1] if n is None else n - 1
                            unit_rest(ul + o, o % 2, CLO[:, o, :], CHI[:, o, :])
                    w_lo_part(p + 1, 1)
                    dve.scalar_tensor_tensor(out=GA[:, j, :], in0=GA[:, j, :], scalar=1.0, in1=G[1][:, :],
                                             op0=ALU.add, op1=ALU.mult).then_inc(acc_read[1], 1)
                with dve.Fori(0, KT // 2) as i:
                    for t in range(2):
                        j = i * 2 + t
                        w_lo_part(l * PAIRS + PAIR0["brb"] + i + 1, t)
                        if t == 0:
                            dve.wait_ge(acc_read[1], l * USES + USE0["brb"] + i)
                        dve.scalar_tensor_tensor(out=T[t][:, :], in0=tile(GB2, j), scalar=1.0, in1=G[t][:, :],
                                                 op0=ALU.add, op1=ALU.mult).then_inc(acc_read[t], 1)
                        dve.wait_ge(acc_read[t], l * USES + USE0["brb"] + i + 1)
                        dve.wait_ge(sem("m_lo"), l * KT + j)
                        dve.tensor_tensor(F[t][:, :], tile(GA2, j), T[t][:, :], ALU.add).then_inc(sem("merged"), 1)
                        dve.wait_ge(sem("m_hi"), l * KT + j + 1)
                        dve.tensor_tensor(tile(MLO2, j), F[t][:, :], tile(MHI2, j).bitcast(F32), ALU.subtract)\
                            .then_inc(sem("m_lo"), 1)
                clear_sum()
                with dve.Fori(0, KT // 2) as i:
                    for t in range(2):
                        p = l * PAIRS + PAIR0["mo"] + i
                        w_lo_part(p + 1, t)
                        update_x(p, t, l * USES + USE0["mo"] + i, t, 1, i * 2 + t)
                        sum_cleared(l * ZEROS + 1 + ZERO_MO)
                        add_square((l * 3 + 2) * KT, i * 2 + t)

        reciprocal(DEPTH * AUXN, DEPTH * RSN)
        for j in range(KT + 2):
            if j < KT:
                if j == 0:
                    dve.wait_ge(sem("unit_hi"), DEPTH * UNITS)
                if j >= 2:
                    dve.wait_ge(sem("fin"), j - 1)
                dve.tensor_tensor(T[j % 2][:, :], X[:, j, :], RSTD[:, :], ALU.mult).then_inc(sem("unit_t"), 1)
            if j >= 2:
                n = j - 2
                dve.wait_ge(sem("yt_ready"), n + 1)
                dve.tensor_copy(YO[:, :, n * P:(n + 1) * P], TP[n % 2][:, :].rearrange("p (t c) -> p t c", c=P))\
                    .then_inc(sem("y_ready"), 1)

    @block.tensor
    def _(pe):
        def slab(pair, slot, acc, hi, lo, k0=0, n=8, first=True, last=True, ready=None, at_half=None):
            pe.wait_ge(w_hi[slot], pair + 1)
            pe.wait_ge(w_lo[slot], pair + 1)
            for k in range(n):
                if ready:
                    ready(k0 + k)
                if at_half and k == n // 2:
                    at_half()
                wh, wl = whi[slot][:, k, :], wlo[slot][:, k, :]
                pe.matmul(acc, wh, hi[:, k0 + k, :], start=first and k == 0, stop=False)
                pe.matmul(acc, wh, lo[:, k0 + k, :], start=False, stop=False)
                mm = pe.matmul(acc, wl, hi[:, k0 + k, :], start=False, stop=last and k == n - 1)
            mm.then_inc(w_used[slot], 1)

        def mean(aux, src):
            pe.wait_ge(sem("aux_read"), aux)
            pe.matmul(AUX[:, :], invd[:, :], src, start=True, stop=True).then_inc(sem("aux_ready"), 1)

        def norm_mean(aux, n8):
            pe.wait_ge(sem("ssum_add"), n8)
            mean(aux, SSUM[:, :])

        def mod_sum(l, hc, slot):
            c = l * HC + hc
            pe.wait_ge(sem("mod_acc"), c + 1)
            pe.wait_ge(sem("modc_ready"), c)
            for q in range(4):
                mm = pe.matmul(O[:, q:q + 1], ACC[:, slot, q * P:(q + 1) * P], invd[:, 0:1], start=True, stop=True)
            mm.then_inc(sem("modp_ready"), 1)

        pe.wait_ge(sem("consts"), 3)
        pe.wait_ge(sem("rows_in"), 16 * (8 * DEPTH + 2))
        pe.transpose(TP[0][:, 0:PC], PV[0][0:PC, :], ident[0:PC, 0:PC]).then_inc(sem("ptp_ready"), 1)
        pe.transpose(TP[1][:, 0:PC], PV[1][0:PC, :], ident[0:PC, 0:PC]).then_inc(sem("ptp_ready"), 1)
        pe.transpose(O[:, 0:2 * KT], PV2[0:2 * KT, :], ident[0:2 * KT, 0:2 * KT]).then_inc(sem("ptp_ready"), 1)
        pe.wait_ge(sem("taps_in"), 16 * DEPTH)
        for l in range(DEPTH):
            for h in range(HEADS):
                mm = pe.transpose(G[l][:, h * CK:(h + 1) * CK], CWR[0:CK, l, h * P:(h + 1) * P], ident[0:CK, 0:CK])
            mm.then_inc(sem("tapsp_ready"), 1)
        for j in range(KT):
            if j >= 2:
                pe.wait_ge(sem("x_ready"), j - 1)
            for t in range(QB):
                if j == 0:
                    pe.wait_ge(sem(f"x_in{t}"), 16)
                mm = pe.transpose(bank[2 + j % 2][:, t * P:(t + 1) * P], XS[:, t, j * P:(j + 1) * P], ident[:, :])
            mm.then_inc(sem("xp_ready"), 1)
        pe.wait_ge(sem("table_in"), 32)
        pe.wait_ge(sem("pt_ready"), 3)
        pe.transpose(TP[0][0:BUCKETS, 0:HEADS], TBR[0:HEADS, :], ident[0:HEADS, 0:HEADS]).then_inc(sem("tbp_ready"), 1)
        pe.wait_ge(sem("tbx_ready"), 1)
        for h in range(HEADS):
            pe.wait_ge(sem("br_copied"), h)
            pe.matmul(O[:, :], TBX[0:BUCKETS + 1, h, :], OH[0:BUCKETS + 1, 0:TOK], start=True, stop=True)
            pe.matmul(AUX[:, 0:P], TBX[0:BUCKETS + 1, h, :], OH[0:BUCKETS + 1, TOK:TOK + P], start=True, stop=True)\
                .then_inc(sem("br_ready"), 1)
        pe.wait_ge(sem("br_copied"), HEADS)
        pe.wait_ge(sem("cw_ready"), DEPTH)

        with pe.Fori(0, DEPTH) as l:
            pe.wait_ge(sem("o_read"), l * HEADS)
            for w in range(2):
                n_in, n_out = f"ffn{w + 1}_in", f"ffn{w + 1}_out"
                norm_mean(l * AUXN + AUX_NORM[2 * w], (l * 3 + 2 * w + 1) * KT)
                if w == 0:
                    for hc in range(4):
                        mod_sum(l, hc, hc)

                def ffn_tile(i):
                    p = l * PAIRS + PAIR0[n_in] + i
                    u = l * USES + USE0[n_in] + i
                    pe.wait_ge(acc_read[0], u)
                    slab(p, 0, G[0][:, :], HHI, HLO,
                         ready=lambda k: pe.wait_ge(sem("unit_lo"), l * UNITS + UNIT_NORM[2 * w] + k + 1))
                    pe.wait_ge(acc_read[1], u)
                    slab(p, 1, G[1][:, :], HHI, HLO)

                if w == 0:
                    with pe.Fori(0, 5) as i:
                        ffn_tile(i)
                    mod_sum(l, 4, 4)
                    mod_sum(l, 5, 5)
                    with pe.Fori(0, 2) as g:
                        for q in range(8):
                            ffn_tile(g * 8 + 5 + q)
                            if q % 4 < 3:
                                mod_sum(l, g * 6 + (6 + 3 * (q // 4) + q % 4), 3 * (q // 4) + q % 4)
                    with pe.Fori(FT - 1, FT) as i:
                        ffn_tile(i)
                else:
                    with pe.Fori(0, FT) as i:
                        ffn_tile(i)

                with pe.Fori(0, KT // 2) as i:
                    for m in range(6):
                        t, g = m // 3, m % 3
                        if g == 0:
                            pe.wait_ge(acc_read[t], l * USES + USE0[n_out] + i)
                        k0 = sum(OUTG[:g])
                        pe.wait_ge(sem("s_lo"), (l * 2 + w) * FT + (k0 + OUTG[g]))
                        slab(l * PAIRS + PAIR0[n_out] + i * 3 + m // 2, m % 2, G[t][:, :], SHI, SLO,
                             k0, OUTG[g], g == 0, g == 2)
                if w == 1:
                    continue

                norm_mean(l * AUXN + AUX_NORM[1], (l * 3 + 2) * KT)

                def mix(h, first):
                    hh = l * HEADS + h
                    p = l * PAIRS + PAIR0["mix"] + h * 3
                    b = l * USES + USE0["mix"] + h * 3

                    def scores(i):
                        si, n = hh * 4 + (QB - 1 - i), (i + 1) * P
                        pe.wait_ge(sem("nmax_ready"), si)
                        for m in range(2):
                            mm = pe.matmul(S[m][:, 0:n], QT[m * HD:(m + 1) * HD, i * P:(i + 1) * P],
                                           KTT[m * HD:(m + 1) * HD, 0:n], start=True, stop=True)
                        mm.then_inc(sem("s_ready"), 1)

                    def turn_v():
                        pe.wait_ge(acc_read[0], b + 2)
                        for j in range(QB):
                            mm = pe.transpose(TP[0][:, j * P:(j + 1) * P], VT[:, j * P:(j + 1) * P], ident[:, :])
                        mm.then_inc(sem("vtp_ready"), 1)

                    def turn_weights(i):
                        si = hh * 4 + (QB - 1 - i)
                        pe.wait_ge(sem("w_ready"), si + 1)
                        if i == 2:
                            pe.wait_ge(sem("v_ready"), hh + 1)
                        elif i < 2:
                            pe.wait_ge(sem("wt_ready"), si - 1)
                        for j in range(i + 1):
                            mm = pe.transpose(TP[i % 2][:, j * P:(j + 1) * P], PR[i % 2][0][:, j * P:(j + 1) * P], ident[:, :])
                        mm.then_inc(sem("t_ready"), 1)

                    def values():
                        pe.wait_ge(sem("wt_ready"), hh * 4 + 4)
                        pe.wait_ge(sem("o_read"), hh)
                        for j in range(QB):
                            mm = pe.matmul(O[:, j * P:TOK], V[:, j, :], WT[:, j, j * P:TOK], start=(j == 0), stop=(j == QB - 1))
                        mm.then_inc(sem("o_ready"), 1)

                    pe.wait_ge(acc_read[0], b)
                    slab(p, 0, G[0][:, :], HHI, HLO,
                         ready=lambda k: pe.wait_ge(sem("unit_lo"), l * UNITS + UNIT_NORM[1] + k + 1))
                    if not first:
                        pe.wait_ge(sem("o_read"), hh)
                        mean(l * AUXN + AUX_HEAD + h - 1, SQ[:, :])
                    pe.wait_ge(acc_read[1], b)
                    slab(p, 1, G[1][:, :], HHI, HLO)
                    pe.wait_ge(acc_read[0], b + 1)
                    slab(p + 1, 0, G[0][:, :], HHI, HLO)
                    pe.wait_ge(acc_read[1], b + 1)
                    slab(p + 1, 1, G[1][:, :], HHI, HLO, at_half=lambda: scores(3))
                    scores(2)
                    turn_v()
                    pe.wait_ge(acc_read[0], b + 2)

                    def second():
                        turn_weights(3)
                        scores(1)
                    slab(p + 2, 0, G[0][:, :], HHI, HLO, at_half=second)
                    turn_weights(2)
                    scores(0)
                    pe.wait_ge(acc_read[1], b + 2)
                    slab(p + 2, 1, G[1][:, :], HHI, HLO, at_half=lambda: turn_weights(1))
                    turn_weights(0)
                    values()

                mix(0, True)
                with pe.Fori(1, HEADS) as h:
                    mix(h, False)

                def bra(j, first=False):
                    p = l * PAIRS + PAIR0["bra"] + j
                    u = l * USES + USE0["bra"] + j
                    pe.wait_ge(acc_read[0], u)
                    slab(p, 0, G[0][:, :], HHI, HLO)
                    if first:
                        pe.wait_ge(sem("o_read"), l * HEADS + HEADS)
                        mean(l * AUXN + AUX_HEAD + HEADS - 1, SQ[:, :])
                        pe.wait_ge(sem("unit_lo"), l * UNITS + UNIT_HEAD + HEADS)
                    pe.wait_ge(acc_read[1], u)
                    slab(p, 1, G[1][:, :], AOHI, AOLO)

                bra(0, True)
                with pe.Fori(1, 3) as j:
                    bra(j)
                pe.wait_ge(sem("csum"), (l + 1) * KT)
                mean(l * AUXN + AUX_MEAN, SSUM[:, :])
                with pe.Fori(3, 5) as j:
                    bra(j)
                pe.wait_ge(sem("lnadd"), (l + 1) * KT)
                mean(l * AUXN + AUX_VAR, SSUM[:, :])
                with pe.Fori(5, KT) as j:
                    bra(j)
                with pe.Fori(0, KT // 2) as i:
                    for t in range(2):
                        pe.wait_ge(acc_read[t], l * USES + USE0["brb"] + i)
                        slab(l * PAIRS + PAIR0["brb"] + i, t, G[t][:, :], CHI, CLO,
                             ready=lambda k: pe.wait_ge(sem("unit_lo"), l * UNITS + UNIT_LN + k + 1))
                with pe.Fori(0, KT // 2) as i:
                    for t in range(2):
                        pe.wait_ge(acc_read[t], l * USES + USE0["mo"] + i)
                        slab(l * PAIRS + PAIR0["mo"] + i, t, G[t][:, :], MHI, MLO,
                             ready=lambda k: pe.wait_ge(sem("m_lo"), l * KT + k + 1))

        norm_mean(DEPTH * AUXN, (DEPTH * 3 + 1) * KT)
        for j in range(KT):
            pe.wait_ge(sem("fin"), j + 1)
            if j >= 2:
                pe.wait_ge(sem("y_ready"), j - 1)
            for t in range(QB):
                mm = pe.transpose(TP[j % 2][:, t * P:(t + 1) * P], F[j % 2][:, t * P:(t + 1) * P], ident[:, :])
            mm.then_inc(sem("yt_ready"), 1)

    ctx.close()


NAMES = ["x", "c", "ffn1_norm", "ffn1_w_in", "ffn1_w_out", "mix_norm", "w_mix_in", "lambda_q1", "lambda_k1",
         "lambda_q2", "lambda_k2", "subln_gain", "w_attn_branch", "conv_dw", "conv_dw_bias", "conv_ln_gain",
         "conv_ln_bias", "w_conv_branch", "w_mix_out", "ffn2_norm", "ffn2_w_in", "ffn2_w_out", "ada_w", "ada_b",
         "rel_bias", "final_norm"]


def kernel(**inputs):
    import concourse.bacc as bacc
    from concourse.bass_utils import run_bass_kernel_spmd

    nc = bacc.Bacc("TRN2", target_bir_lowering=False, num_devices=1)
    arrays, aps = {}, {}
    for name in NAMES:
        arr = np.ascontiguousarray(inputs[name])
        arrays[f"in_{name}"] = arr
        aps[name] = nc.dram_tensor(f"in_{name}", arr.shape, F32, kind="ExternalInput").ap()
    sel = bias_selection()
    arrays["in_bias_selection"] = sel
    onehot = nc.dram_tensor("in_bias_selection", sel.shape, F32, kind="ExternalInput").ap()
    out = nc.dram_tensor("out_0", (1, TOK, D), F32, kind="ExternalOutput").ap()
    build(nc, aps, onehot, out)
    r = run_bass_kernel_spmd(nc, [arrays], core_ids=[0])
    return r.results[0]["out_0"]
```

```python
import math
from contextlib import ExitStack

import numpy as np

import concourse.bass as bass
from concourse import mybir
from concourse.bass import ds

F32 = mybir.dt.float32
F32R = mybir.dt.float32r
ACT = mybir.ActivationFunctionType
ALU = mybir.AluOpType

P = 128
D = 1024
TOK = 512
DEPTH = 2
HEADS = D // 128
HD = 64
CK = 31
PADL = CK - 1
FF = ((8 * D // 3 + 255) // 256) * 256
BUCKETS = 32
MAXDIST = 128
EPS = 1e-6
NEG = -3.0e38

KT = D // P
FT = FF // P
QB = TOK // P
NMOD = 9
CHUNKS_IN = (3, 2)
CHUNKS_OUT = 4
CHUNK_SEQ = dict(ffn1_in=0, ffn1_out=3, ffn2_in=7)
GROUP = 7
GROUP_STEPS = ((0, 1), (2, 3), (4, 5), (6,), (7,), (), ())
OUT_STEPS = ((0, 1), (2,), (3, 4), (5,), (6, 7), ())
ROWS_MAX = 4
OUTG = (8, 8, 6)
assert sum(OUTG) == FT and DEPTH == 2 and 1 + CHUNKS_IN[0] * GROUP == FT

PH_PAIRS = dict(ffn1_in=FT, ffn1_out=12, mix=3 * HEADS, gb=KT // 2, ab=KT // 2, brb=KT // 2, mo=KT // 2, ffn2_in=FT, ffn2_out=12)
PH_USES = dict(ffn1_in=FT, ffn1_out=KT // 2, mix=3 * HEADS, gb=KT // 2, ab=KT // 2, brb=KT // 2, mo=KT // 2, ffn2_in=FT, ffn2_out=KT // 2)


def starts(sizes):
    out, at = {}, 0
    for name, n in sizes.items():
        out[name] = at
        at += n
    return out, at


PAIR0, PAIRS = starts(PH_PAIRS)
USE0, USES = starts(PH_USES)

AUXN = 3 + HEADS + 2
AUX_NORM = (0, 1, AUXN - 1)
AUX_HEAD, AUX_MEAN, AUX_VAR = 2, 2 + HEADS, 3 + HEADS
RSN = 3 + HEADS + 1
RS_NORM = (0, 1, RSN - 1)
RS_HEAD, RS_VAR = 2, 2 + HEADS
UNITS = 3 * KT + HEADS + KT
UNIT_NORM = (0, KT, UNITS - KT)
UNIT_HEAD, UNIT_LN = 2 * KT, 2 * KT + HEADS
ZERO_FFN1, ZERO_CONV, ZERO_LN, ZERO_MO, ZERO_FFN2, ZEROS = 1, 2, 3, 4, 5, 5

LN_MEAN, LN_VAR = KT // 2 - 1, 5
LN_UNITS = {5: (0, 1), 6: (2, 3, 4), 7: (5, 6, 7)}

PC_NORM = (0, 8, 16)
PC_DWB, PC_LNG, PC_LNB, PC_SUB, PC_ADA = 24, 32, 40, 48, 49
PC = PC_ADA + NMOD * KT
DVE_TAPS = 23
POOL_TAPS = CK - DVE_TAPS


def bias_selection():
    x = np.arange(TOK + P)
    dist = (TOK - 1) - x
    n = np.maximum(dist, 0)
    exact = BUCKETS // 2
    nf = np.maximum(n, 1).astype(np.float32)
    large = exact + (np.log(nf / np.float32(exact)) / np.float32(math.log(MAXDIST / exact))
                     * np.float32(BUCKETS - exact)).astype(np.int32)
    large = np.minimum(large, BUCKETS - 1)
    bucket = np.where(n < exact, n, large)
    sel = np.zeros((BUCKETS + 1, x.size), np.float32)
    ok = dist >= 0
    sel[bucket[ok], x[ok]] = 1.0
    sel[BUCKETS, ~ok] = 1.0
    return sel



def build(nc, a, onehot, out):
    ctx = ExitStack()
    names = {}

    def sem(name):
        if name not in names:
            names[name] = ctx.enter_context(nc.semaphore(name))
        return names[name]

    place = [(nc.sbuf_base + 31) // 32 * 32]

    def at(name, shape, dt, offset=None):
        size = int(np.prod(shape[1:])) * 4
        if offset is None:
            offset = place[0]
            place[0] += (size + 31) // 32 * 32
        assert offset + size <= nc.sbuf_usable_end - 64, name
        return nc.alloc_sbuf_tensor_at(name, shape, dt, offset=offset)

    KB = 1024
    X = at("x_res", [P, KT, TOK], F32)
    h0 = place[0]
    HHI = at("h_hi", [P, KT, TOK], F32R)
    HLO = at("h_lo", [P, KT, TOK], F32R)
    r0 = place[0]
    place[0] += 96 * KB
    raw = [at(f"w_raw{s}", [P, 8, P], F32) for s in range(2)]
    whi = [at(f"w_hi{s}", [P, 8, P], F32R) for s in range(2)]
    wlo = [at(f"w_lo{s}", [P, 8, P], F32R) for s in range(2)]
    SQ = at("squares", [P, TOK], F32)
    SSUM = at("running_sum", [P, TOK], F32)
    RSTD = at("rstd", [P, TOK], F32)
    T = [at(f"scaled{i}", [P, TOK], F32) for i in range(2)]
    F = [at(f"full{i}", [P, TOK], F32) for i in range(2)]
    ada_raw = [at(f"ada_raw{i}", [P, D], F32) for i in range(2)]
    acc0 = place[0]
    ACC = at("ada_acc", [P, D], F32)
    mr0 = place[0]
    MR = at("mod_rows", [P, TOK], F32)
    tap_tmp = [at(f"tap_tmp{i}", [P, TOK], F32, acc0 + 2 * KB * i) for i in range(2)]
    SEL = at("row_select", [P, 64 + ROWS_MAX - 1], F32)
    BT = at("bias_tile", [P, TOK], F32)
    ident = at("ident", [P, P], F32)
    invd = at("inv_d", [P, P], F32)
    PT = at("params", [P, DEPTH * PC], F32)
    PT2 = at("params2", [P, 2 * KT], F32)
    CA = at("c_act", [P, KT], F32)
    MODC = at("modulation", [P, DEPTH * NMOD * KT], F32)
    AC = at("norm_scale", [P, 3, KT], F32)
    GC = at("gates", [P, 3, KT], F32)
    CW = at("conv_taps", [P, DEPTH * HEADS, CK], F32)
    tapw = at("pool_taps", [P, POOL_TAPS], F32)
    spare = at("spare", [P, 2], F32)
    eps = at("eps", [P, 1], F32)
    lam_dot = at("lam_dot", [P, 2 * DEPTH], F32)
    lam_exp = at("lam_exp", [P, 2 * DEPTH], F32)
    nlam = at("neg_lambda", [P, DEPTH], F32)
    subg = at("subln", [P, DEPTH], F32)
    mx = at("row_max", [P, 2, 2], F32)
    nmx = at("neg_row_max", [P, 2, 2], F32)
    rsum = at("row_sum", [P, 2, 2], F32)
    rinv = at("row_inv", [P, 2, 2], F32)
    rlam = at("row_inv_lam", [P, 2], F32)
    SHI = at("s_hi", [P, FT, TOK], F32R, r0)
    SLO = at("s_lo", [P, FT, TOK], F32R, r0 + FT * TOK * 4)
    AOHI = at("ao_hi", [P, KT, TOK], F32R, r0)
    AOLO = at("ao_lo", [P, KT, TOK], F32R, r0 + 16 * KB)
    C = at("conv", [P, KT, TOK], F32, r0 + 32 * KB)
    CHI = at("conv_hi", [P, KT, TOK], F32R, r0 + 32 * KB)
    GA = at("gate_a", [P, KT, TOK], F32, r0 + 48 * KB)
    MHI = at("merged_hi", [P, KT, TOK], F32R, r0 + 48 * KB)
    MLO = HLO
    ph = r0 + 64 * KB
    QT = at("q_t", [P, TOK], F32, ph)
    KTT = at("k_t", [P, TOK], F32, ph + 2 * KB)
    VT = at("v_t", [P, TOK], F32, ph + 4 * KB)
    OT = at("o_t", [P, TOK], F32, mr0)
    V = at("v", [P, QB, P], F32, ph + 6 * KB)
    WT = at("weights_t", [P, QB, TOK], F32, ph + 8 * KB)
    GB = at("gate_b", [P, KT, TOK], F32, ph)
    CLO = at("conv_lo", [P, KT, TOK], F32R, ph + 16 * KB)
    PR = [[at(f"probs{par}_{m}", [P, (3 + par) * P], F32, ph + 16 * KB + par * 3 * KB + m * (3 + par) * 512)
           for m in range(2)] for par in range(2)]
    z0 = ph + 23 * KB
    Z = at("glu", [P, TOK + 32], F32, z0)
    CAB = [at(f"conv_part{i}", [P, TOK], F32, z0 + 2176 + 2 * KB * i) for i in range(2)]
    CP = at("conv_pool", [P, TOK], F32, z0 + 2176 + 4 * KB)
    ADA0 = at("ada_first", [P, KT, 2 * D], F32, r0)
    XS = at("x_rows", [P, QB, D], F32, r0 + 64 * KB)
    s0 = r0 + 80 * KB
    PV = [at(f"param_rows{l}", [P, P], F32, s0 + 512 * l) for l in range(DEPTH)]
    PV2 = at("param_rows2", [P, P], F32, s0 + 1024)
    OH = at("onehot_sb", [P, TOK + P], F32, s0 + 1536)
    TBR = at("table_rows", [P, BUCKETS], F32, s0 + 4096)
    TB = at("table_t", [P, HEADS], F32, s0 + 4224)
    TBX = at("table_wide", [P, HEADS, P], F32, s0 + 4256)
    LV = at("lambda_rows", [P, DEPTH, 4, HD], F32, s0 + 8352)
    ACC0 = at("ada_acc_first", [P, 2 * D], F32, h0 + 16 * KB)
    BR = [at(f"bias_row{i}", [P, TOK + P], F32, h0 + 8 * KB + 2560 * i) for i in range(2)]
    CWR = at("tap_rows", [P, DEPTH, D], F32, h0)
    YO = at("y_rows", [P, QB, D], F32, r0)

    bank = [ctx.enter_context(nc.psum_tensor(f"bank{i}", [P, TOK], F32)) for i in range(8)]
    G = bank[0:2]
    S = bank[2:4]
    TP = bank[4:6]
    O = bank[6]
    AUX = bank[7]

    def flat(t):
        return t[:, :, :].rearrange("p k t -> p (k t)")

    def tile(view, j, width=TOK):
        return view[:, ds(j * width, width)]

    X2, C2, GA2, GB2 = flat(X), flat(C), flat(GA), flat(GB)
    SHI2, SLO2, MHI2, MLO2 = flat(SHI), flat(SLO), flat(MHI), flat(MLO)
    AOHI2, AOLO2, CW2 = flat(AOHI), flat(AOLO), flat(CW)

    BD = nc.dram_tensor("bias_rows", [HEADS + 1, P * (TOK + P)], F32, kind="Internal")

    w_in = [a["ffn1_w_in"].rearrange("l (k p) f -> p (l k) f", p=P), a["ffn2_w_in"].rearrange("l (k p) f -> p (l k) f", p=P)]
    w_out = [a["ffn1_w_out"].rearrange("l (k p) f -> p (l k) f", p=P), a["ffn2_w_out"].rearrange("l (k p) f -> p (l k) f", p=P)]
    w_mix = a["w_mix_in"].rearrange("l (k p) f -> p (l k) f", p=P)
    w_ab = a["w_attn_branch"].rearrange("l (k p) f -> p (l k) f", p=P)
    w_cb = a["w_conv_branch"].rearrange("l (k p) f -> p (l k) f", p=P)
    w_mo = a["w_mix_out"].rearrange("l (k p) f -> p (l k) f", p=P)
    w_ada = a["ada_w"].rearrange("l (k p) f -> p (l k) f", p=P)

    block = ctx.enter_context(nc.Block())
    w_raw = [sem(f"w_raw_in{s}") for s in range(2)]
    w_hi = [sem(f"w_hi_done{s}") for s in range(2)]
    w_lo = [sem(f"w_lo_done{s}") for s in range(2)]
    w_used = [sem(f"w_used{s}") for s in range(2)]
    acc_read = [sem(f"acc_read{b}") for b in range(2)]

    @block.sync
    def _(sp):
        def slab(pair, slot, src, n=8):
            sp.wait_ge(w_lo[slot], pair)
            sp.dma_start(raw[slot][:, 0:n, :], src).then_inc(w_raw[slot], 16)

        def cols(w, k0, n, c0):
            return w[:, ds(k0, n), ds(c0, P)]

        for l in range(DEPTH):
            rows = [("ffn1_norm", KT), ("mix_norm", KT), ("ffn2_norm", KT), ("conv_dw_bias", KT),
                    ("conv_ln_gain", KT), ("conv_ln_bias", KT), ("subln_gain", 1), ("ada_b", NMOD * KT)]
            r = 0
            for name, n in rows:
                sp.dma_start(PV[l][r:r + n, :], a[name][l, :].rearrange("(r c) -> r c", c=P)).then_inc(sem("rows_in"), 16)
                r += n
            assert r == PC
        sp.dma_start(PV2[0:KT, :], a["final_norm"].rearrange("(r c) -> r c", c=P)).then_inc(sem("rows_in"), 16)
        sp.dma_start(PV2[KT:2 * KT, :], a["c"][0, :].rearrange("(r c) -> r c", c=P)).then_inc(sem("rows_in"), 16)
        for t in range(QB):
            sp.dma_start(XS[:, t, :], a["x"][0, t * P:(t + 1) * P, :]).then_inc(sem(f"x_in{t}"), 16)
        for k in range(KT):
            sp.dma_start(ADA0[:, k, :], w_ada[:, k, 0:2 * D]).then_inc(sem(f"ada0_in{k}"), 16)

        with sp.Fori(0, DEPTH) as l:
            pair = l * PAIRS
            for w in range(2):
                with sp.Fori(0, FT) as i:
                    p = pair + PAIR0[f"ffn{w + 1}_in"] + i
                    slab(p, 0, cols(w_in[w], l * KT, 8, i * P))
                    slab(p, 1, cols(w_in[w], l * KT, 8, i * P + FF))
                with sp.Fori(0, KT // 2) as i:
                    for m in range(6):
                        p = pair + PAIR0[f"ffn{w + 1}_out"] + i * 3 + m // 2
                        slab(p, m % 2, cols(w_out[w], l * FT + sum(OUTG[:m % 3]), OUTG[m % 3], i * (2 * P) + (m // 3) * P), OUTG[m % 3])
                if w == 1:
                    continue
                with sp.Fori(0, HEADS) as h:
                    for m in range(6):
                        slab(pair + PAIR0["mix"] + h * 3 + m // 2, m % 2, cols(w_mix, l * KT, 8, h * P + m * D))
                for name, wt, c0 in (("gb", w_mix, 6 * D), ("ab", w_ab, 0), ("brb", w_cb, 0), ("mo", w_mo, 0)):
                    with sp.Fori(0, KT // 2) as i:
                        for t in range(2):
                            slab(pair + PAIR0[name] + i, t, cols(wt, l * KT, 8, i * (2 * P) + t * P + c0))
        for s in range(2):
            slab(DEPTH * PAIRS, s, cols(w_mo, 0, 8, 0))

        for t in range(QB):
            sp.wait_ge(sem("y_ready"), KT)
            sp.dma_start(out[0, t * P:(t + 1) * P, :], YO[:, t, :]).then_inc(sem("y_out"), 16)
        sp.wait_ge(sem("y_out"), 16 * QB)
        for s in range(2):
            sp.wait_ge(w_raw[s], 16 * (DEPTH * PAIRS + 1))


    @block.gpsimd
    def _(pool):
        pool.memset(ident[:, :], 0.0).then_inc(sem("ident0"), 1)
        pool.memset(invd[:, :], 1.0 / D).then_inc(sem("consts"), 1)
        pool.memset(eps[:, :], EPS).then_inc(sem("consts"), 1)
        pool.memset(SEL[:, :], 0.0).then_inc(sem("sel0"), 1)
        pool.wait_ge(sem("sel0"), 1)
        pool.memset(SEL[:, ROWS_MAX - 1:ROWS_MAX], 1.0).then_inc(sem("consts"), 1)
        pool.wait_ge(sem("ident0"), 1)
        pool.affine_select(out=ident[:, :], in_=ident[:, :], compare_op=ALU.not_equal, fill=1.0, base=0,
                           pattern=[[-1, P]], channel_multiplier=1).then_inc(sem("consts"), 1)

        def carry_wait():
            pool.tensor_tensor(spare[:, 0:1], eps[:, 0:1], eps[:, 0:1], ALU.add)

        def ada_chunk(layer, m, seq):
            for k in range(KT):
                pool.wait_ge(sem("ada_step"), seq * KT + (k - 1 if k else 0))
                pool.dma_start(ada_raw[k % 2][:, :], w_ada[:, ds(layer * KT + k, 1), ds(m * D, D)].rearrange("p o f -> p (o f)"))\
                    .then_inc(sem(f"ada_in{k % 2}"), 16)

        def pool_taps(l, h):
            q = h + l * HEADS
            pool.wait_ge(sem("z_ready"), q + 1)
            pool.wait_ge(sem("c_ready"), q)
            pool.tensor_copy(tapw[:, :], CW2[:, ds(q * CK + DVE_TAPS, POOL_TAPS)]).then_inc(sem("tapw_ready"), 1)
            pool.wait_ge(sem("tapw_ready"), q + 1)
            carry_wait()
            for n in range(POOL_TAPS):
                t = DVE_TAPS + n
                tmp = tap_tmp[n % 2][:, :]
                dst = CP[:, :] if n == 0 else tmp
                pool.tensor_scalar(dst, Z[:, t:t + TOK], tapw[:, n:n + 1], 0.0, ALU.mult, ALU.add)\
                    .then_inc(sem("ptap_mul"), 1)
                if n == 0:
                    continue
                pool.wait_ge(sem("ptap_mul"), q * POOL_TAPS + (n + 1))
                if n > 1:
                    pool.wait_ge(sem("ptap_add"), q * (POOL_TAPS - 2) + (n - 1))
                pool.tensor_tensor(CP[:, :], CP[:, :], tmp, ALU.add)\
                    .then_inc(sem("cp_ready" if n == POOL_TAPS - 1 else "ptap_add"), 1)

        with pool.Fori(0, DEPTH) as l:
            with pool.Fori(0, CHUNKS_IN[0]) as g:
                ada_chunk(l, g + 2, l * NMOD + g)
            with pool.Fori(0, CHUNKS_OUT) as g:
                ada_chunk(l, g + (2 + CHUNKS_IN[0]), l * NMOD + CHUNK_SEQ["ffn1_out"] + g)
            pool.wait_ge(sem("cw_ready"), 2)
            with pool.Fori(0, HEADS) as h:
                pool_taps(l, h)
            with pool.Fori(0, CHUNKS_IN[1]) as g:
                ada_chunk(1, g, l * NMOD + CHUNK_SEQ["ffn2_in"] + g)
        for i in range(2):
            pool.wait_ge(sem(f"ada_in{i}"), DEPTH * NMOD * (KT // 2) * 16)

    @block.scalar
    def _(act):
        def w_hi_part(pair, slot, n=8):
            act.wait_ge(w_raw[slot], (pair + 1) * 16)
            act.wait_ge(w_used[slot], pair)
            act.activation(whi[slot][:, 0:n, :], raw[slot][:, 0:n, :], ACT.Copy).then_inc(w_hi[slot], 1)

        def root(aux, unit, scale=1.0):
            act.wait_ge(sem("aux_ready"), aux + 1)
            act.wait_ge(sem("unit_t"), unit)
            act.activation(RSTD[:, :], AUX[:, :], ACT.Sqrt, bias=eps[:, 0:1], scale=scale).then_inc(sem("aux_read"), 1)

        def unit_split(u, b, first, hi, func, scale, bias):
            act.wait_ge(sem("unit_t"), u + 1)
            act.wait_ge(sem("unit_lo"), u if first else u - 1)
            act.activation(F[b][:, :], T[b][:, :], func, bias=bias, scale=scale).then_inc(sem("unit_f"), 1)
            act.activation(hi, T[b][:, :], func, bias=bias, scale=scale).then_inc(sem("unit_hi"), 1)

        def norm_units(l, k):
            root(l * AUXN + AUX_NORM[k], l * UNITS + UNIT_NORM[k])
            act.wait_ge(sem("ac_ready"), l * 3 + (k + 1))
            for j in range(KT):
                unit_split(l * UNITS + UNIT_NORM[k] + j, j % 2, j == 0, HHI[:, j, :], ACT.Identity,
                           AC[:, k, j:j + 1], MODC[:, ds(l * (NMOD * KT) + 3 * k * KT + j, 1)])

        def square_x(bank_use, t, n8, j):
            act.wait_ge(acc_read[t], bank_use + 1)
            act.wait_ge(sem("ssum_add"), n8 + j)
            act.activation(SQ[:, :], tile(X2, j), ACT.Square).then_inc(sem("sq_ready"), 1)

        for l in range(DEPTH):
            act.dma_start(CWR[0:CK, l, :], a["conv_dw"][l, :, :]).then_inc(sem("taps_in"), 16)
        act.dma_start(TBR[0:HEADS, :], a["rel_bias"]).then_inc(sem("table_in"), 16)
        act.dma_start(OH[0:BUCKETS + 1, :], onehot).then_inc(sem("table_in"), 16)
        for l in range(DEPTH):
            for n, name in enumerate(("lambda_q1", "lambda_k1", "lambda_q2", "lambda_k2")):
                act.dma_start(LV[:, l, n, :], bass.AP(a[name].tensor, l * HD, [[0, P], [1, HD]]))\
                    .then_inc(sem("lambda_in"), 16)
        act.wait_ge(sem("pt_ready"), 3)
        act.activation(CA[:, :], PT2[:, KT:2 * KT], ACT.Silu).then_inc(sem("ca_ready"), 1)
        act.wait_ge(sem("tapsp_ready"), DEPTH)
        for l in range(DEPTH):
            act.activation(CW2[:, l * HEADS * CK:(l + 1) * HEADS * CK], G[l][:, 0:HEADS * CK], ACT.Copy)\
                .then_inc(sem("cw_ready"), 1)
        for s in range(2):
            w_hi_part(0, s)
        act.wait_ge(sem("consts"), 4)
        for j in range(KT):
            act.wait_ge(sem("x_ready"), j + 1)
            act.wait_ge(sem("ssum_add"), j)
            act.activation(SQ[:, :], X[:, j, :], ACT.Square).then_inc(sem("sq_ready"), 1)
        act.wait_ge(sem("lam_dots"), 2 * DEPTH)
        act.activation(lam_exp[:, :], lam_dot[:, :], ACT.Exp).then_inc(sem("lam_exps"), 1)
        for h in range(HEADS):
            act.wait_ge(sem("br_ready"), h + 1)
            if h >= 2:
                act.wait_ge(sem(f"br_out{h % 2}"), 16 * (h // 2))
            if h == 2:
                act.wait_ge(sem("br_again"), 16)
            act.activation(BR[h % 2][:, 0:TOK], O[:, :], ACT.Copy).then_inc(sem("br_part"), 1)
            act.activation(BR[h % 2][:, TOK:TOK + P], AUX[:, 0:P], ACT.Copy).then_inc(sem("br_copied"), 1)
            act.wait_ge(sem("br_copied"), h + 1)
            act.wait_ge(sem("br_part"), h + 1)
            act.dma_start(BD[h, :].rearrange("(p x) -> p x", p=P), BR[h % 2][:, :]).then_inc(sem(f"br_out{h % 2}"), 16)
            if h == 0:
                act.dma_start(BD[HEADS, :].rearrange("(p x) -> p x", p=P), BR[0][:, :]).then_inc(sem("br_again"), 16)
        for i in range(2):
            act.wait_ge(sem(f"br_out{i}"), 16 * (HEADS // 2))

        def load_bias_tile(h):
            src = BD[ds(h, 1), :]
            src = bass.AP(src.tensor, src.offset + (P - 1), [[TOK + P - 1, P], [1, TOK]])
            act.dma_start(BT[:, :], src).then_inc(sem("bt_in"), 16)

        load_bias_tile(0)

        with act.Fori(0, DEPTH) as l:
            for w in range(2):
                n_in, n_out = f"ffn{w + 1}_in", f"ffn{w + 1}_out"
                norm_units(l, 2 * w)
                with act.Fori(0, FT) as i:
                    p = l * PAIRS + PAIR0[n_in] + i
                    u = l * USES + USE0[n_in] + i
                    w_hi_part(p + 1, 0)
                    act.wait_ge(acc_read[0], u)
                    act.activation(T[0][:, :], G[0][:, :], ACT.Tanh, scale=0.5).then_inc(sem("g_tanh"), 1)
                    w_hi_part(p + 1, 1)
                    act.wait_ge(acc_read[1], u + 1)
                    act.activation(tile(SHI2, i), F[0][:, :], ACT.Copy).then_inc(sem("s_hi"), 1)
                with act.Fori(0, KT // 2) as i:
                    for m in range(6):
                        w_hi_part(l * PAIRS + PAIR0[n_out] + i * 3 + m // 2 + 1, m % 2,
                                  OUTG[(m + 2) % 3] if m < 4 else 8)
                        if m % 3 == 2:
                            square_x(l * USES + USE0[n_out] + i, m // 3, (l * 3 + 1 + 2 * w) * KT, i * 2 + m // 3)
                if w == 1:
                    continue

                norm_units(l, 1)

                def weights(i, hh):
                    act.wait_ge(sem("t_ready"), hh * 4 + (QB - i))
                    act.activation(WT[:, 0:i + 1, i * P:(i + 1) * P],
                                   TP[i % 2][:, 0:(i + 1) * P].rearrange("p (j t) -> p j t", t=P),
                                   ACT.Copy).then_inc(sem("wt_ready"), 1)

                def head_output(hh):
                    act.wait_ge(sem("o_ready"), hh + 1)
                    act.activation(OT[:, :], O[:, :], ACT.Copy).then_inc(sem("o_copied"), 1)
                    act.activation(SQ[:, :], O[:, :], ACT.Square).then_inc(sem("o_read"), 1)

                def mix(h, first):
                    hh = l * HEADS + h
                    p = l * PAIRS + PAIR0["mix"] + h * 3
                    b = l * USES + USE0["mix"] + h * 3

                    def exps(i):
                        par, si, n = i % 2, hh * 4 + (QB - 1 - i), (i + 1) * P
                        act.wait_ge(sem("nmax_ready"), si + 1)
                        for m in range(2):
                            act.activation(PR[par][m][:, 0:n], PR[par][m][:, 0:n], ACT.Exp, bias=nmx[:, par, m:m + 1],
                                           accum_out=rsum[:, par, m:m + 1]).then_inc(sem("exp_done"), 1)

                    if not first:
                        weights(1, hh - 1)
                    w_hi_part(p + 1, 0)
                    act.activation(QT[:, :], G[0][:, :], ACT.Copy, scale=HD ** -0.5).then_inc(acc_read[0], 1)
                    if not first:
                        weights(0, hh - 1)
                        head_output(hh - 1)
                    w_hi_part(p + 1, 1)
                    act.activation(KTT[:, :], G[1][:, :], ACT.Copy).then_inc(acc_read[1], 1)
                    if not first:
                        root(l * AUXN + AUX_HEAD + h - 1, l * UNITS + UNIT_HEAD + h - 1, float(D // P))
                    w_hi_part(p + 2, 0)
                    act.activation(VT[:, :], G[0][:, :], ACT.Copy).then_inc(acc_read[0], 1)
                    if not first:
                        unit_split(l * UNITS + UNIT_HEAD + h - 1, 0, True, tile(AOHI2, h - 1), ACT.Identity,
                                   subg[:, ds(l, 1)], 0.0)
                    exps(3)
                    w_hi_part(p + 2, 1)
                    act.wait_ge(sem("z_ready"), hh)
                    act.activation(T[1][:, :], G[1][:, :], ACT.Copy, scale=0.5).then_inc(acc_read[1], 1)
                    act.wait_ge(sem("vtp_ready"), hh + 1)
                    act.activation(V[:, :, :].rearrange("p j e -> p (j e)"), TP[0][:, :], ACT.Copy).then_inc(sem("v_ready"), 1)
                    exps(2)
                    exps(1)
                    weights(3, hh)
                    w_hi_part(p + 3, 0)
                    act.activation(F[1][:, :], G[0][:, :], ACT.Tanh, scale=0.5).then_inc(acc_read[0], 1)
                    exps(0)
                    load_bias_tile(h + 1)
                    weights(2, hh)
                    w_hi_part(p + 3, 1)
                    act.activation(tile(GA2, h), G[1][:, :], ACT.Tanh, scale=0.5).then_inc(acc_read[1], 1)

                mix(0, True)
                with act.Fori(1, HEADS) as h:
                    mix(h, False)

                for j in range(KT):
                    p = l * PAIRS + PAIR0["gb"] + j
                    if j == 0:
                        weights(1, l * HEADS + HEADS - 1)
                    w_hi_part(p + 1, 0)
                    if j < KT // 2:
                        act.activation(GB[:, 2 * j, :], G[0][:, :], ACT.Tanh, scale=0.5).then_inc(acc_read[0], 1)
                    if j == 0:
                        weights(0, l * HEADS + HEADS - 1)
                        head_output(l * HEADS + HEADS - 1)
                        root(l * AUXN + AUX_HEAD + HEADS - 1, l * UNITS + UNIT_HEAD + HEADS - 1, float(D // P))
                    w_hi_part(p + 1, 1)
                    if j < KT // 2:
                        act.activation(GB[:, 2 * j + 1, :], G[1][:, :], ACT.Tanh, scale=0.5).then_inc(acc_read[1], 1)
                    if j == 0:
                        unit_split(l * UNITS + UNIT_HEAD + HEADS - 1, 0, True, AOHI[:, HEADS - 1, :], ACT.Identity,
                                   subg[:, ds(l, 1)], 0.0)
                    if j == LN_MEAN:
                        act.wait_ge(sem("aux_ready"), l * AUXN + AUX_MEAN + 1)
                        act.activation(F[1][:, :], AUX[:, :], ACT.Copy).then_inc(sem("aux_read"), 1)
                    if j in (LN_MEAN, LN_MEAN + 1):
                        for n in range(4 * (j - LN_MEAN), 4 * (j - LN_MEAN) + 4):
                            act.wait_ge(sem("xc_ready"), l * KT + n + 1)
                            act.wait_ge(sem("lnadd"), l * KT + n)
                            act.activation(SQ[:, :], C[:, n, :], ACT.Square).then_inc(sem("lnsq"), 1)
                    if j == LN_VAR:
                        root(l * AUXN + AUX_VAR, l * UNITS + UNIT_LN)
                    for n in LN_UNITS.get(j, ()):
                        unit_split(l * UNITS + UNIT_LN + n, n % 2, n == 0, CHI[:, n, :], ACT.Silu,
                                   PT[:, ds(l * PC + PC_LNG + n, 1)], PT[:, ds(l * PC + PC_LNB + n, 1)])
                with act.Fori(0, KT // 2) as i:
                    for t in range(2):
                        w_hi_part(l * PAIRS + PAIR0["brb"] + i + 1, t)
                        act.wait_ge(sem("merged"), l * KT + i * 2 + (t + 1))
                        act.activation(tile(MHI2, i * 2 + t), F[t][:, :], ACT.Copy).then_inc(sem("m_hi"), 1)
                with act.Fori(0, KT // 2) as i:
                    for t in range(2):
                        w_hi_part(l * PAIRS + PAIR0["mo"] + i + 1, t)
                        square_x(l * USES + USE0["mo"] + i, t, (l * 3 + 2) * KT, i * 2 + t)

        root(DEPTH * AUXN, DEPTH * UNITS)
        for j in range(KT):
            act.wait_ge(sem("unit_t"), DEPTH * UNITS + j + 1)
            if j >= 2:
                act.wait_ge(sem("yt_ready"), j - 1)
            act.activation(F[j % 2][:, :], T[j % 2][:, :], ACT.Identity, scale=PT2[:, j:j + 1]).then_inc(sem("fin"), 1)
        act.wait_ge(sem("bt_in"), 16 * (DEPTH * HEADS + 1))

    @block.vector
    def _(dve):
        def w_lo_part(pair, slot, n=8):
            dve.wait_ge(w_hi[slot], pair + 1)
            dve.tensor_tensor(wlo[slot][:, 0:n, :], raw[slot][:, 0:n, :], whi[slot][:, 0:n, :].bitcast(F32),
                              ALU.subtract).then_inc(w_lo[slot], 1)

        def clear_sum():
            dve.memset(SSUM[:, :], 0.0).then_inc(sem("ssum_clear"), 1)

        def sum_cleared(count):
            dve.wait_ge(sem("ssum_clear"), count)

        def reciprocal(aux, r):
            dve.wait_ge(sem("aux_read"), aux + 1)
            dve.reciprocal(RSTD[:, :], RSTD[:, :]).then_inc(sem("rstd_ready"), 1)
            dve.wait_ge(sem("rstd_ready"), r + 1)

        def unit_scale(u, b, first, src):
            dve.wait_ge(sem("unit_hi"), u if first else u - 1)
            dve.tensor_tensor(T[b][:, :], src, RSTD[:, :], ALU.mult).then_inc(sem("unit_t"), 1)

        def unit_rest(u, b, lo, hi):
            dve.wait_ge(sem("unit_hi"), u + 1)
            dve.tensor_tensor(lo, F[b][:, :], hi.bitcast(F32), ALU.subtract).then_inc(sem("unit_lo"), 1)

        def norm_units(l, k):
            reciprocal(l * AUXN + AUX_NORM[k], l * RSN + RS_NORM[k])
            u = l * UNITS + UNIT_NORM[k]
            for j in range(KT + 1):
                if j < KT:
                    unit_scale(u + j, j % 2, j == 0, X[:, j, :])
                if j:
                    unit_rest(u + (j - 1), (j - 1) % 2, HLO[:, j - 1, :], HHI[:, j - 1, :])

        def update_x(pair, slot, bank_use, t, k, j):
            dve.wait_ge(w_used[slot], pair + 1)
            dve.scalar_tensor_tensor(out=tile(X2, j), in0=G[t][:, :], scalar=GC[:, k, ds(j, 1)], in1=tile(X2, j),
                                     op0=ALU.mult, op1=ALU.add).then_inc(acc_read[t], 1)

        def add_square(n8, j):
            dve.wait_ge(sem("sq_ready"), n8 + j + 1)
            dve.wait_ge(sem("ssum_add"), n8 + j)
            dve.tensor_tensor(SSUM[:, :], SSUM[:, :], SQ[:, :], ALU.add).then_inc(sem("ssum_add"), 1)

        def ada_step(seq, k):
            n = seq * KT + k
            dve.wait_ge(sem(f"ada_in{k % 2}"), (seq * (KT // 2) + (k // 2 + 1)) * 16)
            if k == 0:
                dve.wait_ge(sem("mod_summed"), seq + 1)
                ins = dve.tensor_scalar(ACC[:, :], ada_raw[0][:, :], CA[:, 0:1], None, ALU.mult)
            else:
                dve.wait_ge(sem("ada_step"), n)
                ins = dve.scalar_tensor_tensor(out=ACC[:, :], in0=ada_raw[k % 2][:, :], scalar=CA[:, k:k + 1],
                                               in1=ACC[:, :], op0=ALU.mult, op1=ALU.add)
            ins.then_inc(sem("ada_step"), 1)

        def mod_rows(turn):
            dve.wait_ge(sem("mod_summed"), turn + 1)
            dve.wait_ge(sem("mod_turned"), turn)
            dve.tensor_copy(MR[0:64, :], O[0:64, :]).then_inc(sem("mod_copied"), 1)

        def mod_columns(layer, hc, rows, turn):
            dve.wait_ge(sem("mod_turned"), turn + 1)
            dve.tensor_tensor(MODC[:, ds(layer * (NMOD * KT) + hc * 4, rows * 4)], O[:, 0:rows * 4],
                              PT[:, ds(layer * PC + PC_ADA + hc * 4, rows * 4)], ALU.add).then_inc(sem("modc_ready"), 1)

        def scale_columns(l, k):
            return dve.scalar_tensor_tensor(out=AC[:, k, :], in0=MODC[:, ds(l * (NMOD * KT) + (3 * k + 1) * KT, KT)],
                                            scalar=1.0, in1=PT[:, ds(l * PC + PC_NORM[k], KT)], op0=ALU.add, op1=ALU.mult)

        def gate_columns(l, k):
            return dve.tensor_scalar(GC[:, k, :], MODC[:, ds(l * (NMOD * KT) + (3 * k + 2) * KT, KT)],
                                     0.5 if k == 1 else 0.25, None, ALU.mult)

        dve.memset(TB[BUCKETS:BUCKETS + 1, :], NEG).then_inc(sem("tb_rows"), 1)
        clear_sum()
        sum_cleared(1)
        for n, (dst, src) in enumerate(((PT[:, 0:PC], TP[0][:, 0:PC]), (PT[:, PC:2 * PC], TP[1][:, 0:PC]),
                                        (PT2[:, :], O[:, 0:2 * KT]))):
            dve.wait_ge(sem("ptp_ready"), n + 1)
            dve.tensor_copy(dst, src).then_inc(sem("pt_ready"), 1)
        for j in range(KT + 1):
            if j < KT:
                dve.wait_ge(sem("xp_ready"), j + 1)
                dve.tensor_copy(X[:, j, :], bank[2 + j % 2][:, :]).then_inc(sem("x_ready"), 1)
            if j:
                add_square(0, j - 1)
        dve.wait_ge(sem("tbp_ready"), 1)
        dve.tensor_copy(TB[0:BUCKETS, :], TP[0][0:BUCKETS, 0:HEADS]).then_inc(sem("tb_rows"), 1)
        dve.wait_ge(sem("tb_rows"), 2)
        dve.tensor_copy(TBX[0:BUCKETS + 1, :, :], TB[0:BUCKETS + 1, :].unsqueeze(2).to_broadcast([BUCKETS + 1, HEADS, P]))\
            .then_inc(sem("tbx_ready"), 1)
        dve.wait_ge(sem("lambda_in"), 16 * 4 * DEPTH)
        for l in range(DEPTH):
            for n in range(2):
                dve.tensor_tensor_reduce(LV[:, l, 2 * n, :], LV[:, l, 2 * n, :], LV[:, l, 2 * n + 1, :], 1.0, 0.0,
                                         ALU.mult, ALU.add, lam_dot[:, 2 * l + n:2 * l + n + 1]).then_inc(sem("lam_dots"), 1)
        dve.wait_ge(sem("ca_ready"), 1)
        acc = ACC0[:, :]
        for k in range(KT):
            dve.wait_ge(sem(f"ada0_in{k}"), 16)
            if k == 0:
                dve.tensor_scalar(acc, ADA0[:, 0, :], CA[:, 0:1], None, ALU.mult).then_inc(sem("ada0_step"), 1)
                continue
            dve.wait_ge(sem("ada0_step"), k)
            dve.scalar_tensor_tensor(out=acc, in0=ADA0[:, k, :], scalar=CA[:, k:k + 1], in1=acc,
                                     op0=ALU.mult, op1=ALU.add).then_inc(sem("ada0_step"), 1)
        mod_rows(0)
        mod_columns(0, 0, 4, 0)
        for s in range(2):
            w_lo_part(0, s)
        dve.wait_ge(sem("lam_exps"), 1)
        for l in range(DEPTH):
            lam_init = 0.8 - 0.6 * math.exp(-0.3 * l)
            dve.scalar_tensor_tensor(out=nlam[:, l:l + 1], in0=lam_exp[:, 2 * l + 1:2 * l + 2], scalar=lam_init,
                                     in1=lam_exp[:, 2 * l:2 * l + 1], op0=ALU.subtract, op1=ALU.subtract)\
                .then_inc(sem("lam_ready"), 1)
            dve.tensor_scalar(subg[:, l:l + 1], PT[:, l * PC + PC_SUB:l * PC + PC_SUB + 1], 1.0 - lam_init, None,
                              ALU.mult).then_inc(sem("lam_ready"), 1)
        dve.wait_ge(sem("lam_ready"), 2 * DEPTH)

        with dve.Fori(0, DEPTH) as l:
            for w in range(2):
                n_in, n_out = f"ffn{w + 1}_in", f"ffn{w + 1}_out"
                if w == 0:
                    dve.wait_ge(sem("modc_ready"), l * NMOD + 1)
                    scale_columns(l, 0).then_inc(sem("ac_ready"), 1)
                norm_units(l, 2 * w)

                def ffn_tile(i, seq=0, steps=()):
                    p = l * PAIRS + PAIR0[n_in] + i
                    u = l * USES + USE0[n_in] + i
                    w_lo_part(p + 1, 0)
                    dve.wait_ge(sem("g_tanh"), (l * 2 + w) * FT + i + 1)
                    dve.wait_ge(acc_read[1], u)
                    dve.scalar_tensor_tensor(out=T[1][:, :], in0=T[0][:, :], scalar=1.0, in1=G[0][:, :],
                                             op0=ALU.add, op1=ALU.mult).then_inc(acc_read[0], 1)
                    for k in steps[:1]:
                        ada_step(seq, k)
                    w_lo_part(p + 1, 1)
                    dve.wait_ge(acc_read[0], u + 1)
                    dve.wait_ge(w_used[1], p + 1)
                    dve.wait_ge(sem("s_lo"), (l * 2 + w) * FT + i)
                    dve.tensor_tensor(F[0][:, :], G[1][:, :], T[1][:, :], ALU.mult).then_inc(acc_read[1], 1)
                    dve.wait_ge(sem("s_hi"), (l * 2 + w) * FT + i + 1)
                    dve.tensor_tensor(tile(SLO2, i), F[0][:, :], tile(SHI2, i).bitcast(F32), ALU.subtract)\
                        .then_inc(sem("s_lo"), 1)
                    for k in steps[1:]:
                        ada_step(seq, k)

                ffn_tile(0)
                with dve.Fori(0, CHUNKS_IN[w]) as g:
                    seq = l * NMOD + CHUNK_SEQ[n_in] + g
                    for r in range(GROUP):
                        if r == 5:
                            mod_rows(seq + 1)
                        ffn_tile(g * GROUP + (r + 1), seq, GROUP_STEPS[r])
                        if r == 5:
                            mod_columns(1 if w else l, g * 2 + (0 if w else 4), 2, seq + 1)
                if w:
                    with dve.Fori(1 + CHUNKS_IN[w] * GROUP, FT) as i:
                        ffn_tile(i)
                if w == 0:
                    dve.wait_ge(sem("modc_ready"), l * NMOD + CHUNKS_IN[0] + 1)
                    scale_columns(l, 1)
                    gate_columns(l, 0).then_inc(sem("ac_ready"), 1)
                    dve.wait_ge(sem("ac_ready"), l * 3 + 2)

                clear_sum()
                with dve.Fori(0, KT // 2) as i:
                    for m in range(6):
                        p = l * PAIRS + PAIR0[n_out] + i * 3 + m // 2
                        if w == 0:
                            seq = l * NMOD + CHUNK_SEQ[n_out] + i
                            for k in OUT_STEPS[m][:1]:
                                ada_step(seq, k)
                        w_lo_part(p + 1, m % 2, OUTG[(m + 2) % 3] if m < 4 else 8)
                        if w == 0:
                            for k in OUT_STEPS[m][1:]:
                                ada_step(seq, k)
                            if m == 5:
                                mod_rows(seq + 1)
                        if m % 3 == 2:
                            t = m // 3
                            update_x(p, m % 2, l * USES + USE0[n_out] + i, t, 2 * w, i * 2 + t)
                            sum_cleared(l * ZEROS + 1 + (ZERO_FFN2 if w else ZERO_FFN1))
                            add_square((l * 3 + 1 + 2 * w) * KT, i * 2 + t)
                    if w == 0:
                        mod_columns(l, i * 2 + (4 + 2 * CHUNKS_IN[0]), 2, seq + 1)
                if w == 1:
                    continue
                dve.wait_ge(sem("modc_ready"), l * NMOD + CHUNKS_IN[0] + CHUNKS_OUT + 1)
                scale_columns(l, 2)
                for k in (1, 2):
                    g = gate_columns(l, k)
                g.then_inc(sem("ac_ready"), 1)

                norm_units(l, 1)
                clear_sum()
                dve.memset(Z[:, 0:PADL], 0.0).then_inc(sem("z_pad"), 1)
                dve.wait_ge(sem("z_pad"), l + 1)

                def taps(h, lo, hi):
                    q = l * HEADS + h
                    for t in range(lo, hi):
                        wt = CW2[:, ds(q * CK + t, 1)]
                        if t == 0:
                            dve.wait_ge(sem("z_ready"), q + 1)
                            ins = dve.tensor_scalar(CAB[0][:, :], Z[:, 0:TOK], wt, PT[:, ds(l * PC + PC_DWB + h, 1)],
                                                    ALU.mult, ALU.add)
                        elif t == 1:
                            ins = dve.tensor_scalar(CAB[1][:, :], Z[:, 1:1 + TOK], wt, None, ALU.mult)
                        else:
                            dve.wait_ge(sem("tap_done"), q * DVE_TAPS + (t - 1))
                            ins = dve.scalar_tensor_tensor(out=CAB[t % 2][:, :], in0=Z[:, t:t + TOK], scalar=wt,
                                                           in1=CAB[t % 2][:, :], op0=ALU.mult, op1=ALU.add)
                        ins.then_inc(sem("tap_done"), 1)

                def join(h):
                    q = l * HEADS + h
                    c = tile(C2, h)
                    dve.wait_ge(sem("tap_done"), q * DVE_TAPS + DVE_TAPS)
                    dve.tensor_tensor(c, CAB[0][:, :], CAB[1][:, :], ALU.add).then_inc(sem("c_part"), 1)
                    dve.wait_ge(sem("c_part"), q + 1)
                    dve.wait_ge(sem("cp_ready"), q + 1)
                    dve.tensor_tensor(c, c, CP[:, :], ALU.add).then_inc(sem("c_ready"), 1)
                    dve.wait_ge(sem("c_ready"), q + 1)
                    dve.wait_ge(sem("csum"), q)
                    sum_cleared(l * ZEROS + 1 + ZERO_CONV)
                    dve.tensor_tensor(SSUM[:, :], SSUM[:, :], c, ALU.add).then_inc(sem("csum"), 1)

                def mix(h, first):
                    hh = l * HEADS + h
                    p = l * PAIRS + PAIR0["mix"] + h * 3
                    b = l * USES + USE0["mix"] + h * 3
                    uh = l * UNITS + UNIT_HEAD + h - 1

                    def conv(lo, hi):
                        if not first:
                            taps(h - 1, lo, hi)

                    def scores(i):
                        par, r, n = i % 2, QB - 1 - i, (i + 1) * P
                        si = hh * 4 + r
                        dve.wait_ge(sem("s_ready"), si + 1)
                        dve.wait_ge(sem("t_ready"), si - 1 if r >= 2 else hh * 4)
                        dve.memset(spare[:, 1:2], 0.0)
                        for m in range(2):
                            dve.tensor_tensor_reduce(PR[par][m][:, 0:n], S[m][:, 0:n], BT[:, TOK - n:TOK], 1.0, NEG,
                                                     ALU.add, ALU.max, mx[:, par, m:m + 1]).then_inc(sem("max_done"), 1)
                        dve.wait_ge(sem("max_done"), (si + 1) * 2)
                        dve.tensor_scalar(nmx[:, par, :], mx[:, par, :], -1.0, None, ALU.mult).then_inc(sem("nmax_ready"), 1)

                    def combine(i):
                        par, n = i % 2, (i + 1) * P
                        si = hh * 4 + (QB - 1 - i)
                        p0, p1 = PR[par][0][:, 0:n], PR[par][1][:, 0:n]
                        dve.wait_ge(sem("exp_done"), (si + 1) * 2)
                        dve.reciprocal(rinv[:, par, :], rsum[:, par, :]).then_inc(sem("comb"), 1)
                        dve.wait_ge(sem("comb"), si * 3 + 1)
                        dve.tensor_scalar(rlam[:, par:par + 1], rinv[:, par, 1:2], nlam[:, ds(l, 1)], None, ALU.mult)\
                            .then_inc(sem("comb"), 1)
                        dve.wait_ge(sem("comb"), si * 3 + 2)
                        dve.tensor_scalar(p1, p1, rlam[:, par:par + 1], None, ALU.mult).then_inc(sem("comb"), 1)
                        dve.wait_ge(sem("comb"), si * 3 + 3)
                        dve.scalar_tensor_tensor(out=p0, in0=p0, scalar=rinv[:, par, 0:1], in1=p1,
                                                 op0=ALU.mult, op1=ALU.add).then_inc(sem("w_ready"), 1)

                    conv(0, 5)
                    w_lo_part(p + 1, 0)
                    conv(5, 10)
                    w_lo_part(p + 1, 1)
                    conv(10, 11)
                    if not first:
                        reciprocal(l * AUXN + AUX_HEAD + h - 1, l * RSN + RS_HEAD + h - 1)
                        unit_scale(uh, 0, True, OT[:, :])
                    w_lo_part(p + 2, 0)
                    if not first:
                        unit_rest(uh, 0, tile(AOLO2, h - 1), tile(AOHI2, h - 1))
                    dve.wait_ge(sem("bt_in"), (hh + 1) * 16)
                    scores(3)
                    conv(11, 12)
                    w_lo_part(p + 2, 1)
                    scores(2)
                    combine(3)
                    conv(12, 14)
                    scores(1)
                    combine(2)
                    conv(14, 18)
                    w_lo_part(p + 3, 0)
                    scores(0)
                    combine(1)
                    conv(18, 22)
                    combine(0)
                    conv(22, 23)
                    if not first:
                        join(h - 1)
                    w_lo_part(p + 3, 1)
                    dve.wait_ge(acc_read[0], b + 3)
                    dve.wait_ge(acc_read[1], b + 2)
                    dve.scalar_tensor_tensor(out=Z[:, PADL:PADL + TOK], in0=F[1][:, :], scalar=1.0, in1=T[1][:, :],
                                             op0=ALU.add, op1=ALU.mult).then_inc(sem("z_ready"), 1)

                mix(0, True)
                with dve.Fori(1, HEADS) as h:
                    mix(h, False)

                dve.wait_ge(acc_read[1], l * USES + USE0["gb"])
                for j in range(KT):
                    p = l * PAIRS + PAIR0["gb"] + j
                    for t in range(2):
                        w_lo_part(p + 1, t)
                        if j >= KT // 2:
                            n = 2 * (j - KT // 2) + t
                            dve.scalar_tensor_tensor(out=GA[:, n, :], in0=GA[:, n, :], scalar=1.0, in1=G[t][:, :],
                                                     op0=ALU.add, op1=ALU.mult).then_inc(acc_read[t], 1)
                        if j == 0 and t == 0:
                            taps(HEADS - 1, 0, 4)
                    if j == 0:
                        uh = l * UNITS + UNIT_HEAD + HEADS - 1
                        reciprocal(l * AUXN + AUX_HEAD + HEADS - 1, l * RSN + RS_HEAD + HEADS - 1)
                        unit_scale(uh, 0, True, OT[:, :])
                        taps(HEADS - 1, 4, 6)
                        unit_rest(uh, 0, AOLO[:, HEADS - 1, :], AOHI[:, HEADS - 1, :])
                    if j == 1:
                        taps(HEADS - 1, 6, 16)
                    if j == 2:
                        taps(HEADS - 1, 16, DVE_TAPS)
                        join(HEADS - 1)
                    if j == LN_MEAN:
                        dve.wait_ge(sem("aux_read"), l * AUXN + AUX_MEAN + 1)
                        clear_sum()
                        sum_cleared(l * ZEROS + 1 + ZERO_LN)
                    if j in (LN_MEAN, LN_MEAN + 1):
                        n0 = 4 * (j - LN_MEAN)
                        for n in range(n0, n0 + 5):
                            if n < n0 + 4:
                                dve.tensor_tensor(C[:, n, :], C[:, n, :], F[1][:, :], ALU.subtract).then_inc(sem("xc_ready"), 1)
                            if n > n0:
                                dve.wait_ge(sem("lnsq"), l * KT + n)
                                dve.wait_ge(sem("lnadd"), l * KT + n - 1)
                                dve.tensor_tensor(SSUM[:, :], SSUM[:, :], SQ[:, :], ALU.add).then_inc(sem("lnadd"), 1)
                    if j == LN_VAR:
                        reciprocal(l * AUXN + AUX_VAR, l * RSN + RS_VAR)
                    units = LN_UNITS.get(j, ())
                    for n in (*units, None):
                        ul = l * UNITS + UNIT_LN
                        if n is not None:
                            unit_scale(ul + n, n % 2, n == 0, C[:, n, :])
                        if units and n != units[0]:
                            o = units[-1] if n is None else n - 1
                            unit_rest(ul + o, o % 2, CLO[:, o, :], CHI[:, o, :])
                with dve.Fori(0, KT // 2) as i:
                    for t in range(2):
                        j = i * 2 + t
                        w_lo_part(l * PAIRS + PAIR0["brb"] + i + 1, t)
                        if t == 0:
                            dve.wait_ge(acc_read[1], l * USES + USE0["brb"] + i)
                        dve.scalar_tensor_tensor(out=T[t][:, :], in0=tile(GB2, j), scalar=1.0, in1=G[t][:, :],
                                                 op0=ALU.add, op1=ALU.mult).then_inc(acc_read[t], 1)
                        dve.wait_ge(acc_read[t], l * USES + USE0["brb"] + i + 1)
                        dve.wait_ge(sem("m_lo"), l * KT + j)
                        dve.tensor_tensor(F[t][:, :], tile(GA2, j), T[t][:, :], ALU.add).then_inc(sem("merged"), 1)
                        dve.wait_ge(sem("m_hi"), l * KT + j + 1)
                        dve.tensor_tensor(tile(MLO2, j), F[t][:, :], tile(MHI2, j).bitcast(F32), ALU.subtract)\
                            .then_inc(sem("m_lo"), 1)
                clear_sum()
                with dve.Fori(0, KT // 2) as i:
                    for t in range(2):
                        p = l * PAIRS + PAIR0["mo"] + i
                        w_lo_part(p + 1, t)
                        update_x(p, t, l * USES + USE0["mo"] + i, t, 1, i * 2 + t)
                        sum_cleared(l * ZEROS + 1 + ZERO_MO)
                        add_square((l * 3 + 2) * KT, i * 2 + t)

        reciprocal(DEPTH * AUXN, DEPTH * RSN)
        for j in range(KT + 2):
            if j < KT:
                if j == 0:
                    dve.wait_ge(sem("unit_hi"), DEPTH * UNITS)
                if j >= 2:
                    dve.wait_ge(sem("fin"), j - 1)
                dve.tensor_tensor(T[j % 2][:, :], X[:, j, :], RSTD[:, :], ALU.mult).then_inc(sem("unit_t"), 1)
            if j >= 2:
                n = j - 2
                dve.wait_ge(sem("yt_ready"), n + 1)
                dve.tensor_copy(YO[:, :, n * P:(n + 1) * P], TP[n % 2][:, :].rearrange("p (t c) -> p t c", c=P))\
                    .then_inc(sem("y_ready"), 1)

    @block.tensor
    def _(pe):
        def slab(pair, slot, acc, hi, lo, k0=0, n=8, first=True, last=True, ready=None, at_half=None):
            pe.wait_ge(w_hi[slot], pair + 1)
            pe.wait_ge(w_lo[slot], pair + 1)
            for k in range(n):
                if ready:
                    ready(k0 + k)
                if at_half and k == n // 2:
                    at_half()
                wh, wl = whi[slot][:, k, :], wlo[slot][:, k, :]
                pe.matmul(acc, wh, hi[:, k0 + k, :], start=first and k == 0, stop=False)
                pe.matmul(acc, wh, lo[:, k0 + k, :], start=False, stop=False)
                mm = pe.matmul(acc, wl, hi[:, k0 + k, :], start=False, stop=last and k == n - 1)
            mm.then_inc(w_used[slot], 1)

        def two_slabs(pair, hi, lo, ready):
            lag = 4
            for k in range(KT + lag):
                for slot, n in ((0, k), (1, k - lag)):
                    if not 0 <= n < KT:
                        continue
                    if n == 0:
                        pe.wait_ge(w_hi[slot], pair + 1)
                        pe.wait_ge(w_lo[slot], pair + 1)
                    if slot == 0:
                        ready(n)
                    wh, wl, acc = whi[slot][:, n, :], wlo[slot][:, n, :], G[slot][:, :]
                    pe.matmul(acc, wh, hi[:, n, :], start=n == 0, stop=False)
                    pe.matmul(acc, wh, lo[:, n, :], start=False, stop=False)
                    mm = pe.matmul(acc, wl, hi[:, n, :], start=False, stop=n == KT - 1)
                    if n == KT - 1:
                        mm.then_inc(w_used[slot], 1)

        def mean(aux, src):
            pe.wait_ge(sem("aux_read"), aux)
            pe.matmul(AUX[:, :], invd[:, :], src, start=True, stop=True).then_inc(sem("aux_ready"), 1)

        def norm_mean(aux, n8):
            pe.wait_ge(sem("ssum_add"), n8)
            mean(aux, SSUM[:, :])

        def mod_sum(turn, src, rows):
            pe.wait_ge(sem("modc_ready"), turn)
            for r in range(rows):
                mm = pe.matmul(O[0:64, :], SEL[:, ROWS_MAX - 1 - r:ROWS_MAX - 1 - r + 64],
                               src[:, r * TOK:(r + 1) * TOK], start=(r == 0), stop=(r == rows - 1))
            mm.then_inc(sem("mod_summed"), 1)

        def mod_turn(turn, rows):
            pe.wait_ge(sem("mod_copied"), turn + 1)
            for q in range(4):
                mm = pe.matmul(O[:, q:4 * rows:4], MR[0:64, q * P:(q + 1) * P], ident[0:64, 0:rows], start=True, stop=True)
            mm.then_inc(sem("mod_turned"), 1)

        pe.wait_ge(sem("consts"), 4)
        pe.wait_ge(sem("rows_in"), 16 * (8 * DEPTH + 2))
        pe.transpose(TP[0][:, 0:PC], PV[0][0:PC, :], ident[0:PC, 0:PC]).then_inc(sem("ptp_ready"), 1)
        pe.transpose(TP[1][:, 0:PC], PV[1][0:PC, :], ident[0:PC, 0:PC]).then_inc(sem("ptp_ready"), 1)
        pe.transpose(O[:, 0:2 * KT], PV2[0:2 * KT, :], ident[0:2 * KT, 0:2 * KT]).then_inc(sem("ptp_ready"), 1)
        pe.wait_ge(sem("taps_in"), 16 * DEPTH)
        for l in range(DEPTH):
            for h in range(HEADS):
                mm = pe.transpose(G[l][:, h * CK:(h + 1) * CK], CWR[0:CK, l, h * P:(h + 1) * P], ident[0:CK, 0:CK])
            mm.then_inc(sem("tapsp_ready"), 1)
        for j in range(KT):
            if j >= 2:
                pe.wait_ge(sem("x_ready"), j - 1)
            for t in range(QB):
                if j == 0:
                    pe.wait_ge(sem(f"x_in{t}"), 16)
                mm = pe.transpose(bank[2 + j % 2][:, t * P:(t + 1) * P], XS[:, t, j * P:(j + 1) * P], ident[:, :])
            mm.then_inc(sem("xp_ready"), 1)
        pe.wait_ge(sem("table_in"), 32)
        pe.wait_ge(sem("pt_ready"), 3)
        pe.transpose(TP[0][0:BUCKETS, 0:HEADS], TBR[0:HEADS, :], ident[0:HEADS, 0:HEADS]).then_inc(sem("tbp_ready"), 1)
        pe.wait_ge(sem("tbx_ready"), 1)
        for h in range(HEADS):
            pe.wait_ge(sem("br_copied"), h)
            pe.matmul(O[:, :], TBX[0:BUCKETS + 1, h, :], OH[0:BUCKETS + 1, 0:TOK], start=True, stop=True)
            pe.matmul(AUX[:, 0:P], TBX[0:BUCKETS + 1, h, :], OH[0:BUCKETS + 1, TOK:TOK + P], start=True, stop=True)\
                .then_inc(sem("br_ready"), 1)
        pe.wait_ge(sem("br_copied"), HEADS)
        pe.wait_ge(sem("cw_ready"), DEPTH)
        pe.wait_ge(sem("ada0_step"), KT)
        mod_sum(0, ACC0, 4)
        mod_turn(0, 4)

        with pe.Fori(0, DEPTH) as l:
            pe.wait_ge(sem("o_read"), l * HEADS)
            for w in range(2):
                n_in, n_out = f"ffn{w + 1}_in", f"ffn{w + 1}_out"
                norm_mean(l * AUXN + AUX_NORM[2 * w], (l * 3 + 2 * w + 1) * KT)

                def ffn_tile(i):
                    p = l * PAIRS + PAIR0[n_in] + i
                    u = l * USES + USE0[n_in] + i
                    pe.wait_ge(acc_read[0], u)
                    slab(p, 0, G[0][:, :], HHI, HLO)
                    pe.wait_ge(acc_read[1], u)
                    slab(p, 1, G[1][:, :], HHI, HLO)

                for b in range(2):
                    pe.wait_ge(acc_read[b], l * USES + USE0[n_in])
                two_slabs(l * PAIRS + PAIR0[n_in], HHI, HLO,
                          lambda k: pe.wait_ge(sem("unit_lo"), l * UNITS + UNIT_NORM[2 * w] + k + 1))
                with pe.Fori(0, CHUNKS_IN[w]) as g:
                    seq = l * NMOD + CHUNK_SEQ[n_in] + g
                    for r in range(GROUP):
                        ffn_tile(g * GROUP + (r + 1))
                        if r == 4:
                            pe.wait_ge(sem("ada_step"), (seq + 1) * KT)
                            mod_sum(seq + 1, ACC, 2)
                        if r == 5:
                            mod_turn(seq + 1, 2)
                if w == 1:
                    with pe.Fori(1 + CHUNKS_IN[w] * GROUP, FT) as i:
                        ffn_tile(i)

                with pe.Fori(0, KT // 2) as i:
                    for m in range(6):
                        t, g = m // 3, m % 3
                        if g == 0:
                            pe.wait_ge(acc_read[t], l * USES + USE0[n_out] + i)
                        k0 = sum(OUTG[:g])
                        pe.wait_ge(sem("s_lo"), (l * 2 + w) * FT + (k0 + OUTG[g]))
                        slab(l * PAIRS + PAIR0[n_out] + i * 3 + m // 2, m % 2, G[t][:, :], SHI, SLO,
                             k0, OUTG[g], g == 0, g == 2)
                        if w == 0:
                            seq = l * NMOD + CHUNK_SEQ[n_out] + i
                            if m == 4:
                                pe.wait_ge(sem("ada_step"), (seq + 1) * KT)
                                mod_sum(seq + 1, ACC, 2)
                    if w == 0:
                        mod_turn(seq + 1, 2)
                if w == 1:
                    continue

                norm_mean(l * AUXN + AUX_NORM[1], (l * 3 + 2) * KT)

                def turn_weights(i, hh):
                    si = hh * 4 + (QB - 1 - i)
                    pe.wait_ge(sem("w_ready"), si + 1)
                    if i == 2:
                        pe.wait_ge(sem("v_ready"), hh + 1)
                    elif i < 2:
                        pe.wait_ge(sem("wt_ready"), si - 1)
                    for j in range(i + 1):
                        mm = pe.transpose(TP[i % 2][:, j * P:(j + 1) * P], PR[i % 2][0][:, j * P:(j + 1) * P], ident[:, :])
                    mm.then_inc(sem("t_ready"), 1)

                def values(hh):
                    pe.wait_ge(sem("wt_ready"), hh * 4 + 4)
                    pe.wait_ge(sem("o_read"), hh)
                    for j in range(QB):
                        mm = pe.matmul(O[:, j * P:TOK], V[:, j, :], WT[:, j, j * P:TOK], start=(j == 0), stop=(j == QB - 1))
                    mm.then_inc(sem("o_ready"), 1)

                def head_mean(h):
                    pe.wait_ge(sem("o_read"), l * HEADS + h + 1)
                    mean(l * AUXN + AUX_HEAD + h, SQ[:, :])

                def mix(h, first):
                    hh = l * HEADS + h
                    p = l * PAIRS + PAIR0["mix"] + h * 3
                    b = l * USES + USE0["mix"] + h * 3

                    def scores(i):
                        si, n = hh * 4 + (QB - 1 - i), (i + 1) * P
                        pe.wait_ge(sem("nmax_ready"), si)
                        for m in range(2):
                            mm = pe.matmul(S[m][:, 0:n], QT[m * HD:(m + 1) * HD, i * P:(i + 1) * P],
                                           KTT[m * HD:(m + 1) * HD, 0:n], start=True, stop=True)
                        mm.then_inc(sem("s_ready"), 1)

                    def turn_v():
                        pe.wait_ge(acc_read[0], b + 2)
                        pe.wait_ge(sem("wt_ready"), hh * 4)
                        for j in range(QB):
                            mm = pe.transpose(TP[0][:, j * P:(j + 1) * P], VT[:, j * P:(j + 1) * P], ident[:, :])
                        mm.then_inc(sem("vtp_ready"), 1)

                    if first:
                        for t in range(2):
                            pe.wait_ge(acc_read[t], b)
                        two_slabs(p, HHI, HLO,
                                  lambda k: pe.wait_ge(sem("unit_lo"), l * UNITS + UNIT_NORM[1] + k + 1))
                    else:
                        pe.wait_ge(acc_read[0], b)
                        slab(p, 0, G[0][:, :], HHI, HLO, at_half=lambda: turn_weights(1, hh - 1))
                        turn_weights(0, hh - 1)
                        pe.wait_ge(acc_read[1], b)
                        slab(p, 1, G[1][:, :], HHI, HLO, at_half=lambda: values(hh - 1))
                    pe.wait_ge(acc_read[0], b + 1)
                    slab(p + 1, 0, G[0][:, :], HHI, HLO, at_half=None if first else lambda: head_mean(h - 1))
                    pe.wait_ge(acc_read[1], b + 1)
                    slab(p + 1, 1, G[1][:, :], HHI, HLO, at_half=lambda: scores(3))
                    scores(2)
                    turn_v()
                    pe.wait_ge(acc_read[0], b + 2)
                    slab(p + 2, 0, G[0][:, :], HHI, HLO, at_half=lambda: scores(1))
                    turn_weights(3, hh)
                    scores(0)
                    pe.wait_ge(acc_read[1], b + 2)
                    slab(p + 2, 1, G[1][:, :], HHI, HLO, at_half=lambda: turn_weights(2, hh))

                mix(0, True)
                with pe.Fori(1, HEADS) as h:
                    mix(h, False)

                def branch(name, i, hi, lo, halves=(None, None)):
                    for t in range(2):
                        pe.wait_ge(acc_read[t], l * USES + USE0[name] + i)
                        slab(l * PAIRS + PAIR0[name] + i, t, G[t][:, :], hi, lo, at_half=halves[t])

                last = l * HEADS + HEADS - 1

                def last_head():
                    turn_weights(0, last)
                    values(last)

                branch("gb", 0, HHI, HLO, (lambda: turn_weights(1, last), last_head))
                head_mean(HEADS - 1)
                with pe.Fori(1, KT // 2) as i:
                    branch("gb", i, HHI, HLO)
                pe.wait_ge(sem("csum"), (l + 1) * KT)
                mean(l * AUXN + AUX_MEAN, SSUM[:, :])
                with pe.Fori(0, LN_VAR + 1 - KT // 2) as i:
                    pe.wait_ge(sem("unit_lo"), l * UNITS + UNIT_HEAD + HEADS)
                    branch("ab", i, AOHI, AOLO)
                pe.wait_ge(sem("lnadd"), (l + 1) * KT)
                mean(l * AUXN + AUX_VAR, SSUM[:, :])
                with pe.Fori(LN_VAR + 1 - KT // 2, KT // 2) as i:
                    branch("ab", i, AOHI, AOLO)
                with pe.Fori(0, KT // 2) as i:
                    for t in range(2):
                        pe.wait_ge(acc_read[t], l * USES + USE0["brb"] + i)
                        slab(l * PAIRS + PAIR0["brb"] + i, t, G[t][:, :], CHI, CLO,
                             ready=lambda k: pe.wait_ge(sem("unit_lo"), l * UNITS + UNIT_LN + k + 1))
                with pe.Fori(0, KT // 2) as i:
                    for t in range(2):
                        pe.wait_ge(acc_read[t], l * USES + USE0["mo"] + i)
                        slab(l * PAIRS + PAIR0["mo"] + i, t, G[t][:, :], MHI, MLO,
                             ready=lambda k: pe.wait_ge(sem("m_lo"), l * KT + k + 1))

        norm_mean(DEPTH * AUXN, (DEPTH * 3 + 1) * KT)
        for j in range(KT):
            pe.wait_ge(sem("fin"), j + 1)
            if j >= 2:
                pe.wait_ge(sem("y_ready"), j - 1)
            for t in range(QB):
                mm = pe.transpose(TP[j % 2][:, t * P:(t + 1) * P], F[j % 2][:, t * P:(t + 1) * P], ident[:, :])
            mm.then_inc(sem("yt_ready"), 1)

    ctx.close()


NAMES = ["x", "c", "ffn1_norm", "ffn1_w_in", "ffn1_w_out", "mix_norm", "w_mix_in", "lambda_q1", "lambda_k1",
         "lambda_q2", "lambda_k2", "subln_gain", "w_attn_branch", "conv_dw", "conv_dw_bias", "conv_ln_gain",
         "conv_ln_bias", "w_conv_branch", "w_mix_out", "ffn2_norm", "ffn2_w_in", "ffn2_w_out", "ada_w", "ada_b",
         "rel_bias", "final_norm"]


def kernel(**inputs):
    import concourse.bacc as bacc
    from concourse.bass_utils import run_bass_kernel_spmd

    nc = bacc.Bacc("TRN2", target_bir_lowering=False, num_devices=1)
    arrays, aps = {}, {}
    for name in NAMES:
        arr = np.ascontiguousarray(inputs[name])
        arrays[f"in_{name}"] = arr
        aps[name] = nc.dram_tensor(f"in_{name}", arr.shape, F32, kind="ExternalInput").ap()
    sel = bias_selection()
    arrays["in_bias_selection"] = sel
    onehot = nc.dram_tensor("in_bias_selection", sel.shape, F32, kind="ExternalInput").ap()
    out = nc.dram_tensor("out_0", (1, TOK, D), F32, kind="ExternalOutput").ap()
    build(nc, aps, onehot, out)
    r = run_bass_kernel_spmd(nc, [arrays], core_ids=[0])
    return r.results[0]["out_0"]
```

```python
import math
from contextlib import ExitStack

import numpy as np

import concourse.bass as bass
from concourse import mybir
from concourse.bass import ds

F32 = mybir.dt.float32
F32R = mybir.dt.float32r
ACT = mybir.ActivationFunctionType
ALU = mybir.AluOpType

P = 128
D = 1024
TOK = 512
DEPTH = 2
HEADS = D // 128
HD = 64
CK = 31
PADL = CK - 1
FF = ((8 * D // 3 + 255) // 256) * 256
BUCKETS = 32
MAXDIST = 128
EPS = 1e-6
NEG = -3.0e38

KT = D // P
FT = FF // P
QB = TOK // P
NMOD = 9
CHUNKS_IN = (3, 2)
CHUNKS_OUT = 4
CHUNK_SEQ = dict(ffn1_in=0, ffn1_out=3, ffn2_in=7)
GROUP = 7
GROUP_STEPS = ((0, 1), (2, 3), (4, 5), (6,), (7,), (), ())
OUT_STEPS = ((0, 1), (2, 3), (4, 5), (6, 7), (), ())
ROWS_MAX = 4
OUTG = (8, 8, 6)
assert sum(OUTG) == FT and DEPTH == 2 and 1 + CHUNKS_IN[0] * GROUP == FT

PH_PAIRS = dict(ffn1_in=FT, ffn1_out=12, mix=3 * HEADS, gb=KT // 2, ab=KT // 2, brb=KT // 2, mo=KT // 2, ffn2_in=FT, ffn2_out=12)
PH_USES = dict(ffn1_in=FT, ffn1_out=KT // 2, mix=3 * HEADS, gb=KT // 2, ab=KT // 2, brb=KT // 2, mo=KT // 2, ffn2_in=FT, ffn2_out=KT // 2)


def starts(sizes):
    out, at = {}, 0
    for name, n in sizes.items():
        out[name] = at
        at += n
    return out, at


PAIR0, PAIRS = starts(PH_PAIRS)
USE0, USES = starts(PH_USES)

AUXN = 3 + HEADS + 2
AUX_NORM = (0, 1, AUXN - 1)
AUX_HEAD, AUX_MEAN, AUX_VAR = 2, 2 + HEADS, 3 + HEADS
RSN = 3 + HEADS + 1
RS_NORM = (0, 1, RSN - 1)
RS_HEAD, RS_VAR = 2, 2 + HEADS
UNITS = 3 * KT + HEADS + KT
UNIT_NORM = (0, KT, UNITS - KT)
UNIT_HEAD, UNIT_LN = 2 * KT, 2 * KT + HEADS
ZERO_FFN1, ZERO_CONV, ZERO_LN, ZERO_MO, ZERO_FFN2, ZEROS = 1, 2, 3, 4, 5, 5

LN_MEAN, LN_VAR = 2, 4
LN_UNITS = {4: (0, 1), 5: (2, 3), 6: (4, 5, 6), 7: (7,)}

PC_NORM = (0, 8, 16)
PC_DWB, PC_LNG, PC_LNB, PC_SUB, PC_ADA = 24, 32, 40, 48, 49
PC = PC_ADA + NMOD * KT
DVE_TAPS = 21
POOL_TAPS = CK - DVE_TAPS


def bias_selection():
    x = np.arange(TOK + P)
    dist = (TOK - 1) - x
    n = np.maximum(dist, 0)
    exact = BUCKETS // 2
    nf = np.maximum(n, 1).astype(np.float32)
    large = exact + (np.log(nf / np.float32(exact)) / np.float32(math.log(MAXDIST / exact))
                     * np.float32(BUCKETS - exact)).astype(np.int32)
    large = np.minimum(large, BUCKETS - 1)
    bucket = np.where(n < exact, n, large)
    sel = np.zeros((BUCKETS + 1, x.size), np.float32)
    ok = dist >= 0
    sel[bucket[ok], x[ok]] = 1.0
    sel[BUCKETS, ~ok] = 1.0
    return sel


def build(nc, a, onehot, out):
    ctx = ExitStack()
    names = {}

    def sem(name):
        if name not in names:
            names[name] = ctx.enter_context(nc.semaphore(name))
        return names[name]

    place = [(nc.sbuf_base + 31) // 32 * 32]

    def at(name, shape, dt, offset=None):
        size = int(np.prod(shape[1:])) * 4
        if offset is None:
            offset = place[0]
            place[0] += (size + 31) // 32 * 32
        assert offset + size <= nc.sbuf_usable_end - 64, name
        return nc.alloc_sbuf_tensor_at(name, shape, dt, offset=offset)

    KB = 1024
    X = at("x_res", [P, KT, TOK], F32)
    h0 = place[0]
    HHI = at("h_hi", [P, KT, TOK], F32R)
    HLO = at("h_lo", [P, KT, TOK], F32R)
    r0 = place[0]
    place[0] += 96 * KB
    raw = [at(f"w_raw{s}", [P, 8, P], F32) for s in range(2)]
    whi = [at(f"w_hi{s}", [P, 8, P], F32R) for s in range(2)]
    wlo = [at(f"w_lo{s}", [P, 8, P], F32R) for s in range(2)]
    SQ = at("squares", [P, TOK], F32)
    SSUM = at("running_sum", [P, TOK], F32)
    RSTD = at("rstd", [P, TOK], F32)
    T = [at(f"scaled{i}", [P, TOK], F32) for i in range(2)]
    F = [at(f"full{i}", [P, TOK], F32) for i in range(2)]
    raw_at = place[0]
    ada_raw = [at(f"ada_raw{i}", [P, D], F32, None if i < 2 else r0 + 2 * FT * TOK * 4 + (i - 2) * 4 * KB)
               for i in range(4)]
    acc0 = place[0]
    ACC = at("ada_acc", [P, D], F32)
    mr0 = place[0]
    MR = at("mod_rows", [P, TOK], F32)
    tap_tmp = [at(f"tap_tmp{i}", [P, TOK], F32, acc0 + 2 * KB * i) for i in range(2)]
    ACCH = at("ada_acc_hi", [P, D], F32R, raw_at)
    ACCL = at("ada_acc_lo", [P, D], F32R, raw_at + 4 * KB)
    SELR = at("row_select_r", [P, 64 + ROWS_MAX - 1], F32R)
    SEL = at("row_select", [P, 64 + ROWS_MAX - 1], F32)
    BT = at("bias_tile", [P, TOK], F32)
    ident = at("ident", [P, P], F32)
    invd = at("inv_d", [P, P], F32)
    PT = at("params", [P, DEPTH * PC], F32)
    PT2 = at("params2", [P, 2 * KT], F32)
    CA = at("c_act", [P, KT], F32)
    MODC = at("modulation", [P, DEPTH * NMOD * KT], F32)
    AC = at("norm_scale", [P, 3, KT], F32)
    GC = at("gates", [P, 3, KT], F32)
    CW = at("conv_taps", [P, DEPTH * HEADS, CK], F32)
    tapw = at("pool_taps", [P, POOL_TAPS], F32)
    spare = at("spare", [P, 2], F32)
    eps = at("eps", [P, 1], F32)
    root_warm = at("root_warm", [P, 1], F32)
    lam_dot = at("lam_dot", [P, 2 * DEPTH], F32)
    lam_exp = at("lam_exp", [P, 2 * DEPTH], F32)
    nlam = at("neg_lambda", [P, DEPTH], F32)
    subg = at("subln", [P, DEPTH], F32)
    mx = at("row_max", [P, 2, 2], F32)
    nmx = at("neg_row_max", [P, 2, 2], F32)
    rsum = at("row_sum", [P, 2, 2], F32)
    rinv = at("row_inv", [P, 2, 2], F32)
    rlam = at("row_inv_lam", [P, 2], F32)
    SHI = at("s_hi", [P, FT, TOK], F32R, r0)
    SLO = at("s_lo", [P, FT, TOK], F32R, r0 + FT * TOK * 4)
    AOHI = at("ao_hi", [P, KT, TOK], F32R, r0)
    AOLO = at("ao_lo", [P, KT, TOK], F32R, r0 + 16 * KB)
    C = at("conv", [P, KT, TOK], F32, r0 + 32 * KB)
    CHI = at("conv_hi", [P, KT, TOK], F32R, r0 + 32 * KB)
    GA = at("gate_a", [P, KT, TOK], F32, r0 + 48 * KB)
    MHI = at("merged_hi", [P, KT, TOK], F32R, r0 + 48 * KB)
    MLO = HLO
    ph = r0 + 64 * KB
    QT = at("q_t", [P, TOK], F32, ph)
    KTT = at("k_t", [P, TOK], F32, ph + 2 * KB)
    VT = at("v_t", [P, TOK], F32, ph + 4 * KB)
    OT = at("o_t", [P, TOK], F32, mr0)
    V = at("v", [P, QB, P], F32, ph + 6 * KB)
    WT = at("weights_t", [P, QB, TOK], F32, ph + 8 * KB)
    GB = at("gate_b", [P, KT, TOK], F32, ph)
    CLO = at("conv_lo", [P, KT, TOK], F32R, ph + 16 * KB)
    PR = [[at(f"probs{par}_{m}", [P, (3 + par) * P], F32, ph + 16 * KB + par * 3 * KB + m * (3 + par) * 512)
           for m in range(2)] for par in range(2)]
    z0 = ph + 23 * KB
    Z = at("glu", [P, TOK + 32], F32, z0)
    CAB = [at(f"conv_part{i}", [P, TOK], F32, z0 + 2176 + 2 * KB * i) for i in range(2)]
    CP = at("conv_pool", [P, TOK], F32, z0 + 2176 + 4 * KB)
    ADA0 = at("ada_first", [P, KT, 2 * D], F32, r0)
    XS = at("x_rows", [P, QB, D], F32, r0 + 64 * KB)
    s0 = r0 + 80 * KB
    PV = [at(f"param_rows{l}", [P, P], F32, s0 + 512 * l) for l in range(DEPTH)]
    PV2 = at("param_rows2", [P, P], F32, s0 + 1024)
    OH = at("onehot_sb", [P, TOK + P], F32, s0 + 1536)
    TBR = at("table_rows", [P, BUCKETS], F32, s0 + 4096)
    TB = at("table_t", [P, HEADS], F32, s0 + 4224)
    TBX = at("table_wide", [P, HEADS, P], F32, s0 + 4256)
    LV = at("lambda_rows", [P, DEPTH, 4, HD], F32, s0 + 8352)
    ACC0 = at("ada_acc_first", [P, 2 * D], F32, h0 + 16 * KB)
    BR = [at(f"bias_row{i}", [P, TOK + P], F32, h0 + (8 if i < 3 else 24) * KB + 2560 * (i % 3)) for i in range(6)]
    CWR = at("tap_rows", [P, DEPTH, D], F32, h0)
    YO = at("y_rows", [P, QB, D], F32, r0)

    bank = [ctx.enter_context(nc.psum_tensor(f"bank{i}", [P, TOK], F32)) for i in range(8)]
    G = bank[0:2]
    S = bank[2:4]
    TP = bank[4:6]
    O = bank[6]
    AUX = bank[7]
    ROW_BANKS = ((O, AUX), (TP[1], TP[0]))

    def flat(t):
        return t[:, :, :].rearrange("p k t -> p (k t)")

    def tile(view, j, width=TOK):
        return view[:, ds(j * width, width)]

    X2, C2, GA2, GB2 = flat(X), flat(C), flat(GA), flat(GB)
    SHI2, SLO2, MHI2, MLO2 = flat(SHI), flat(SLO), flat(MHI), flat(MLO)
    AOHI2, AOLO2, CW2 = flat(AOHI), flat(AOLO), flat(CW)

    BD = nc.dram_tensor("bias_rows", [HEADS + 1, P * (TOK + P)], F32, kind="Internal")

    w_in = [a["ffn1_w_in"].rearrange("l (k p) f -> p (l k) f", p=P), a["ffn2_w_in"].rearrange("l (k p) f -> p (l k) f", p=P)]
    w_out = [a["ffn1_w_out"].rearrange("l (k p) f -> p (l k) f", p=P), a["ffn2_w_out"].rearrange("l (k p) f -> p (l k) f", p=P)]
    w_mix = a["w_mix_in"].rearrange("l (k p) f -> p (l k) f", p=P)
    w_ab = a["w_attn_branch"].rearrange("l (k p) f -> p (l k) f", p=P)
    w_cb = a["w_conv_branch"].rearrange("l (k p) f -> p (l k) f", p=P)
    w_mo = a["w_mix_out"].rearrange("l (k p) f -> p (l k) f", p=P)
    w_ada = a["ada_w"].rearrange("l (k p) f -> p (l k) f", p=P)

    block = ctx.enter_context(nc.Block())
    w_raw = [sem(f"w_raw_in{s}") for s in range(2)]
    w_hi = [sem(f"w_hi_done{s}") for s in range(2)]
    w_lo = [sem(f"w_lo_done{s}") for s in range(2)]
    w_used = [sem(f"w_used{s}") for s in range(2)]
    acc_read = [sem(f"acc_read{b}") for b in range(2)]

    @block.sync
    def _(sp):
        def slab(pair, slot, src, n=8):
            sp.wait_ge(w_lo[slot], pair)
            sp.dma_start(raw[slot][:, 0:n, :], src).then_inc(w_raw[slot], 16)

        def cols(w, k0, n, c0):
            return w[:, ds(k0, n), ds(c0, P)]

        for t in range(QB):
            sp.dma_start(XS[:, t, :], a["x"][0, t * P:(t + 1) * P, :]).then_inc(sem(f"x_in{t}"), 16)
        for l in range(DEPTH):
            rows = [("ffn1_norm", KT), ("mix_norm", KT), ("ffn2_norm", KT), ("conv_dw_bias", KT),
                    ("conv_ln_gain", KT), ("conv_ln_bias", KT), ("subln_gain", 1), ("ada_b", NMOD * KT)]
            r = 0
            for name, n in rows:
                sp.dma_start(PV[l][r:r + n, :], a[name][l, :].rearrange("(r c) -> r c", c=P)).then_inc(sem("rows_in"), 16)
                r += n
            assert r == PC

        with sp.Fori(0, DEPTH) as l:
            pair = l * PAIRS
            for w in range(2):
                with sp.Fori(0, FT) as i:
                    p = pair + PAIR0[f"ffn{w + 1}_in"] + i
                    slab(p, 0, cols(w_in[w], l * KT, 8, i * P))
                    slab(p, 1, cols(w_in[w], l * KT, 8, i * P + FF))
                with sp.Fori(0, KT // 2) as i:
                    for m in range(6):
                        p = pair + PAIR0[f"ffn{w + 1}_out"] + i * 3 + m // 2
                        slab(p, m % 2, cols(w_out[w], l * FT + sum(OUTG[:m % 3]), OUTG[m % 3], i * (2 * P) + (m // 3) * P), OUTG[m % 3])
                if w == 1:
                    continue
                with sp.Fori(0, HEADS) as h:
                    for m in range(6):
                        slab(pair + PAIR0["mix"] + h * 3 + m // 2, m % 2, cols(w_mix, l * KT, 8, h * P + m * D))
                for name, wt, c0 in (("gb", w_mix, 6 * D), ("ab", w_ab, 0), ("brb", w_cb, 0), ("mo", w_mo, 0)):
                    with sp.Fori(0, KT // 2) as i:
                        for t in range(2):
                            slab(pair + PAIR0[name] + i, t, cols(wt, l * KT, 8, i * (2 * P) + t * P + c0))
        for s in range(2):
            slab(DEPTH * PAIRS, s, cols(w_mo, 0, 8, 0))

        for half in range(2):
            for t in range(QB):
                sp.wait_ge(sem("y_ready"), (half + 1) * KT // 2)
                c0 = half * (D // 2)
                sp.dma_start(out[0, t * P:(t + 1) * P, c0:c0 + D // 2], YO[:, t, c0:c0 + D // 2]).then_inc(sem("y_out"), 16)
        sp.wait_ge(sem("y_out"), 16 * 2 * QB)
        for s in range(2):
            sp.wait_ge(w_raw[s], 16 * (DEPTH * PAIRS + 1))

    @block.gpsimd
    def _(pool):
        pool.memset(ident[:, :], 0.0).then_inc(sem("ident0"), 1)
        pool.memset(invd[:, :], 1.0 / D).then_inc(sem("consts"), 1)
        pool.memset(eps[:, :], EPS).then_inc(sem("consts"), 1)
        pool.memset(SEL[:, :], 0.0).then_inc(sem("sel0"), 1)
        pool.wait_ge(sem("sel0"), 1)
        pool.memset(SEL[:, ROWS_MAX - 1:ROWS_MAX], 1.0).then_inc(sem("consts"), 1)
        pool.wait_ge(sem("ident0"), 1)
        pool.affine_select(out=ident[:, :], in_=ident[:, :], compare_op=ALU.not_equal, fill=1.0, base=0,
                           pattern=[[-1, P]], channel_multiplier=1).then_inc(sem("consts"), 1)
        for k in range(KT):
            pool.dma_start(ADA0[:, k, :], w_ada[:, k, 0:2 * D]).then_inc(sem(f"ada0_in{k}"), 16)

        def carry_wait():
            pool.tensor_tensor(spare[:, 0:1], eps[:, 0:1], eps[:, 0:1], ALU.add)

        def ada_chunk(layer, m, seq):
            for k in range(KT):
                if k < 4:
                    pool.wait_ge(sem("mod_summed"), seq + 1)
                else:
                    pool.wait_ge(sem("ada_step"), seq * KT + (k - 3))
                pool.dma_start(ada_raw[k % 4][:, :], w_ada[:, ds(layer * KT + k, 1), ds(m * D, D)].rearrange("p o f -> p (o f)"))\
                    .then_inc(sem(f"ada_in{k % 4}"), 16)

        def pool_taps(l, h):
            q = h + l * HEADS
            pool.wait_ge(sem("z_ready"), q + 1)
            pool.wait_ge(sem("c_ready"), q)
            pool.tensor_copy(tapw[:, :], CW2[:, ds(q * CK + DVE_TAPS, POOL_TAPS)]).then_inc(sem("tapw_ready"), 1)
            pool.wait_ge(sem("tapw_ready"), q + 1)
            carry_wait()
            for n in range(POOL_TAPS):
                t = DVE_TAPS + n
                tmp = tap_tmp[n % 2][:, :]
                dst = CP[:, :] if n == 0 else tmp
                pool.tensor_scalar(dst, Z[:, t:t + TOK], tapw[:, n:n + 1], 0.0, ALU.mult, ALU.add)\
                    .then_inc(sem("ptap_mul"), 1)
                if n == 0:
                    continue
                pool.wait_ge(sem("ptap_mul"), q * POOL_TAPS + (n + 1))
                if n > 1:
                    pool.wait_ge(sem("ptap_add"), q * (POOL_TAPS - 2) + (n - 1))
                pool.tensor_tensor(CP[:, :], CP[:, :], tmp, ALU.add)\
                    .then_inc(sem("cp_ready" if n == POOL_TAPS - 1 else "ptap_add"), 1)
            c = tile(C2, h)
            pool.wait_ge(sem("c_part"), q + 1)
            pool.wait_ge(sem("cp_ready"), q + 1)
            carry_wait()
            pool.tensor_tensor(c, c, CP[:, :], ALU.add).then_inc(sem("c_ready"), 1)
            pool.wait_ge(sem("csum"), q)
            pool.wait_ge(sem("ssum_clear"), l * ZEROS + 1 + ZERO_CONV)
            pool.wait_ge(sem("c_ready"), q + 1)
            carry_wait()
            pool.tensor_tensor(SSUM[:, :], SSUM[:, :], c, ALU.add).then_inc(sem("csum"), 1)

        pool.wait_ge(sem("ada0_step"), KT)
        pool.wait_ge(sem("lam_dots"), 2 * DEPTH)
        pool.wait_ge(sem("br_ready"), HEADS)
        with pool.Fori(0, DEPTH) as l:
            with pool.Fori(0, CHUNKS_IN[0]) as g:
                ada_chunk(l, g + 2, l * NMOD + g)
            with pool.Fori(0, CHUNKS_OUT) as g:
                ada_chunk(l, g + (2 + CHUNKS_IN[0]), l * NMOD + CHUNK_SEQ["ffn1_out"] + g)
            pool.wait_ge(sem("cw_ready"), 2)
            with pool.Fori(0, HEADS) as h:
                pool_taps(l, h)
            with pool.Fori(0, CHUNKS_IN[1]) as g:
                pool.wait_ge(acc_read[1], l * USES + USE0["mo"])
                ada_chunk(1, g, l * NMOD + CHUNK_SEQ["ffn2_in"] + g)
        for i in range(4):
            pool.wait_ge(sem(f"ada_in{i}"), DEPTH * NMOD * (KT // 4) * 16)

    @block.scalar
    def _(act):
        def w_hi_part(pair, slot, n=8):
            act.wait_ge(w_raw[slot], (pair + 1) * 16)
            act.wait_ge(w_used[slot], pair)
            act.activation(whi[slot][:, 0:n, :], raw[slot][:, 0:n, :], ACT.Copy).then_inc(w_hi[slot], 1)

        def root(aux, unit, scale=1.0):
            act.activation(root_warm[:, :], eps[:, :], ACT.Sqrt)
            act.wait_ge(sem("aux_ready"), aux + 1)
            act.wait_ge(sem("unit_t"), unit)
            act.activation(RSTD[:, :], AUX[:, :], ACT.Sqrt, bias=eps[:, 0:1], scale=scale).then_inc(sem("aux_read"), 1)

        def unit_split(u, b, first, hi, func, scale, bias):
            act.wait_ge(sem("unit_t"), u + 1)
            act.wait_ge(sem("unit_lo"), u if first else u - 1)
            act.activation(F[b][:, :], T[b][:, :], func, bias=bias, scale=scale).then_inc(sem("unit_f"), 1)
            act.activation(hi, T[b][:, :], func, bias=bias, scale=scale).then_inc(sem("unit_hi"), 1)

        def unit_hi(u, b, hi, bias=0.0):
            act.wait_ge(sem("unit_t"), u + 1)
            act.activation(hi, T[b][:, :], ACT.Identity, bias=bias).then_inc(sem("unit_hi"), 1)

        def norm_units(l, k):
            root(l * AUXN + AUX_NORM[k], l * UNITS + UNIT_NORM[k])
            act.wait_ge(sem("ac_ready"), l * 3 + (k + 1))
            for j in range(KT):
                unit_hi(l * UNITS + UNIT_NORM[k] + j, j % 2, HHI[:, j, :],
                        MODC[:, ds(l * (NMOD * KT) + 3 * k * KT + j, 1)])

        def square_x(bank_use, t, n8, j):
            act.wait_ge(acc_read[t], bank_use + 1)
            act.wait_ge(sem("ssum_add"), n8 + j)
            act.activation(SQ[:, :], tile(X2, j), ACT.Square).then_inc(sem("sq_ready"), 1)

        act.dma_start(PV2[KT:2 * KT, :], a["c"][0, :].rearrange("(r c) -> r c", c=P)).then_inc(sem("rows2_in"), 16)
        act.dma_start(PV2[0:KT, :], a["final_norm"].rearrange("(r c) -> r c", c=P)).then_inc(sem("rows2_in"), 16)
        for l in range(DEPTH):
            act.dma_start(CWR[0:CK, l, :], a["conv_dw"][l, :, :]).then_inc(sem("taps_in"), 16)
        act.dma_start(TBR[0:HEADS, :], a["rel_bias"]).then_inc(sem("table_in"), 16)
        act.dma_start(OH[0:BUCKETS + 1, :], onehot).then_inc(sem("table_in"), 16)
        for l in range(DEPTH):
            for n, name in enumerate(("lambda_q1", "lambda_k1", "lambda_q2", "lambda_k2")):
                act.dma_start(LV[:, l, n, :], bass.AP(a[name].tensor, l * HD, [[0, P], [1, HD]]))\
                    .then_inc(sem("lambda_in"), 16)
        act.wait_ge(sem("pt_ready"), 1)
        act.activation(CA[:, :], PT2[:, KT:2 * KT], ACT.Silu).then_inc(sem("ca_ready"), 1)
        act.wait_ge(sem("consts"), 4)
        for j in range(KT):
            act.wait_ge(sem("xp_ready"), j + 1)
            act.activation(X[:, j, :], bank[2 + j % 2][:, :], ACT.Copy).then_inc(sem("x_ready"), 1)
            act.wait_ge(sem("ssum_add"), j)
            act.activation(SQ[:, :], bank[2 + j % 2][:, :], ACT.Square).then_inc(sem("sq_ready"), 1)
        act.wait_ge(sem("tapsp_ready"), DEPTH)
        for l in range(DEPTH):
            act.activation(CW2[:, l * HEADS * CK:(l + 1) * HEADS * CK], G[l][:, 0:HEADS * CK], ACT.Copy)\
                .then_inc(sem("cw_ready"), 1)
        for h in range(HEADS):
            act.wait_ge(sem("br_ready"), h + 1)
            if h >= len(BR):
                act.wait_ge(sem(f"br_out{h % len(BR)}"), 16)
            if h == len(BR):
                act.wait_ge(sem("br_again"), 16)
            act.activation(BR[h % len(BR)][:, 0:TOK], ROW_BANKS[h % 2][0][:, :], ACT.Copy).then_inc(sem("br_part"), 1)
            act.activation(BR[h % len(BR)][:, TOK:TOK + P], ROW_BANKS[h % 2][1][:, 0:P], ACT.Copy).then_inc(sem("br_copied"), 1)
            act.wait_ge(sem("br_copied"), h + 1)
            act.wait_ge(sem("br_part"), h + 1)
            act.dma_start(BD[h, :].rearrange("(p x) -> p x", p=P), BR[h % len(BR)][:, :]).then_inc(sem(f"br_out{h % len(BR)}"), 16)
            if h == 0:
                act.dma_start(BD[HEADS, :].rearrange("(p x) -> p x", p=P), BR[0][:, :]).then_inc(sem("br_again"), 16)
        for i in range(len(BR)):
            act.wait_ge(sem(f"br_out{i}"), 16 * len(range(i, HEADS, len(BR))))

        act.wait_ge(sem("lam_dots"), 2 * DEPTH)
        act.activation(lam_exp[:, :], lam_dot[:, :], ACT.Exp).then_inc(sem("lam_exps"), 1)
        for s in range(2):
            w_hi_part(0, s)

        def load_bias_tile(h):
            src = BD[ds(h, 1), :]
            src = bass.AP(src.tensor, src.offset + (P - 1), [[TOK + P - 1, P], [1, TOK]])
            act.dma_start(BT[:, :], src).then_inc(sem("bt_in"), 16)

        load_bias_tile(0)

        with act.Fori(0, DEPTH) as l:
            for w in range(2):
                n_in, n_out = f"ffn{w + 1}_in", f"ffn{w + 1}_out"
                norm_units(l, 2 * w)
                with act.Fori(0, FT) as i:
                    p = l * PAIRS + PAIR0[n_in] + i
                    u = l * USES + USE0[n_in] + i
                    w_hi_part(p + 1, 0)
                    act.wait_ge(acc_read[0], u)
                    act.activation(T[0][:, :], G[0][:, :], ACT.Tanh, scale=0.5).then_inc(sem("g_tanh"), 1)
                    w_hi_part(p + 1, 1)
                    act.wait_ge(acc_read[1], u + 1)
                    act.activation(tile(SHI2, i), F[0][:, :], ACT.Copy).then_inc(sem("s_hi"), 1)
                with act.Fori(0, KT // 2) as i:
                    for m in range(6):
                        w_hi_part(l * PAIRS + PAIR0[n_out] + i * 3 + m // 2 + 1, m % 2,
                                  OUTG[(m + 2) % 3] if m < 4 else 8)
                        if m % 3 == 2:
                            square_x(l * USES + USE0[n_out] + i, m // 3, (l * 3 + 1 + 2 * w) * KT, i * 2 + m // 3)
                if w == 1:
                    continue

                norm_units(l, 1)

                def weights(i, hh):
                    act.wait_ge(sem("t_ready"), hh * 4 + (QB - i))
                    act.activation(WT[:, 0:i + 1, i * P:(i + 1) * P],
                                   TP[i % 2][:, 0:(i + 1) * P].rearrange("p (j t) -> p j t", t=P),
                                   ACT.Copy).then_inc(sem("wt_ready"), 1)

                def head_output(hh):
                    act.wait_ge(sem("o_ready"), hh + 1)
                    act.activation(OT[:, :], O[:, :], ACT.Copy).then_inc(sem("o_copied"), 1)
                    act.activation(SQ[:, :], O[:, :], ACT.Square).then_inc(sem("o_read"), 1)

                def mix(h, first):
                    hh = l * HEADS + h
                    p = l * PAIRS + PAIR0["mix"] + h * 3
                    b = l * USES + USE0["mix"] + h * 3

                    def exps(i):
                        par, si, n = i % 2, hh * 4 + (QB - 1 - i), (i + 1) * P
                        act.wait_ge(sem("nmax_ready"), si + 1)
                        for m in range(2):
                            act.activation(PR[par][m][:, 0:n], PR[par][m][:, 0:n], ACT.Exp, bias=nmx[:, par, m:m + 1],
                                           accum_out=rsum[:, par, m:m + 1]).then_inc(sem("exp_done"), 1)

                    if not first:
                        weights(1, hh - 1)
                    w_hi_part(p + 1, 0)
                    act.activation(QT[:, :], G[0][:, :], ACT.Copy, scale=HD ** -0.5).then_inc(acc_read[0], 1)
                    if not first:
                        weights(0, hh - 1)
                        head_output(hh - 1)
                    w_hi_part(p + 1, 1)
                    act.activation(KTT[:, :], G[1][:, :], ACT.Copy).then_inc(acc_read[1], 1)
                    if not first:
                        root(l * AUXN + AUX_HEAD + h - 1, l * UNITS + UNIT_HEAD + h - 1, float(D // P))
                    w_hi_part(p + 2, 0)
                    act.activation(VT[:, :], G[0][:, :], ACT.Copy).then_inc(acc_read[0], 1)
                    if not first:
                        unit_hi(l * UNITS + UNIT_HEAD + h - 1, 0, tile(AOHI2, h - 1))
                    exps(3)
                    w_hi_part(p + 2, 1)
                    act.wait_ge(sem("z_ready"), hh)
                    act.activation(T[1][:, :], G[1][:, :], ACT.Copy, scale=0.5).then_inc(acc_read[1], 1)
                    act.wait_ge(sem("vtp_ready"), hh + 1)
                    act.activation(V[:, :, :].rearrange("p j e -> p (j e)"), TP[0][:, :], ACT.Copy).then_inc(sem("v_ready"), 1)
                    exps(2)
                    weights(3, hh)
                    exps(1)
                    w_hi_part(p + 3, 0)
                    act.activation(F[1][:, :], G[0][:, :], ACT.Tanh, scale=0.5).then_inc(acc_read[0], 1)
                    exps(0)
                    load_bias_tile(h + 1)
                    weights(2, hh)
                    w_hi_part(p + 3, 1)
                    act.activation(tile(GA2, h), G[1][:, :], ACT.Tanh, scale=0.5).then_inc(acc_read[1], 1)

                mix(0, True)
                with act.Fori(1, HEADS) as h:
                    mix(h, False)

                for j in range(KT):
                    p = l * PAIRS + PAIR0["gb"] + j
                    if j == 0:
                        weights(1, l * HEADS + HEADS - 1)
                    w_hi_part(p + 1, 0)
                    if j < KT // 2:
                        act.activation(GB[:, 2 * j, :], G[0][:, :], ACT.Tanh, scale=0.5).then_inc(acc_read[0], 1)
                    if j == 0:
                        weights(0, l * HEADS + HEADS - 1)
                        head_output(l * HEADS + HEADS - 1)
                        root(l * AUXN + AUX_HEAD + HEADS - 1, l * UNITS + UNIT_HEAD + HEADS - 1, float(D // P))
                    w_hi_part(p + 1, 1)
                    if j < KT // 2:
                        act.activation(GB[:, 2 * j + 1, :], G[1][:, :], ACT.Tanh, scale=0.5).then_inc(acc_read[1], 1)
                    if j == 0:
                        unit_hi(l * UNITS + UNIT_HEAD + HEADS - 1, 0, AOHI[:, HEADS - 1, :])
                    if j == LN_MEAN:
                        act.wait_ge(sem("aux_ready"), l * AUXN + AUX_MEAN + 1)
                        act.activation(F[1][:, :], AUX[:, :], ACT.Copy).then_inc(sem("aux_read"), 1)
                    if j in (LN_MEAN, LN_MEAN + 1):
                        for n in range(4 * (j - LN_MEAN), 4 * (j - LN_MEAN) + 4):
                            act.wait_ge(sem("xc_ready"), l * KT + n + 1)
                            act.wait_ge(sem("lnadd"), l * KT + n)
                            act.activation(SQ[:, :], C[:, n, :], ACT.Square).then_inc(sem("lnsq"), 1)
                    if j == LN_VAR:
                        root(l * AUXN + AUX_VAR, l * UNITS + UNIT_LN)
                    for n in LN_UNITS.get(j, ()):
                        unit_split(l * UNITS + UNIT_LN + n, n % 2, n == 0, CHI[:, n, :], ACT.Silu,
                                   PT[:, ds(l * PC + PC_LNG + n, 1)], PT[:, ds(l * PC + PC_LNB + n, 1)])
                with act.Fori(0, KT // 2) as i:
                    for t in range(2):
                        w_hi_part(l * PAIRS + PAIR0["brb"] + i + 1, t)
                        act.wait_ge(sem("merged"), l * KT + i * 2 + (t + 1))
                        act.activation(tile(MHI2, i * 2 + t), F[t][:, :], ACT.Copy).then_inc(sem("m_hi"), 1)
                with act.Fori(0, KT // 2) as i:
                    for t in range(2):
                        w_hi_part(l * PAIRS + PAIR0["mo"] + i + 1, t)
                        square_x(l * USES + USE0["mo"] + i, t, (l * 3 + 2) * KT, i * 2 + t)

        root(DEPTH * AUXN, DEPTH * UNITS)
        for j in range(KT):
            act.wait_ge(sem("yt_ready"), j + 1)
            act.activation(YO[:, :, j * P:(j + 1) * P], TP[j % 2][:, :].rearrange("p (t c) -> p t c", c=P), ACT.Copy)\
                .then_inc(sem("y_ready"), 1)
        act.wait_ge(sem("bt_in"), 16 * (DEPTH * HEADS + 1))

    @block.vector
    def _(dve):
        def w_lo_part(pair, slot, n=8):
            dve.wait_ge(w_hi[slot], pair + 1)
            dve.tensor_tensor(wlo[slot][:, 0:n, :], raw[slot][:, 0:n, :], whi[slot][:, 0:n, :].bitcast(F32),
                              ALU.subtract).then_inc(w_lo[slot], 1)

        def clear_sum():
            dve.memset(SSUM[:, :], 0.0).then_inc(sem("ssum_clear"), 1)

        def sum_cleared(count):
            dve.wait_ge(sem("ssum_clear"), count)

        def reciprocal(aux, r):
            dve.wait_ge(sem("aux_read"), aux + 1)
            dve.reciprocal(RSTD[:, :], RSTD[:, :]).then_inc(sem("rstd_ready"), 1)
            dve.wait_ge(sem("rstd_ready"), r + 1)

        def unit_scale(u, b, first, src):
            dve.wait_ge(sem("unit_hi"), u if first else u - 1)
            dve.tensor_tensor(T[b][:, :], src, RSTD[:, :], ALU.mult).then_inc(sem("unit_t"), 1)

        def unit_gain(u, b, first, src, gain):
            dve.wait_ge(sem("unit_lo"), u if first else u - 1)
            dve.scalar_tensor_tensor(out=T[b][:, :], in0=src, scalar=gain, in1=RSTD[:, :],
                                     op0=ALU.mult, op1=ALU.mult).then_inc(sem("unit_t"), 1)

        def unit_lo(u, b, lo, hi, shift=None):
            dve.wait_ge(sem("unit_hi"), u + 1)
            if shift is None:
                ins = dve.tensor_tensor(lo, T[b][:, :], hi.bitcast(F32), ALU.subtract)
            else:
                ins = dve.scalar_tensor_tensor(out=lo, in0=T[b][:, :], scalar=shift, in1=hi.bitcast(F32),
                                               op0=ALU.add, op1=ALU.subtract)
            ins.then_inc(sem("unit_lo"), 1)

        def unit_rest(u, b, lo, hi):
            dve.wait_ge(sem("unit_hi"), u + 1)
            dve.tensor_tensor(lo, F[b][:, :], hi.bitcast(F32), ALU.subtract).then_inc(sem("unit_lo"), 1)

        def norm_units(l, k):
            reciprocal(l * AUXN + AUX_NORM[k], l * RSN + RS_NORM[k])
            u = l * UNITS + UNIT_NORM[k]
            for j in range(KT + 1):
                if j < KT:
                    unit_gain(u + j, j % 2, j == 0, X[:, j, :], AC[:, k, j:j + 1])
                if j:
                    unit_lo(u + (j - 1), (j - 1) % 2, HLO[:, j - 1, :], HHI[:, j - 1, :],
                            MODC[:, ds(l * (NMOD * KT) + (3 * k * KT + j - 1), 1)])

        def update_x(pair, slot, bank_use, t, k, j):
            dve.wait_ge(w_used[slot], pair + 1)
            dve.scalar_tensor_tensor(out=tile(X2, j), in0=G[t][:, :], scalar=GC[:, k, ds(j, 1)], in1=tile(X2, j),
                                     op0=ALU.mult, op1=ALU.add).then_inc(acc_read[t], 1)

        def add_square(n8, j):
            dve.wait_ge(sem("sq_ready"), n8 + j + 1)
            dve.wait_ge(sem("ssum_add"), n8 + j)
            dve.tensor_tensor(SSUM[:, :], SSUM[:, :], SQ[:, :], ALU.add).then_inc(sem("ssum_add"), 1)

        def ada_step(seq, k):
            n = seq * KT + k
            dve.wait_ge(sem(f"ada_in{k % 4}"), (seq * (KT // 4) + (k // 4 + 1)) * 16)
            if k == 0:
                dve.wait_ge(sem("acc_parts"), seq)
                ins = dve.tensor_scalar(ACC[:, :], ada_raw[0][:, :], CA[:, 0:1], None, ALU.mult)
            else:
                dve.wait_ge(sem("ada_step"), n)
                ins = dve.scalar_tensor_tensor(out=ACC[:, :], in0=ada_raw[k % 4][:, :], scalar=CA[:, k:k + 1],
                                               in1=ACC[:, :], op0=ALU.mult, op1=ALU.add)
            ins.then_inc(sem("ada_step"), 1)

        def chunk_parts(seq):
            dve.wait_ge(sem("ada_step"), (seq + 1) * KT)
            dve.tensor_copy(ACCH[:, :], ACC[:, :]).then_inc(sem("acc_hi"), 1)
            dve.wait_ge(sem("acc_hi"), seq + 1)
            dve.tensor_tensor(ACCL[:, :], ACC[:, :], ACCH[:, :].bitcast(F32), ALU.subtract).then_inc(sem("acc_parts"), 1)

        def mod_rows(turn):
            dve.wait_ge(sem("mod_summed"), turn + 1)
            dve.wait_ge(sem("mod_turned"), turn)
            dve.tensor_copy(MR[0:64, :], O[0:64, :]).then_inc(sem("mod_copied"), 1)

        def mod_columns(layer, hc, rows, turn):
            dve.wait_ge(sem("mod_turned"), turn + 1)
            dve.tensor_tensor(MODC[:, ds(layer * (NMOD * KT) + hc * 4, rows * 4)], O[:, 0:rows * 4],
                              PT[:, ds(layer * PC + PC_ADA + hc * 4, rows * 4)], ALU.add).then_inc(sem("modc_ready"), 1)

        def scale_columns(l, k):
            return dve.scalar_tensor_tensor(out=AC[:, k, :], in0=MODC[:, ds(l * (NMOD * KT) + (3 * k + 1) * KT, KT)],
                                            scalar=1.0, in1=PT[:, ds(l * PC + PC_NORM[k], KT)], op0=ALU.add, op1=ALU.mult)

        def gate_columns(l, k):
            return dve.tensor_scalar(GC[:, k, :], MODC[:, ds(l * (NMOD * KT) + (3 * k + 2) * KT, KT)],
                                     0.5 if k == 1 else 0.25, None, ALU.mult)

        dve.memset(TB[BUCKETS:BUCKETS + 1, :], NEG).then_inc(sem("tb_rows"), 1)
        clear_sum()
        sum_cleared(1)
        dve.wait_ge(sem("ptp_ready"), 1)
        dve.tensor_copy(PT2[:, :], O[:, 0:2 * KT]).then_inc(sem("pt_ready"), 1)
        dve.wait_ge(sem("consts"), 4)
        dve.tensor_copy(SELR[:, :], SEL[:, :]).then_inc(sem("selr"), 1)
        acc = ACC0[:, :]
        dve.wait_ge(sem("ca_ready"), 1)
        for j in range(KT):
            add_square(0, j)
        dve.wait_ge(sem("tbp_ready"), 1)
        dve.tensor_copy(TB[0:BUCKETS, :], TP[0][0:BUCKETS, 0:HEADS]).then_inc(sem("tb_rows"), 1)
        dve.wait_ge(sem("tb_rows"), 2)
        dve.tensor_copy(TBX[0:BUCKETS + 1, :, :], TB[0:BUCKETS + 1, :].unsqueeze(2).to_broadcast([BUCKETS + 1, HEADS, P]))\
            .then_inc(sem("tbx_ready"), 1)
        for k in range(KT):
            dve.wait_ge(sem(f"ada0_in{k}"), 16)
            if k == 0:
                dve.tensor_scalar(acc, ADA0[:, 0, :], CA[:, 0:1], None, ALU.mult).then_inc(sem("ada0_step"), 1)
                continue
            dve.wait_ge(sem("ada0_step"), k)
            dve.scalar_tensor_tensor(out=acc, in0=ADA0[:, k, :], scalar=CA[:, k:k + 1], in1=acc,
                                     op0=ALU.mult, op1=ALU.add).then_inc(sem("ada0_step"), 1)
        dve.wait_ge(sem("lambda_in"), 16 * 4 * DEPTH)
        for l in range(DEPTH):
            for n in range(2):
                dve.tensor_tensor_reduce(LV[:, l, 2 * n, :], LV[:, l, 2 * n, :], LV[:, l, 2 * n + 1, :], 1.0, 0.0,
                                         ALU.mult, ALU.add, lam_dot[:, 2 * l + n:2 * l + n + 1]).then_inc(sem("lam_dots"), 1)
        for l in range(DEPTH):
            dve.wait_ge(sem("ptp_ready"), l + 2)
            dve.tensor_copy(PT[:, l * PC:(l + 1) * PC], TP[l][:, 0:PC]).then_inc(sem("pt_ready"), 1)
        mod_rows(0)
        mod_columns(0, 0, 4, 0)
        for s in range(2):
            w_lo_part(0, s)
        dve.wait_ge(sem("lam_exps"), 1)
        for l in range(DEPTH):
            lam_init = 0.8 - 0.6 * math.exp(-0.3 * l)
            dve.scalar_tensor_tensor(out=nlam[:, l:l + 1], in0=lam_exp[:, 2 * l + 1:2 * l + 2], scalar=lam_init,
                                     in1=lam_exp[:, 2 * l:2 * l + 1], op0=ALU.subtract, op1=ALU.subtract)\
                .then_inc(sem("lam_ready"), 1)
            dve.tensor_scalar(subg[:, l:l + 1], PT[:, l * PC + PC_SUB:l * PC + PC_SUB + 1], 1.0 - lam_init, None,
                              ALU.mult).then_inc(sem("lam_ready"), 1)
        dve.wait_ge(sem("lam_ready"), 2 * DEPTH)

        with dve.Fori(0, DEPTH) as l:
            for w in range(2):
                n_in, n_out = f"ffn{w + 1}_in", f"ffn{w + 1}_out"
                if w == 0:
                    dve.wait_ge(sem("modc_ready"), l * NMOD + 1)
                    scale_columns(l, 0).then_inc(sem("ac_ready"), 1)
                norm_units(l, 2 * w)

                def ffn_tile(i, seq=0, steps=()):
                    p = l * PAIRS + PAIR0[n_in] + i
                    u = l * USES + USE0[n_in] + i
                    w_lo_part(p + 1, 0)
                    dve.wait_ge(sem("g_tanh"), (l * 2 + w) * FT + i + 1)
                    dve.wait_ge(acc_read[1], u)
                    dve.scalar_tensor_tensor(out=T[1][:, :], in0=T[0][:, :], scalar=1.0, in1=G[0][:, :],
                                             op0=ALU.add, op1=ALU.mult).then_inc(acc_read[0], 1)
                    for k in steps[:1]:
                        ada_step(seq, k)
                    w_lo_part(p + 1, 1)
                    dve.wait_ge(acc_read[0], u + 1)
                    dve.wait_ge(w_used[1], p + 1)
                    dve.wait_ge(sem("s_lo"), (l * 2 + w) * FT + i)
                    dve.tensor_tensor(F[0][:, :], G[1][:, :], T[1][:, :], ALU.mult).then_inc(acc_read[1], 1)
                    dve.wait_ge(sem("s_hi"), (l * 2 + w) * FT + i + 1)
                    dve.tensor_tensor(tile(SLO2, i), F[0][:, :], tile(SHI2, i).bitcast(F32), ALU.subtract)\
                        .then_inc(sem("s_lo"), 1)
                    for k in steps[1:]:
                        ada_step(seq, k)

                ffn_tile(0)
                with dve.Fori(0, CHUNKS_IN[w]) as g:
                    seq = l * NMOD + CHUNK_SEQ[n_in] + g
                    for r in range(GROUP):
                        if r == 6:
                            mod_rows(seq + 1)
                        ffn_tile(g * GROUP + (r + 1), seq, GROUP_STEPS[r])
                        if r == 4:
                            chunk_parts(seq)
                        if r == 6:
                            mod_columns(1 if w else l, g * 2 + (0 if w else 4), 2, seq + 1)
                if w:
                    with dve.Fori(1 + CHUNKS_IN[w] * GROUP, FT) as i:
                        ffn_tile(i)
                if w == 0:
                    dve.wait_ge(sem("modc_ready"), l * NMOD + CHUNKS_IN[0] + 1)
                    scale_columns(l, 1)
                    gate_columns(l, 0).then_inc(sem("ac_ready"), 1)
                    dve.wait_ge(sem("ac_ready"), l * 3 + 2)

                clear_sum()
                with dve.Fori(0, KT // 2) as i:
                    for m in range(6):
                        p = l * PAIRS + PAIR0[n_out] + i * 3 + m // 2
                        if w == 0:
                            seq = l * NMOD + CHUNK_SEQ[n_out] + i
                            if m == 5:
                                mod_rows(seq + 1)
                            for k in OUT_STEPS[m][:1]:
                                ada_step(seq, k)
                        w_lo_part(p + 1, m % 2, OUTG[(m + 2) % 3] if m < 4 else 8)
                        if w == 0:
                            for k in OUT_STEPS[m][1:]:
                                ada_step(seq, k)
                            if m == 3:
                                chunk_parts(seq)
                        if m % 3 == 2:
                            t = m // 3
                            update_x(p, m % 2, l * USES + USE0[n_out] + i, t, 2 * w, i * 2 + t)
                            sum_cleared(l * ZEROS + 1 + (ZERO_FFN2 if w else ZERO_FFN1))
                            add_square((l * 3 + 1 + 2 * w) * KT, i * 2 + t)
                    if w == 0:
                        mod_columns(l, i * 2 + (4 + 2 * CHUNKS_IN[0]), 2, seq + 1)
                if w == 1:
                    continue
                dve.wait_ge(sem("modc_ready"), l * NMOD + CHUNKS_IN[0] + CHUNKS_OUT + 1)
                scale_columns(l, 2)
                for k in (1, 2):
                    g = gate_columns(l, k)
                g.then_inc(sem("ac_ready"), 1)

                norm_units(l, 1)
                clear_sum()
                dve.memset(Z[:, 0:PADL], 0.0).then_inc(sem("z_pad"), 1)
                dve.wait_ge(sem("z_pad"), l + 1)

                def taps(h, lo, hi):
                    q = l * HEADS + h
                    for t in range(lo, hi):
                        wt = CW2[:, ds(q * CK + t, 1)]
                        if t == 0:
                            dve.wait_ge(sem("z_ready"), q + 1)
                            dve.wait_ge(sem("c_part"), q)
                            ins = dve.tensor_scalar(CAB[0][:, :], Z[:, 0:TOK], wt, PT[:, ds(l * PC + PC_DWB + h, 1)],
                                                    ALU.mult, ALU.add)
                        elif t == 1:
                            ins = dve.tensor_scalar(CAB[1][:, :], Z[:, 1:1 + TOK], wt, None, ALU.mult)
                        else:
                            dve.wait_ge(sem("tap_done"), q * DVE_TAPS + (t - 1))
                            ins = dve.scalar_tensor_tensor(out=CAB[t % 2][:, :], in0=Z[:, t:t + TOK], scalar=wt,
                                                           in1=CAB[t % 2][:, :], op0=ALU.mult, op1=ALU.add)
                        ins.then_inc(sem("tap_done"), 1)

                def chains(h):
                    q = l * HEADS + h
                    dve.wait_ge(sem("tap_done"), (q + 1) * DVE_TAPS)
                    dve.tensor_tensor(tile(C2, h), CAB[0][:, :], CAB[1][:, :], ALU.add).then_inc(sem("c_part"), 1)

                def mix(h, first):
                    hh = l * HEADS + h
                    p = l * PAIRS + PAIR0["mix"] + h * 3
                    b = l * USES + USE0["mix"] + h * 3
                    uh = l * UNITS + UNIT_HEAD + h - 1

                    def conv(lo, hi):
                        if not first:
                            taps(h - 1, lo, hi)

                    def scores(i):
                        par, r, n = i % 2, QB - 1 - i, (i + 1) * P
                        si = hh * 4 + r
                        dve.wait_ge(sem("s_ready"), si + 1)
                        dve.wait_ge(sem("t_ready"), si - 1 if r >= 2 else hh * 4)
                        dve.memset(spare[:, 1:2], 0.0)
                        for m in range(2):
                            dve.tensor_tensor_reduce(PR[par][m][:, 0:n], S[m][:, 0:n], BT[:, TOK - n:TOK], 1.0, NEG,
                                                     ALU.add, ALU.max, mx[:, par, m:m + 1]).then_inc(sem("max_done"), 1)
                        dve.wait_ge(sem("max_done"), (si + 1) * 2)
                        dve.tensor_scalar(nmx[:, par, :], mx[:, par, :], -1.0, None, ALU.mult).then_inc(sem("nmax_ready"), 1)

                    def combine(i):
                        par, n = i % 2, (i + 1) * P
                        si = hh * 4 + (QB - 1 - i)
                        p0, p1 = PR[par][0][:, 0:n], PR[par][1][:, 0:n]
                        dve.wait_ge(sem("exp_done"), (si + 1) * 2)
                        dve.reciprocal(rinv[:, par, :], rsum[:, par, :]).then_inc(sem("comb"), 1)
                        dve.wait_ge(sem("comb"), si * 3 + 1)
                        dve.tensor_scalar(rlam[:, par:par + 1], rinv[:, par, 1:2], nlam[:, ds(l, 1)], None, ALU.mult)\
                            .then_inc(sem("comb"), 1)
                        dve.wait_ge(sem("comb"), si * 3 + 2)
                        dve.tensor_scalar(p1, p1, rlam[:, par:par + 1], None, ALU.mult).then_inc(sem("comb"), 1)
                        dve.wait_ge(sem("comb"), si * 3 + 3)
                        dve.scalar_tensor_tensor(out=p0, in0=p0, scalar=rinv[:, par, 0:1], in1=p1,
                                                 op0=ALU.mult, op1=ALU.add).then_inc(sem("w_ready"), 1)

                    conv(0, 5)
                    w_lo_part(p + 1, 0)
                    conv(5, 11)
                    w_lo_part(p + 1, 1)
                    if not first:
                        reciprocal(l * AUXN + AUX_HEAD + h - 1, l * RSN + RS_HEAD + h - 1)
                        unit_gain(uh, 0, True, OT[:, :], subg[:, ds(l, 1)])
                    w_lo_part(p + 2, 0)
                    conv(11, 12)
                    dve.wait_ge(sem("bt_in"), (hh + 1) * 16)
                    scores(3)
                    if not first:
                        unit_lo(uh, 0, tile(AOLO2, h - 1), tile(AOHI2, h - 1))
                    conv(12, 14)
                    scores(2)
                    w_lo_part(p + 2, 1)
                    combine(3)
                    conv(14, 17)
                    scores(1)
                    combine(2)
                    w_lo_part(p + 3, 0)
                    conv(17, 18)
                    scores(0)
                    combine(1)
                    conv(18, DVE_TAPS)
                    w_lo_part(p + 3, 1)
                    combine(0)
                    if not first:
                        chains(h - 1)
                    dve.wait_ge(acc_read[0], b + 3)
                    dve.wait_ge(acc_read[1], b + 2)
                    dve.wait_ge(sem("cp_ready"), hh)
                    dve.wait_ge(sem("tap_done"), hh * DVE_TAPS)
                    dve.scalar_tensor_tensor(out=Z[:, PADL:PADL + TOK], in0=F[1][:, :], scalar=1.0, in1=T[1][:, :],
                                             op0=ALU.add, op1=ALU.mult).then_inc(sem("z_ready"), 1)

                mix(0, True)
                with dve.Fori(1, HEADS) as h:
                    mix(h, False)

                dve.wait_ge(acc_read[1], l * USES + USE0["gb"])
                for j in range(KT):
                    p = l * PAIRS + PAIR0["gb"] + j
                    for t in range(2):
                        w_lo_part(p + 1, t)
                        if j >= KT // 2:
                            n = 2 * (j - KT // 2) + t
                            dve.scalar_tensor_tensor(out=GA[:, n, :], in0=GA[:, n, :], scalar=1.0, in1=G[t][:, :],
                                                     op0=ALU.add, op1=ALU.mult).then_inc(acc_read[t], 1)
                        if j == 0 and t == 0:
                            taps(HEADS - 1, 0, 4)
                        if j == 1 and t == 0:
                            taps(HEADS - 1, 9, 15)
                    if j == 0:
                        uh = l * UNITS + UNIT_HEAD + HEADS - 1
                        reciprocal(l * AUXN + AUX_HEAD + HEADS - 1, l * RSN + RS_HEAD + HEADS - 1)
                        unit_gain(uh, 0, True, OT[:, :], subg[:, ds(l, 1)])
                        taps(HEADS - 1, 4, 6)
                        unit_lo(uh, 0, AOLO[:, HEADS - 1, :], AOHI[:, HEADS - 1, :])
                        taps(HEADS - 1, 6, 9)
                    if j == 1:
                        taps(HEADS - 1, 15, DVE_TAPS)
                        chains(HEADS - 1)
                    if j == LN_MEAN:
                        dve.wait_ge(sem("aux_read"), l * AUXN + AUX_MEAN + 1)
                        clear_sum()
                        sum_cleared(l * ZEROS + 1 + ZERO_LN)
                    if j in (LN_MEAN, LN_MEAN + 1):
                        n0 = 4 * (j - LN_MEAN)
                        for n in range(n0, n0 + 5):
                            if n < n0 + 4:
                                dve.tensor_tensor(C[:, n, :], C[:, n, :], F[1][:, :], ALU.subtract).then_inc(sem("xc_ready"), 1)
                            if n > n0:
                                dve.wait_ge(sem("lnsq"), l * KT + n)
                                dve.wait_ge(sem("lnadd"), l * KT + n - 1)
                                dve.tensor_tensor(SSUM[:, :], SSUM[:, :], SQ[:, :], ALU.add).then_inc(sem("lnadd"), 1)
                    if j == LN_VAR:
                        reciprocal(l * AUXN + AUX_VAR, l * RSN + RS_VAR)
                    units = LN_UNITS.get(j, ())
                    for n in (*units, None):
                        ul = l * UNITS + UNIT_LN
                        if n is not None:
                            unit_scale(ul + n, n % 2, n == 0, C[:, n, :])
                        if units and n != units[0]:
                            o = units[-1] if n is None else n - 1
                            unit_rest(ul + o, o % 2, CLO[:, o, :], CHI[:, o, :])
                with dve.Fori(0, KT // 2) as i:
                    for t in range(2):
                        j = i * 2 + t
                        w_lo_part(l * PAIRS + PAIR0["brb"] + i + 1, t)
                        if t == 0:
                            dve.wait_ge(acc_read[1], l * USES + USE0["brb"] + i)
                        dve.scalar_tensor_tensor(out=T[t][:, :], in0=tile(GB2, j), scalar=1.0, in1=G[t][:, :],
                                                 op0=ALU.add, op1=ALU.mult).then_inc(acc_read[t], 1)
                        dve.wait_ge(acc_read[t], l * USES + USE0["brb"] + i + 1)
                        dve.wait_ge(sem("m_lo"), l * KT + j)
                        dve.tensor_tensor(F[t][:, :], tile(GA2, j), T[t][:, :], ALU.add).then_inc(sem("merged"), 1)
                        dve.wait_ge(sem("m_hi"), l * KT + j + 1)
                        dve.tensor_tensor(tile(MLO2, j), F[t][:, :], tile(MHI2, j).bitcast(F32), ALU.subtract)\
                            .then_inc(sem("m_lo"), 1)
                clear_sum()
                with dve.Fori(0, KT // 2) as i:
                    for t in range(2):
                        p = l * PAIRS + PAIR0["mo"] + i
                        w_lo_part(p + 1, t)
                        update_x(p, t, l * USES + USE0["mo"] + i, t, 1, i * 2 + t)
                        sum_cleared(l * ZEROS + 1 + ZERO_MO)
                        add_square((l * 3 + 2) * KT, i * 2 + t)

        reciprocal(DEPTH * AUXN, DEPTH * RSN)
        for j in range(KT):
            dve.wait_ge(sem("unit_lo"), DEPTH * UNITS)
            if j >= 2:
                dve.wait_ge(sem("yt_ready"), j - 1)
            dve.scalar_tensor_tensor(out=T[j % 2][:, :], in0=X[:, j, :], scalar=PT2[:, j:j + 1], in1=RSTD[:, :],
                                     op0=ALU.mult, op1=ALU.mult).then_inc(sem("unit_t"), 1)

    @block.tensor
    def _(pe):
        def slab(pair, slot, acc, hi, lo, k0=0, n=8, first=True, last=True, ready=None, at=()):
            pe.wait_ge(w_hi[slot], pair + 1)
            pe.wait_ge(w_lo[slot], pair + 1)
            for k in range(n):
                if ready:
                    ready(k0 + k)
                if k in at:
                    at[k]()
                wh, wl = whi[slot][:, k, :], wlo[slot][:, k, :]
                pe.matmul(acc, wh, hi[:, k0 + k, :], start=first and k == 0, stop=False)
                pe.matmul(acc, wh, lo[:, k0 + k, :], start=False, stop=False)
                mm = pe.matmul(acc, wl, hi[:, k0 + k, :], start=False, stop=last and k == n - 1)
            mm.then_inc(w_used[slot], 1)

        def two_slabs(pair, hi, lo, ready):
            lag = 4
            for k in range(KT + lag):
                for slot, n in ((0, k), (1, k - lag)):
                    if not 0 <= n < KT:
                        continue
                    if n == 0:
                        pe.wait_ge(w_hi[slot], pair + 1)
                        pe.wait_ge(w_lo[slot], pair + 1)
                    if slot == 0:
                        ready(n)
                    wh, wl, acc = whi[slot][:, n, :], wlo[slot][:, n, :], G[slot][:, :]
                    pe.matmul(acc, wh, hi[:, n, :], start=n == 0, stop=False)
                    pe.matmul(acc, wh, lo[:, n, :], start=False, stop=False)
                    mm = pe.matmul(acc, wl, hi[:, n, :], start=False, stop=n == KT - 1)
                    if n == KT - 1:
                        mm.then_inc(w_used[slot], 1)

        def mean(aux, src):
            pe.wait_ge(sem("aux_read"), aux)
            pe.matmul(AUX[:, :], invd[:, :], src, start=True, stop=True).then_inc(sem("aux_ready"), 1)

        def norm_mean(aux, n8):
            pe.wait_ge(sem("ssum_add"), n8)
            mean(aux, SSUM[:, :])

        def mod_sum(turn, src, rows):
            pe.wait_ge(sem("modc_ready"), turn)
            for r in range(rows):
                mm = pe.matmul(O[0:64, :], SEL[:, ROWS_MAX - 1 - r:ROWS_MAX - 1 - r + 64],
                               src[:, r * TOK:(r + 1) * TOK], start=(r == 0), stop=(r == rows - 1))
            mm.then_inc(sem("mod_summed"), 1)

        def mod_sum_parts(turn):
            pe.wait_ge(sem("acc_parts"), turn)
            pe.wait_ge(sem("modc_ready"), turn)
            for r in range(2):
                one = SELR[:, ROWS_MAX - 1 - r:ROWS_MAX - 1 - r + 64]
                pe.matmul(O[0:64, :], one, ACCH[:, r * TOK:(r + 1) * TOK], start=(r == 0), stop=False)
                mm = pe.matmul(O[0:64, :], one, ACCL[:, r * TOK:(r + 1) * TOK], start=False, stop=(r == 1))
            mm.then_inc(sem("mod_summed"), 1)

        def mod_turn(turn, rows):
            pe.wait_ge(sem("mod_copied"), turn + 1)
            for q in range(4):
                mm = pe.matmul(O[:, q:4 * rows:4], MR[0:64, q * P:(q + 1) * P], ident[0:64, 0:rows], start=True, stop=True)
            mm.then_inc(sem("mod_turned"), 1)

        pe.wait_ge(sem("consts"), 4)
        pe.wait_ge(sem("rows2_in"), 32)
        pe.transpose(O[:, 0:2 * KT], PV2[0:2 * KT, :], ident[0:2 * KT, 0:2 * KT]).then_inc(sem("ptp_ready"), 1)
        for j in range(KT):
            if j >= 2:
                pe.wait_ge(sem("sq_ready"), j - 1)
            for t in range(QB):
                if j == 0:
                    pe.wait_ge(sem(f"x_in{t}"), 16)
                mm = pe.transpose(bank[2 + j % 2][:, t * P:(t + 1) * P], XS[:, t, j * P:(j + 1) * P], ident[:, :])
            mm.then_inc(sem("xp_ready"), 1)
        pe.wait_ge(sem("table_in"), 32)
        pe.transpose(TP[0][0:BUCKETS, 0:HEADS], TBR[0:HEADS, :], ident[0:HEADS, 0:HEADS]).then_inc(sem("tbp_ready"), 1)
        pe.wait_ge(sem("taps_in"), 16 * DEPTH)
        for l in range(DEPTH):
            for h in range(HEADS):
                mm = pe.transpose(G[l][:, h * CK:(h + 1) * CK], CWR[0:CK, l, h * P:(h + 1) * P], ident[0:CK, 0:CK])
            mm.then_inc(sem("tapsp_ready"), 1)
        pe.wait_ge(sem("tbx_ready"), 1)
        for h in range(HEADS):
            if h >= 2:
                pe.wait_ge(sem("br_copied"), h - 1)
            wide, narrow = ROW_BANKS[h % 2]
            pe.matmul(wide[:, :], TBX[0:BUCKETS + 1, h, :], OH[0:BUCKETS + 1, 0:TOK], start=True, stop=True)
            pe.matmul(narrow[:, 0:P], TBX[0:BUCKETS + 1, h, :], OH[0:BUCKETS + 1, TOK:TOK + P], start=True, stop=True)\
                .then_inc(sem("br_ready"), 1)
        pe.wait_ge(sem("br_copied"), HEADS)
        pe.wait_ge(sem("rows_in"), 16 * 8 * DEPTH)
        for l in range(DEPTH):
            pe.transpose(TP[l][:, 0:PC], PV[l][0:PC, :], ident[0:PC, 0:PC]).then_inc(sem("ptp_ready"), 1)
        pe.wait_ge(sem("cw_ready"), DEPTH)
        pe.wait_ge(sem("ada0_step"), KT)
        mod_sum(0, ACC0, 4)
        mod_turn(0, 4)
        pe.wait_ge(sem("selr"), 1)

        with pe.Fori(0, DEPTH) as l:
            pe.wait_ge(sem("o_read"), l * HEADS)
            for w in range(2):
                n_in, n_out = f"ffn{w + 1}_in", f"ffn{w + 1}_out"
                norm_mean(l * AUXN + AUX_NORM[2 * w], (l * 3 + 2 * w + 1) * KT)

                def ffn_tile(i):
                    p = l * PAIRS + PAIR0[n_in] + i
                    u = l * USES + USE0[n_in] + i
                    pe.wait_ge(acc_read[0], u)
                    slab(p, 0, G[0][:, :], HHI, HLO)
                    pe.wait_ge(acc_read[1], u)
                    slab(p, 1, G[1][:, :], HHI, HLO)

                for b in range(2):
                    pe.wait_ge(acc_read[b], l * USES + USE0[n_in])
                two_slabs(l * PAIRS + PAIR0[n_in], HHI, HLO,
                          lambda k: pe.wait_ge(sem("unit_lo"), l * UNITS + UNIT_NORM[2 * w] + k + 1))
                with pe.Fori(0, CHUNKS_IN[w]) as g:
                    seq = l * NMOD + CHUNK_SEQ[n_in] + g
                    for r in range(GROUP):
                        ffn_tile(g * GROUP + (r + 1))
                        if r == 5:
                            mod_sum_parts(seq + 1)
                        if r == 6:
                            mod_turn(seq + 1, 2)
                if w == 1:
                    with pe.Fori(1 + CHUNKS_IN[w] * GROUP, FT) as i:
                        ffn_tile(i)

                with pe.Fori(0, KT // 2) as i:
                    seq = l * NMOD + CHUNK_SEQ[n_out] + i if w == 0 else None
                    for m in range(6):
                        t, g = m // 3, m % 3
                        if g == 0:
                            pe.wait_ge(acc_read[t], l * USES + USE0[n_out] + i)
                        k0 = sum(OUTG[:g])
                        pe.wait_ge(sem("s_lo"), (l * 2 + w) * FT + (k0 + OUTG[g]))
                        slab(l * PAIRS + PAIR0[n_out] + i * 3 + m // 2, m % 2, G[t][:, :], SHI, SLO,
                             k0, OUTG[g], g == 0, g == 2,
                             at={2: lambda: mod_sum_parts(seq + 1)} if w == 0 and m == 5 else {})
                    if w == 0:
                        mod_turn(seq + 1, 2)
                if w == 1:
                    continue

                norm_mean(l * AUXN + AUX_NORM[1], (l * 3 + 2) * KT)

                def turn_weights(i, hh):
                    si = hh * 4 + (QB - 1 - i)
                    pe.wait_ge(sem("w_ready"), si + 1)
                    if i == 2:
                        pe.wait_ge(sem("v_ready"), hh + 1)
                    elif i < 2:
                        pe.wait_ge(sem("wt_ready"), si - 1)
                    for j in range(i + 1):
                        mm = pe.transpose(TP[i % 2][:, j * P:(j + 1) * P], PR[i % 2][0][:, j * P:(j + 1) * P], ident[:, :])
                    mm.then_inc(sem("t_ready"), 1)

                def values(hh):
                    pe.wait_ge(sem("wt_ready"), hh * 4 + 4)
                    pe.wait_ge(sem("o_read"), hh)
                    for j in range(QB):
                        mm = pe.matmul(O[:, j * P:TOK], V[:, j, :], WT[:, j, j * P:TOK], start=(j == 0), stop=(j == QB - 1))
                    mm.then_inc(sem("o_ready"), 1)

                def head_mean(h):
                    pe.wait_ge(sem("o_read"), l * HEADS + h + 1)
                    mean(l * AUXN + AUX_HEAD + h, SQ[:, :])

                def mix(h, first):
                    hh = l * HEADS + h
                    p = l * PAIRS + PAIR0["mix"] + h * 3
                    b = l * USES + USE0["mix"] + h * 3

                    def scores(i):
                        si, n = hh * 4 + (QB - 1 - i), (i + 1) * P
                        pe.wait_ge(sem("nmax_ready"), si)
                        for m in range(2):
                            mm = pe.matmul(S[m][:, 0:n], QT[m * HD:(m + 1) * HD, i * P:(i + 1) * P],
                                           KTT[m * HD:(m + 1) * HD, 0:n], start=True, stop=True)
                        mm.then_inc(sem("s_ready"), 1)

                    def turn_v():
                        pe.wait_ge(acc_read[0], b + 2)
                        pe.wait_ge(sem("wt_ready"), hh * 4)
                        for j in range(QB):
                            mm = pe.transpose(TP[0][:, j * P:(j + 1) * P], VT[:, j * P:(j + 1) * P], ident[:, :])
                        mm.then_inc(sem("vtp_ready"), 1)

                    if first:
                        for t in range(2):
                            pe.wait_ge(acc_read[t], b)
                        two_slabs(p, HHI, HLO,
                                  lambda k: pe.wait_ge(sem("unit_lo"), l * UNITS + UNIT_NORM[1] + k + 1))
                    else:
                        pe.wait_ge(acc_read[0], b)
                        slab(p, 0, G[0][:, :], HHI, HLO, at={4: lambda: turn_weights(1, hh - 1)})
                        turn_weights(0, hh - 1)
                        pe.wait_ge(acc_read[1], b)
                        slab(p, 1, G[1][:, :], HHI, HLO, at={4: lambda: values(hh - 1)})
                    pe.wait_ge(acc_read[0], b + 1)
                    slab(p + 1, 0, G[0][:, :], HHI, HLO, at={} if first else {3: lambda: head_mean(h - 1)})
                    pe.wait_ge(acc_read[1], b + 1)
                    slab(p + 1, 1, G[1][:, :], HHI, HLO, at={4: lambda: scores(3)})
                    scores(2)
                    turn_v()
                    pe.wait_ge(acc_read[0], b + 2)
                    slab(p + 2, 0, G[0][:, :], HHI, HLO, at={4: lambda: scores(1), 6: lambda: turn_weights(3, hh)})
                    pe.wait_ge(acc_read[1], b + 2)
                    slab(p + 2, 1, G[1][:, :], HHI, HLO, at={4: lambda: scores(0), 6: lambda: turn_weights(2, hh)})

                mix(0, True)
                with pe.Fori(1, HEADS) as h:
                    mix(h, False)

                def branch(name, i, hi, lo, at=({}, {})):
                    for t in range(2):
                        pe.wait_ge(acc_read[t], l * USES + USE0[name] + i)
                        slab(l * PAIRS + PAIR0[name] + i, t, G[t][:, :], hi, lo, at=at[t])

                last = l * HEADS + HEADS - 1

                branch("gb", 0, HHI, HLO, ({4: lambda: turn_weights(1, last)}, {1: lambda: turn_weights(0, last), 6: lambda: values(last)}))
                head_mean(HEADS - 1)
                with pe.Fori(1, LN_MEAN + 1) as i:
                    branch("gb", i, HHI, HLO)
                pe.wait_ge(sem("csum"), (l + 1) * KT)
                mean(l * AUXN + AUX_MEAN, SSUM[:, :])
                with pe.Fori(LN_MEAN + 1, KT // 2) as i:
                    branch("gb", i, HHI, HLO)
                with pe.Fori(0, LN_VAR + 1 - KT // 2) as i:
                    pe.wait_ge(sem("unit_lo"), l * UNITS + UNIT_HEAD + HEADS)
                    branch("ab", i, AOHI, AOLO)
                pe.wait_ge(sem("lnadd"), (l + 1) * KT)
                mean(l * AUXN + AUX_VAR, SSUM[:, :])
                with pe.Fori(LN_VAR + 1 - KT // 2, KT // 2) as i:
                    branch("ab", i, AOHI, AOLO)
                with pe.Fori(0, KT // 2) as i:
                    for t in range(2):
                        pe.wait_ge(acc_read[t], l * USES + USE0["brb"] + i)
                        slab(l * PAIRS + PAIR0["brb"] + i, t, G[t][:, :], CHI, CLO,
                             ready=lambda k: pe.wait_ge(sem("unit_lo"), l * UNITS + UNIT_LN + k + 1))
                with pe.Fori(0, KT // 2) as i:
                    for t in range(2):
                        pe.wait_ge(acc_read[t], l * USES + USE0["mo"] + i)
                        slab(l * PAIRS + PAIR0["mo"] + i, t, G[t][:, :], MHI, MLO,
                             ready=lambda k: pe.wait_ge(sem("m_lo"), l * KT + k + 1))

        norm_mean(DEPTH * AUXN, (DEPTH * 3 + 1) * KT)
        for j in range(KT):
            pe.wait_ge(sem("unit_t"), DEPTH * UNITS + j + 1)
            if j >= 2:
                pe.wait_ge(sem("y_ready"), j - 1)
            for t in range(QB):
                mm = pe.transpose(TP[j % 2][:, t * P:(t + 1) * P], T[j % 2][:, t * P:(t + 1) * P], ident[:, :])
            mm.then_inc(sem("yt_ready"), 1)

    ctx.close()


NAMES = ["x", "c", "ffn1_norm", "ffn1_w_in", "ffn1_w_out", "mix_norm", "w_mix_in", "lambda_q1", "lambda_k1",
         "lambda_q2", "lambda_k2", "subln_gain", "w_attn_branch", "conv_dw", "conv_dw_bias", "conv_ln_gain",
         "conv_ln_bias", "w_conv_branch", "w_mix_out", "ffn2_norm", "ffn2_w_in", "ffn2_w_out", "ada_w", "ada_b",
         "rel_bias", "final_norm"]


def kernel(**inputs):
    import concourse.bacc as bacc
    from concourse.bass_utils import run_bass_kernel_spmd

    nc = bacc.Bacc("TRN2", target_bir_lowering=False, num_devices=1)
    arrays, aps = {}, {}
    for name in NAMES:
        arr = np.ascontiguousarray(inputs[name])
        arrays[f"in_{name}"] = arr
        aps[name] = nc.dram_tensor(f"in_{name}", arr.shape, F32, kind="ExternalInput").ap()
    sel = bias_selection()
    arrays["in_bias_selection"] = sel
    onehot = nc.dram_tensor("in_bias_selection", sel.shape, F32, kind="ExternalInput").ap()
    out = nc.dram_tensor("out_0", (1, TOK, D), F32, kind="ExternalOutput").ap()
    build(nc, aps, onehot, out)
    r = run_bass_kernel_spmd(nc, [arrays], core_ids=[0])
    return r.results[0]["out_0"]
```
